# Optimizing a Trainium2 kernel written in Bass

```python
import math
import jax, jax.numpy as jnp
from jax import lax
import numpy as np
import jax
import jax.numpy as jnp

D_MODEL = 1024
BATCH = 1
SEQ = 512
DEPTH = 1

CHUNK = 64
HEAD_DIM = 64
D_A = 384
HEADS_A = D_A // HEAD_DIM
D_B = 256
HEADS_B = D_B // HEAD_DIM
D_C = 384
HEADS_C = D_C // HEAD_DIM
D_MIX = D_A + D_B + D_C
IN_COLS = 2 * D_A + 3 * D_B + 2 * D_C
CONV_A_WIDTH = 31
CONV_B_WIDTH = 3
SG_BLOCK = 128
PEER_HEADS = 8
D_KEY = 256
N_KEYS = 128
N_EXPERTS = N_KEYS * N_KEYS
TOPK = 16
PEER_BLOCK = 128
PLE_DIM = 256
EPS = 1e-6


def rmsnorm(x, g):
    xf = x.astype(jnp.float32)
    y = xf * lax.rsqrt(jnp.mean(xf * xf, axis=-1, keepdims=True) + EPS)
    return (y * g.astype(jnp.float32)).astype(x.dtype)

def group_layernorm(x, g, b, heads):
    shp = x.shape
    xf = x.astype(jnp.float32).reshape(shp[:-1] + (heads, shp[-1] // heads))
    m = jnp.mean(xf, axis=-1, keepdims=True)
    var = jnp.mean(jnp.square(xf - m), axis=-1, keepdims=True)
    y = ((xf - m) * lax.rsqrt(var + EPS)).reshape(shp)
    return (y * g.astype(jnp.float32) + b.astype(jnp.float32)).astype(x.dtype)

def causal_dwconv(x, w):
    k = w.shape[0]
    return lax.conv_general_dilated(
        x, w.astype(x.dtype)[:, None, :], window_strides=(1,), padding=[(k - 1, 0)],
        dimension_numbers=("NWC", "WIO", "NWC"), feature_group_count=x.shape[-1])

def conformer_conv(za, conv_w, conv_b, ln_g, ln_b):
    val, gate = jnp.split(za, 2, axis=-1)
    y = val * jax.nn.sigmoid(gate)
    y = causal_dwconv(y, conv_w) + conv_b.astype(y.dtype)
    y = group_layernorm(y, ln_g, ln_b, HEADS_A)
    return jax.nn.silu(y)

def short_gated_conv(zb, conv_w):
    bg, cg, xb = jnp.split(zb, 3, axis=-1)
    return bg * causal_dwconv(cg * xb, conv_w)

def spatial_gating(zc, ln_g, ln_b, w_s, b_s):
    u, v = jnp.split(zc, 2, axis=-1)
    bsz, s, _ = v.shape
    v = group_layernorm(v, ln_g, ln_b, HEADS_C)
    vb = v.reshape(bsz, s // SG_BLOCK, SG_BLOCK, HEADS_C, HEAD_DIM)
    pos = jnp.arange(SG_BLOCK)
    mask = (pos[None, :] // CHUNK) <= (pos[:, None] // CHUNK)
    ws = jnp.where(mask[None], w_s, 0).astype(v.dtype)
    mixed = jnp.einsum("hij,bnjhc->bnihc", ws, vb) + b_s.T.astype(v.dtype)[None, None, :, :, None]
    return u * mixed.reshape(bsz, s, D_C)

def peer(n, w_q, sub_keys, expert_u, expert_v):
    bsz, s, d = n.shape
    t = bsz * s
    nf = n.reshape(t, d)
    q = (nf @ w_q).reshape(t, PEER_HEADS, D_KEY)
    q1, q2 = q[..., : D_KEY // 2], q[..., D_KEY // 2:]
    s1 = jnp.einsum("thd,hkd->thk", q1, sub_keys[:, 0])
    s2 = jnp.einsum("thd,hkd->thk", q2, sub_keys[:, 1])
    v1, i1 = lax.top_k(s1, TOPK)
    v2, i2 = lax.top_k(s2, TOPK)
    cand = (v1[..., :, None] + v2[..., None, :]).reshape(t, PEER_HEADS, TOPK * TOPK)
    vals, ci = lax.top_k(cand, TOPK)
    e1 = jnp.take_along_axis(i1, ci // TOPK, axis=-1)
    e2 = jnp.take_along_axis(i2, ci % TOPK, axis=-1)
    idx = (e1 * N_KEYS + e2).reshape(t, PEER_HEADS * TOPK)
    gates = jax.nn.softmax(vals.astype(jnp.float32), axis=-1).astype(n.dtype)
    gates = gates.reshape(t, PEER_HEADS * TOPK)
    nblk = t // PEER_BLOCK

    def block(args):
        xb, ib, gb = args
        ug = expert_u[ib]
        act = jax.nn.gelu(jnp.einsum("td,tkd->tk", xb, ug)) * gb
        vg = expert_v[ib]
        return jnp.einsum("tk,tkd->td", act, vg)

    out = lax.map(block, (nf.reshape(nblk, PEER_BLOCK, d),
                          idx.reshape(nblk, PEER_BLOCK, PEER_HEADS * TOPK),
                          gates.reshape(nblk, PEER_BLOCK, PEER_HEADS * TOPK)))
    return out.reshape(bsz, s, d)

def first_inputs(seed: int = 0) -> dict:
    key = jax.random.key(seed)
    ks = jax.random.split(key, 24)
    L, D = DEPTH, D_MODEL
    nrm = lambda k, shp, sc: jax.random.normal(k, shp, jnp.float32) * sc
    gain = lambda k, shp: 1.0 + 0.05 * jax.random.normal(k, shp, jnp.float32)
    return {
        "x": nrm(ks[0], (BATCH, SEQ, D), 1.0),
        "p": nrm(ks[1], (DEPTH, BATCH, SEQ, PLE_DIM), 1.0),
        "g_mix": gain(ks[2], (L, D)),
        "w_in": nrm(ks[3], (L, D, IN_COLS), D ** -0.5),
        "conv_a_w": nrm(ks[4], (L, CONV_A_WIDTH, D_A), CONV_A_WIDTH ** -0.5),
        "conv_a_b": nrm(ks[5], (L, D_A), 0.02),
        "ln_a_g": gain(ks[6], (L, D_A)),
        "ln_a_b": nrm(ks[7], (L, D_A), 0.02),
        "conv_b_w": nrm(ks[8], (L, CONV_B_WIDTH, D_B), CONV_B_WIDTH ** -0.5),
        "ln_c_g": gain(ks[9], (L, D_C)),
        "ln_c_b": nrm(ks[10], (L, D_C), 0.02),
        "w_s": nrm(ks[11], (L, HEADS_C, SG_BLOCK, SG_BLOCK), 0.5 * SG_BLOCK ** -0.5),
        "b_s": gain(ks[12], (L, HEADS_C, SG_BLOCK)),
        "w_out": nrm(ks[13], (L, D_MIX, D), D_MIX ** -0.5),
        "g_ffn": gain(ks[14], (L, D)),
        "w_q": nrm(ks[15], (L, D, PEER_HEADS * D_KEY), D ** -0.5),
        "sub_keys": nrm(ks[16], (L, PEER_HEADS, 2, N_KEYS, D_KEY // 2), (D_KEY // 2) ** -0.5),
        "expert_u": nrm(ks[17], (L, N_EXPERTS, D), D ** -0.5),
        "expert_v": nrm(ks[18], (L, N_EXPERTS, D), 0.1),
        "g_ple": gain(ks[19], (L, D)),
        "w_pe": nrm(ks[20], (L, PLE_DIM, D), PLE_DIM ** -0.5),
        "w_pg": nrm(ks[21], (L, D, D), D ** -0.5),
        "g_final": gain(ks[22], (D,)),
    }

def first_block(x, p, g_mix, w_in, conv_a_w, conv_a_b, ln_a_g, ln_a_b, conv_b_w, ln_c_g, ln_c_b,
              w_s, b_s, w_out, g_ffn, w_q, sub_keys, expert_u, expert_v, g_ple, w_pe, w_pg,
              g_final):
    h = x
    for i in range(DEPTH):
        a = rmsnorm(h, g_mix[i])
        z = a @ w_in[i]
        za = z[..., : 2 * D_A]
        zb = z[..., 2 * D_A: 2 * D_A + 3 * D_B]
        zc = z[..., 2 * D_A + 3 * D_B:]
        ya = conformer_conv(za, conv_a_w[i], conv_a_b[i], ln_a_g[i], ln_a_b[i])
        yb = short_gated_conv(zb, conv_b_w[i])
        yc = spatial_gating(zc, ln_c_g[i], ln_c_b[i], w_s[i], b_s[i])
        h = h + jnp.concatenate([ya, yb, yc], axis=-1) @ w_out[i]
        h = h + peer(rmsnorm(h, g_ffn[i]), w_q[i], sub_keys[i], expert_u[i], expert_v[i])
        gate = jax.nn.sigmoid(rmsnorm(h, g_ple[i]) @ w_pg[i])
        h = h + (p[i] @ w_pe[i]) * gate
    return rmsnorm(h, g_final)


D_MIX_2 = D_MODEL
SB_HEADS = 8
SB_HEAD_DIM = 64
SB_WIDTH = SB_HEADS * SB_HEAD_DIM
POOL_WINDOWS = (2, 4, 8, 16)
POOL_GROUPS = len(POOL_WINDOWS)
POOL_WIDTH = D_MIX_2 - SB_WIDTH
POOL_GROUP_DIM = POOL_WIDTH // POOL_GROUPS
IN_PROJ_COLS = 3 * SB_WIDTH + POOL_WIDTH
Q_BLOCK = 128
N_MEM = 256
MEM_HEADS = 4
MEM_HEAD_DIM = D_MODEL // MEM_HEADS
N_EXPERTS_2 = 32
TOP_K = 4
D_FF = D_MODEL
SWIGLU_LIMIT = 7.0
SWIGLU_ALPHA = 1.702
MOE_BLOCK = 128
RMS_EPS = 1e-5


def rmsnorm_2(x, g):
    xf = x.astype(jnp.float32)
    y = xf * lax.rsqrt(jnp.mean(xf * xf, axis=-1, keepdims=True) + RMS_EPS)
    return (y * g.astype(jnp.float32)).astype(x.dtype)

def stick_breaking_attention(q, k, v):
    seq = q.shape[2]
    scale = 1.0 / math.sqrt(q.shape[-1])
    outs = []
    for i in range(seq // Q_BLOCK):
        t0 = i * Q_BLOCK
        kv_len = t0 + Q_BLOCK
        qb = q[:, :, t0:kv_len]
        kb = k[:, :, :kv_len]
        vb = v[:, :, :kv_len]
        z = jnp.einsum('bhqd,bhkd->bhqk', qb, kb).astype(jnp.float32) * scale
        t_pos = t0 + jnp.arange(Q_BLOCK)
        s_pos = jnp.arange(kv_len)
        mask = s_pos[None, :] < t_pos[:, None]
        log_stay = jnp.where(mask, jax.nn.log_sigmoid(-z), 0.0)
        rev = lax.cumsum(log_stay, axis=3, reverse=True)
        after = jnp.concatenate([rev[..., 1:], jnp.zeros_like(rev[..., :1])], axis=-1)
        w = jnp.where(mask, jnp.exp(jax.nn.log_sigmoid(z) + after), 0.0)
        outs.append(jnp.einsum('bhqk,bhkd->bhqd', w.astype(vb.dtype), vb))
    return jnp.concatenate(outs, axis=2)

def multiscale_pool(u):
    seq = u.shape[1]
    uf = u.astype(jnp.float32)
    csum = jnp.cumsum(uf, axis=1)
    outs = []
    for g, win in enumerate(POOL_WINDOWS):
        cg = csum[:, :, g]
        shifted = jnp.pad(cg, ((0, 0), (win, 0), (0, 0)))[:, :seq]
        count = jnp.minimum(jnp.arange(seq) + 1, win).astype(jnp.float32)
        outs.append((cg - shifted) / count[None, :, None] - uf[:, :, g])
    return jnp.stack(outs, axis=2).astype(u.dtype)

def memory_cross_attention(h, m, w_q, w_kv, w_o):
    b, s, d = h.shape
    q = (h @ w_q).reshape(b, s, MEM_HEADS, MEM_HEAD_DIM)
    kv = m @ w_kv
    k = kv[..., :d].reshape(b, -1, MEM_HEADS, MEM_HEAD_DIM)
    v = kv[..., d:].reshape(b, -1, MEM_HEADS, MEM_HEAD_DIM)
    scores = jnp.einsum('bshd,bmhd->bhsm', q, k).astype(jnp.float32) / math.sqrt(MEM_HEAD_DIM)
    p = jax.nn.softmax(scores, axis=-1).astype(v.dtype)
    o = jnp.einsum('bhsm,bmhd->bshd', p, v).reshape(b, s, d)
    return o @ w_o

def moe_ffn(h, w_router, b_router, w1, b1, w2, b2):
    b, s, d = h.shape
    n_tok = b * s
    hf = h.reshape(n_tok, d)
    logits = (hf @ w_router + b_router).astype(jnp.float32)
    top_val, top_idx = lax.top_k(logits, TOP_K)
    gates = jax.nn.softmax(top_val, axis=-1)
    nk = n_tok * TOP_K
    flat_e = top_idx.reshape(nk)
    flat_tok = (jnp.arange(nk, dtype=jnp.int32) // TOP_K)
    flat_g = gates.reshape(nk)
    order = jnp.argsort(flat_e)
    sorted_e = flat_e[order]
    counts = jnp.bincount(flat_e, length=N_EXPERTS_2)
    padded = (counts + MOE_BLOCK - 1) // MOE_BLOCK * MOE_BLOCK
    start = jnp.cumsum(counts) - counts
    pend = jnp.cumsum(padded)
    pstart = pend - padded
    dest = pstart[sorted_e] + jnp.arange(nk) - start[sorted_e]
    n_rows = (nk + MOE_BLOCK - 1) // MOE_BLOCK * MOE_BLOCK + N_EXPERTS_2 * MOE_BLOCK
    n_blk = n_rows // MOE_BLOCK
    row_tok = jnp.zeros((n_rows,), jnp.int32).at[dest].set(flat_tok[order])
    row_g = jnp.zeros((n_rows,), h.dtype).at[dest].set(flat_g[order].astype(h.dtype))
    blk_e = jnp.minimum(jnp.searchsorted(pend, jnp.arange(n_blk) * MOE_BLOCK, side='right'),
                        N_EXPERTS_2 - 1)

    def expert_block(args):
        e, tok, g = args
        xb = hf[tok]
        gu = xb @ w1[e] + b1[e]
        gate = jnp.minimum(gu[:, :D_FF], SWIGLU_LIMIT)
        up = jnp.clip(gu[:, D_FF:], -SWIGLU_LIMIT, SWIGLU_LIMIT)
        act = (up + 1.0) * gate * jax.nn.sigmoid(SWIGLU_ALPHA * gate)
        return (act @ w2[e] + b2[e]) * g[:, None]

    y = lax.map(expert_block, (blk_e, row_tok.reshape(n_blk, MOE_BLOCK),
                               row_g.reshape(n_blk, MOE_BLOCK)))
    out = jnp.zeros((n_tok, d), h.dtype).at[row_tok].add(y.reshape(n_rows, d))
    return out.reshape(b, s, d)

def second_inputs(seed: int = 0) -> dict:
    key = jax.random.key(seed)
    ks = jax.random.split(key, 24)
    f32 = jnp.float32
    nrm = lambda k, shape, fan_in: jax.random.normal(k, shape, f32) * (fan_in ** -0.5)
    gain = lambda k, shape: 1.0 + 0.05 * jax.random.normal(k, shape, f32)
    L = DEPTH
    return {
        "x": jax.random.normal(ks[0], (BATCH, SEQ, D_MODEL), f32),
        "mem": jax.random.normal(ks[1], (BATCH, N_MEM, D_MODEL), f32),
        "g_mix": gain(ks[2], (L, D_MODEL)),
        "w_in": nrm(ks[3], (L, D_MODEL, IN_PROJ_COLS), D_MODEL),
        "g_sb_out": gain(ks[4], (L, SB_WIDTH)),
        "g_pool_out": gain(ks[5], (L, POOL_WIDTH)),
        "w_pool": nrm(ks[6], (L, POOL_GROUPS, POOL_GROUP_DIM, POOL_GROUP_DIM), POOL_GROUP_DIM),
        "pool_scale": 1.0 + 0.1 * jax.random.normal(ks[7], (L, POOL_WIDTH), f32),
        "w_out": nrm(ks[8], (L, D_MIX_2, D_MODEL), D_MIX_2),
        "g_mem_q": gain(ks[9], (L, D_MODEL)),
        "g_mem_kv": gain(ks[10], (L, D_MODEL)),
        "w_mem_q": nrm(ks[11], (L, D_MODEL, D_MODEL), D_MODEL),
        "w_mem_kv": nrm(ks[12], (L, D_MODEL, 2 * D_MODEL), D_MODEL),
        "w_mem_o": nrm(ks[13], (L, D_MODEL, D_MODEL), D_MODEL),
        "g_ffn": gain(ks[14], (L, D_MODEL)),
        "w_router": nrm(ks[15], (L, D_MODEL, N_EXPERTS_2), D_MODEL),
        "b_router": 0.01 * jax.random.normal(ks[16], (L, N_EXPERTS_2), f32),
        "w_expert_in": nrm(ks[17], (L, N_EXPERTS_2, D_MODEL, 2 * D_FF), D_MODEL),
        "b_expert_in": 0.01 * jax.random.normal(ks[18], (L, N_EXPERTS_2, 2 * D_FF), f32),
        "w_expert_out": nrm(ks[19], (L, N_EXPERTS_2, D_FF, D_MODEL), D_FF),
        "b_expert_out": 0.01 * jax.random.normal(ks[20], (L, N_EXPERTS_2, D_MODEL), f32),
        "g_final": gain(ks[21], (D_MODEL,)),
    }

def second_block(x, mem, g_mix, w_in, g_sb_out, g_pool_out, w_pool, pool_scale, w_out,
              g_mem_q, g_mem_kv, w_mem_q, w_mem_kv, w_mem_o, g_ffn, w_router, b_router,
              w_expert_in, b_expert_in, w_expert_out, b_expert_out, g_final):
    b, s, d = x.shape
    for l in range(DEPTH):
        h = rmsnorm_2(x, g_mix[l])
        proj = h @ w_in[l]
        q = proj[..., :SB_WIDTH].reshape(b, s, SB_HEADS, SB_HEAD_DIM).transpose(0, 2, 1, 3)
        k = proj[..., SB_WIDTH:2 * SB_WIDTH].reshape(b, s, SB_HEADS, SB_HEAD_DIM).transpose(0, 2, 1, 3)
        v = proj[..., 2 * SB_WIDTH:3 * SB_WIDTH].reshape(b, s, SB_HEADS, SB_HEAD_DIM).transpose(0, 2, 1, 3)
        u = proj[..., 3 * SB_WIDTH:].reshape(b, s, POOL_GROUPS, POOL_GROUP_DIM)
        sb = stick_breaking_attention(q, k, v).transpose(0, 2, 1, 3).reshape(b, s, SB_WIDTH)
        pooled = multiscale_pool(u)
        pooled = jnp.einsum('bsgc,gce->bsge', pooled, w_pool[l]).reshape(b, s, POOL_WIDTH) * pool_scale[l]
        mixed = jnp.concatenate([rmsnorm_2(sb, g_sb_out[l]), rmsnorm_2(pooled, g_pool_out[l])], axis=-1)
        x = x + mixed @ w_out[l]
        x = x + memory_cross_attention(rmsnorm_2(x, g_mem_q[l]), rmsnorm_2(mem, g_mem_kv[l]),
                                       w_mem_q[l], w_mem_kv[l], w_mem_o[l])
        x = x + moe_ffn(rmsnorm_2(x, g_ffn[l]), w_router[l], b_router[l], w_expert_in[l],
                        b_expert_in[l], w_expert_out[l], b_expert_out[l])
    return rmsnorm_2(x, g_final)


def setup_inputs(seed=0):
    out = dict(first_inputs(seed))
    for name, value in second_inputs(seed + 1).items():
        if name != "x":
            out[name + "_2"] = value
    return out


def reference(
    x, p, g_mix, w_in, conv_a_w, conv_a_b, ln_a_g, ln_a_b, conv_b_w, ln_c_g, ln_c_b, w_s, b_s,
    w_out, g_ffn, w_q, sub_keys, expert_u, expert_v, g_ple, w_pe, w_pg, g_final, mem_2, g_mix_2,
    w_in_2, g_sb_out_2, g_pool_out_2, w_pool_2, pool_scale_2, w_out_2, g_mem_q_2, g_mem_kv_2,
    w_mem_q_2, w_mem_kv_2, w_mem_o_2, g_ffn_2, w_router_2, b_router_2, w_expert_in_2,
    b_expert_in_2, w_expert_out_2, b_expert_out_2, g_final_2,
):
    x = first_block(
        x, p, g_mix, w_in, conv_a_w, conv_a_b, ln_a_g, ln_a_b, conv_b_w, ln_c_g, ln_c_b, w_s,
        b_s, w_out, g_ffn, w_q, sub_keys, expert_u, expert_v, g_ple, w_pe, w_pg, g_final,
    )
    return second_block(
        x, mem_2, g_mix_2, w_in_2, g_sb_out_2, g_pool_out_2, w_pool_2, pool_scale_2, w_out_2,
        g_mem_q_2, g_mem_kv_2, w_mem_q_2, w_mem_kv_2, w_mem_o_2, g_ffn_2, w_router_2,
        b_router_2, w_expert_in_2, b_expert_in_2, w_expert_out_2, b_expert_out_2, g_final_2,
    )


_drawn_inputs = setup_inputs


def setup_inputs(seed=0):
    import zlib

    import numpy as np

    out = dict(_drawn_inputs(seed))
    spreads = {}
    factors = {'ln_c_b': 2.682,
     'g_mem_q_2': 2.695,
     'b_expert_in_2': 8.0,
     'b_expert_out_2': 8.0,
     'ln_a_b': 2.706,
     'g_ple': 2.695,
     'g_ffn': 3.083}
    for name, (base, spread) in spreads.items():
        noise = np.random.default_rng([zlib.crc32(name.encode()), seed]).standard_normal(out[name].shape)
        drawn = base * np.exp(spread * noise) if base else spread * noise
        out[name] = jnp.asarray(drawn.astype(out[name].dtype))
    for name, factor in factors.items():
        out[name] = (out[name] * factor).astype(out[name].dtype)
    return out
```

```python
from contextlib import ExitStack

import numpy as np

import concourse.bass as bass
from concourse import mybir

ALU = mybir.AluOpType
ACT = mybir.ActivationFunctionType
F32 = mybir.dt.float32
BF16 = mybir.dt.bfloat16
I32 = mybir.dt.int32
U32 = mybir.dt.uint32
AX = mybir.AxisListType.X

P = 128
S = 512
D = 1024
NT = S // P
KD = D // P
NC = 512
D_A, D_B, D_C = 384, 256, 384
TA, TB, TC = D_A // P, D_B // P, D_C // P
IN_COLS = 2 * D_A + 3 * D_B + 2 * D_C
WA, WB = 31, 3
HC = 6
HH = 16
PH = 8
NK = 128
TOPK = 16
PLE = 256
SBH = 8
HD = 64
WINS = (2, 4, 8, 16)
PADU = 16
NMEM = 256
TM = NMEM // P
MH = 4
NE = 32
EK = 4
FF = 1024
EPS1, EPS2 = 1e-6, 1e-5
NBLK = 47
NBP = 48
LEAST_LIVE = S * EK // P
GRP = 8
LOWEST = -3.0e38

_C = {}
_n = 0
for _name, _w in (("ident", P), ("lt", P), ("gt", P), ("ones", P), ("bones", P), ("wsmask", P),
                  ("iota", NBP), ("tok", NT), ("emod", P), ("rcount", 4 * PADU), ("zero", P), ("eps", 2)):
    _C[_name] = (_n, _w)
    _n += _w
NCONST = _n

_Q = {}
_n = 0
for _name, _w in (("g_mix", KD), ("conv_a_w", TA * WA), ("conv_a_b", TA), ("ln_a_g", TA), ("ln_a_b", TA),
                  ("conv_b_w", TB * WB), ("g_ple", KD), ("g_mix_2", KD), ("g_sb", 4), ("g_pool", 4),
                  ("pool_scale", 4), ("g_mem_q", KD), ("g_mem_kv", KD), ("b_s", TC * P)):
    _Q[_name] = (_n, _w)
    _n += _w
NPAR = _n


def constants():
    c = np.zeros((P, NCONST), np.float32)
    p = np.arange(P)[:, None]
    m = np.arange(P)[None, :]

    def put(name, a):
        o, w = _C[name]
        c[:, o:o + w] = a

    put("ident", p == m)
    put("lt", p < m)
    put("gt", p > m)
    put("ones", 1.0)
    put("bones", (p // HD == m // HD) / HD)
    put("wsmask", p // HD <= m // HD)
    put("iota", np.arange(NBP)[None, :])
    put("tok", p + P * np.arange(NT)[None, :])
    put("emod", p % NE + 0 * m)
    t = np.arange(PADU)
    put("rcount", np.concatenate([1.0 / np.minimum(t + 1, w) for w in WINS])[None, :])
    put("eps", np.array([[EPS1, EPS2]]))
    return c


class Steps:

    def __init__(self, start, labels):
        self.start, self.labels = start, list(labels)
        self.at = {label: start + i + 1 for i, label in enumerate(self.labels)}

    def __getitem__(self, label):
        return self.at[label]

    def end(self):
        return self.start + len(self.labels)


def build(nc, t, out):
    ctx = ExitStack()
    with ctx:
        def sb(name, shape, dt=F32):
            return ctx.enter_context(nc.sbuf_tensor(name, shape, dt))

        def sem(name):
            return ctx.enter_context(nc.semaphore(name))

        wring = [sb(f"wring{i}", [P, KD * NC]) for i in range(4)]
        X = sb("work", [P, 4 * KD * NC])
        h = sb("h", [P, NT, D])
        aT = sb("aT", [P, KD, S])
        tok = sb("tok", [P, NT, D])
        mixT = tok[:, :, :].rearrange("p t d -> p (t d)").rearrange("p (k s) -> p k s", k=KD)
        cst = sb("cst", [P, NCONST])
        par = sb("par", [P, NPAR])
        grow = sb("grow", [P, D])
        stat = sb("stat", [P, 64])
        bank = ctx.enter_context(nc.psum_tensor("banks", [P, 8, NC], F32))

        def const(name, lo=0, hi=None):
            o, w = _C[name]
            return cst[:, o + lo:o + (w if hi is None else hi)]

        def param(name, lo=0, hi=None):
            o, w = _Q[name]
            return par[:, o + lo:o + (w if hi is None else hi)]

        ident = const("ident")

        xn_dram = nc.dram_tensor("ffn_rows", (S, D), F32).ap()
        tokmap_dram = nc.dram_tensor("slot_tokens", (P * NBP, 1), I32).ap()
        y_dram = nc.dram_tensor("expert_rows", (NBP * P, D), F32).ap()

        pe_done = sem("pe_done")
        dve_done = sem("dve_done")
        act_done = sem("act_done")
        pool_done = sem("pool_done")
        first_in = sem("first_in")
        late_in = sem("late_in")
        rows_filled = sem("rows_filled")
        row_in = sem("row_in")
        chunk_in = [sem(f"chunk_in{i}") for i in range(4)]
        at = {"pe": 0, "dve": 0, "act": 0, "pool": 0, "late": 0, "row": 0}

        def steps(eng, labels):
            s = Steps(at[eng], labels)
            at[eng] = s.end()
            return s

        def cols(w, lo, n=NC, k=KD):
            return w.rearrange("(k p) n -> p k n", p=P)[:, 0:k, lo:lo + n], k, n

        w_in, w_in2 = t["w_in"][0], t["w_in_2"][0]
        chunks = [cols(w_in, c) for c in (0, 512, 1024)] + [cols(w_in, 1536, D_C), cols(w_in, 1536 + D_C, D_C)]
        chunks += [cols(t["w_out"][0], c) for c in (0, 512)]
        chunks += [cols(t["w_q"][0], c) for c in (0, 512, 1024, 1536)]
        chunks += [cols(t["w_pg"][0], c) for c in (0, 512)]
        chunks += [cols(t["w_pe"][0], 0, D, PLE // P)]
        chunks += [cols(w_in2, c) for c in (0, 512, 1024, 1536)]
        chunks += [cols(t["w_out_2"][0], c) for c in (0, 512)]
        chunks += [cols(t["w_mem_kv_2"][0], c) for c in (0, 512, 1024, 1536)]
        chunks += [cols(t["w_mem_q_2"][0], c) for c in (0, 512)]
        chunks += [cols(t["w_mem_o_2"][0], c) for c in (0, 512)]
        (C_IN, C_OUT, C_Q, C_PG, C_PE, C_IN2, C_OUT2, C_KV, C_MQ, C_MO) = (0, 5, 7, 11, 13, 14, 18, 20, 24, 26)

        def chunk_view(i):
            _, k, n = chunks[i]
            return wring[i % 4][:, 0:k * n].rearrange("p (k n) -> p k n", k=k)

        def load_chunk(sp, i):
            if i < len(chunks):
                sp.dma_start(chunk_view(i), chunks[i][0]).then_inc(chunk_in[i % 4], 16)

        def wait_chunk(eng, i):
            eng.wait_ge(chunk_in[i % 4], 16 * (i // 4 + 1))

        def dense(jobs, before_sp=None, after_dve=None):
            pe = steps("pe", range(len(jobs)))
            dv = steps("dve", [j for j, job in enumerate(jobs) if job[3] == "dve"])
            ac = steps("act", [j for j, job in enumerate(jobs) if job[3] == "act"])

            def evacuated(j):
                return (dve_done, dv[j]) if jobs[j][3] == "dve" else (act_done, ac[j])

            last_of = {}
            for j, job in enumerate(jobs):
                last_of[job[0]] = j
            with nc.Block() as block:
                @block.sync
                def _(sp):
                    if before_sp:
                        before_sp(sp)
                    for c, j in last_of.items():
                        sp.wait_ge(pe_done, pe[j])
                        load_chunk(sp, c + 4)

                @block.tensor
                def _(eng):
                    seen = set()
                    for j, (c, mms, _, _, _, _) in enumerate(jobs):
                        if c not in seen:
                            wait_chunk(eng, c)
                            seen.add(c)
                        if j >= 8:
                            eng.wait_ge(*evacuated(j - 8))
                        for i, (dst, lhsT, rhs, start, stop) in enumerate(mms):
                            mm = nc.tensor.matmul(dst(j % 8), lhsT, rhs, start=start, stop=stop)
                        mm.then_inc(pe_done, 1)

                def evacuate(eng, which, s, done):
                    for j, job in enumerate(jobs):
                        if job[3] != which:
                            continue
                        eng.wait_ge(pe_done, pe[j])
                        if job[5] is not None:
                            eng.wait_ge(*evacuated(job[5]))
                        job[4](j % 8).then_inc(done, 1)

                @block.vector
                def _(eng):
                    evacuate(eng, "dve", dv, dve_done)

                @block.scalar
                def _(eng):
                    evacuate(eng, "act", ac, act_done)

        def whole(n=NC, rows=P):
            return lambda b: bank[0:rows, b, 0:n]

        def t_job(c, col, src, n, who, evac, after=None, m=P):
            w = chunk_view(c)
            k = chunks[c][1]
            mms = [(whole(n), w[:, i, col:col + m], src[:, i, 0:n], i == 0, i == k - 1) for i in range(k)]
            return (c, mms, m, who, evac, after)

        def tok_job(c, col, n, src, tt, who, evac, after=None):
            w = chunk_view(c)
            k = chunks[c][1]
            mms = [(whole(n), src[:, i, tt * P:(tt + 1) * P], w[:, i, col:col + n], i == 0, i == k - 1)
                   for i in range(k)]
            return (c, mms, P, who, evac, after)

        def normalise(src, ntt, eps_col, gain, dst, dstT, row=None, row_ap=None, sp_work=None):
            ac = steps("act", [("sq", i) for i in range(ntt)] + ["sd"] + [("out", k) for k in range(1, KD, 2)])
            dv = steps("dve", ["rstd"] + [("scale", i) for i in range(ntt)] + [("out", k) for k in range(0, KD, 2)])
            pe = steps("pe", range(KD))
            ss, sd, rstd = stat[:, 0:ntt], stat[:, 4:4 + ntt], stat[:, 8:8 + ntt]
            if row_ap is not None:
                at["row"] += 16
            row_at = at["row"]
            with nc.Block() as block:
                @block.sync
                def _(sp):
                    if row_ap is not None:
                        sp.dma_start(grow[:, :], row_ap.to_broadcast([P, D])).then_inc(row_in, 16)
                    if sp_work:
                        sp_work(sp)

                @block.scalar
                def _(eng):
                    for i in range(ntt):
                        nc.scalar.activation(dst[:, i, :], src[:, i, :], ACT.Square,
                                             accum_out=ss[:, i:i + 1]).then_inc(act_done, 1)
                    eng.wait_ge(act_done, ac["sq", ntt - 1])
                    nc.scalar.activation(sd, ss, ACT.Sqrt, scale=1.0 / D,
                                         bias=const("eps", eps_col, eps_col + 1)).then_inc(act_done, 1)
                    for k in range(1, KD, 2):
                        eng.wait_ge(pe_done, pe[k])
                        g = 1.0 if gain is None else gain[:, k:k + 1]
                        nc.scalar.activation(dstT[:, k, 0:ntt * P], bank[:, k, 0:ntt * P], ACT.Copy,
                                             scale=g).then_inc(act_done, 1)

                @block.vector
                def _(eng):
                    eng.wait_ge(act_done, ac["sd"])
                    nc.vector.reciprocal(rstd, sd).then_inc(dve_done, 1)
                    eng.wait_ge(dve_done, dv["rstd"])
                    if row is not None:
                        eng.wait_ge(row_in, row_at)
                    for i in range(ntt):
                        if row is None:
                            ins = nc.vector.tensor_scalar(dst[:, i, :], src[:, i, :], rstd[:, i:i + 1], None, ALU.mult)
                        else:
                            ins = nc.vector.scalar_tensor_tensor(out=dst[:, i, :], in0=src[:, i, :],
                                                                 scalar=rstd[:, i:i + 1], in1=row[:, :],
                                                                 op0=ALU.mult, op1=ALU.mult)
                        ins.then_inc(dve_done, 1)
                    for k in range(0, KD, 2):
                        eng.wait_ge(pe_done, pe[k])
                        if gain is None:
                            ins = nc.vector.tensor_copy(dstT[:, k, 0:ntt * P], bank[:, k, 0:ntt * P])
                        else:
                            ins = nc.vector.tensor_scalar(dstT[:, k, 0:ntt * P], bank[:, k, 0:ntt * P],
                                                          gain[:, k:k + 1], None, ALU.mult)
                        ins.then_inc(dve_done, 1)

                @block.tensor
                def _(eng):
                    for k in range(KD):
                        for i in range(ntt):
                            if k == 0:
                                eng.wait_ge(dve_done, dv["scale", i])
                            mm = nc.tensor.transpose(bank[:, k, i * P:(i + 1) * P], dst[:, i, k * P:(k + 1) * P], ident)
                        mm.then_inc(pe_done, 1)

        def final_norm(src, eps_col, row_ap, dst, junk, done_sp=None):
            ac = steps("act", [("sq", i) for i in range(NT)] + ["sd"])
            dv = steps("dve", ["rstd"] + [("scale", i) for i in range(NT)])
            ss, sd, rstd = stat[:, 0:NT], stat[:, 4:4 + NT], stat[:, 8:8 + NT]
            at["row"] += 16
            row_at = at["row"]
            with nc.Block() as block:
                @block.sync
                def _(sp):
                    sp.dma_start(grow[:, :], row_ap.to_broadcast([P, D])).then_inc(row_in, 16)
                    if done_sp:
                        done_sp(sp, dv)

                @block.scalar
                def _(eng):
                    for i in range(NT):
                        nc.scalar.activation(junk[:, i, :], src[:, i, :], ACT.Square,
                                             accum_out=ss[:, i:i + 1]).then_inc(act_done, 1)
                    eng.wait_ge(act_done, ac["sq", NT - 1])
                    nc.scalar.activation(sd, ss, ACT.Sqrt, scale=1.0 / D,
                                         bias=const("eps", eps_col, eps_col + 1)).then_inc(act_done, 1)

                @block.vector
                def _(eng):
                    eng.wait_ge(act_done, ac["sd"])
                    nc.vector.reciprocal(rstd, sd).then_inc(dve_done, 1)
                    eng.wait_ge(dve_done, dv["rstd"])
                    eng.wait_ge(row_in, row_at)
                    for i in range(NT):
                        nc.vector.scalar_tensor_tensor(out=dst[:, i, :], in0=src[:, i, :], scalar=rstd[:, i:i + 1],
                                                       in1=grow[:, :], op0=ALU.mult, op1=ALU.mult).then_inc(dve_done, 1)

        def add_to_h(tt, lo, n=NC):
            def evac(b):
                return nc.vector.tensor_tensor(h[:, tt, lo:lo + n], h[:, tt, lo:lo + n], bank[:, b, 0:n], ALU.add)
            return evac

        def project_into_h(c0, src):
            dense([tok_job(c0 + n, 0, NC, src, tt, "dve", add_to_h(tt, n * NC)) for n in range(2) for tt in range(NT)])

        def region(lo, n):
            return X[:, lo:lo + n]

        o = 0
        zT = region(o, 15 * S).rearrange("p (c s) -> p c s", c=15)
        o += 15 * S
        vt = region(o, NT * D_C).rearrange("p (t n) -> p t n", t=NT)
        o += NT * D_C
        LA = S + WA - 1
        ya_in = region(o, TA * LA).rearrange("p (c s) -> p c s", c=TA)
        o += TA * LA
        acc = region(o, TA * S).rearrange("p (c s) -> p c s", c=TA)
        o += TA * S
        LB = S + WB - 1
        yb_in = region(o, TB * LB).rearrange("p (c s) -> p c s", c=TB)
        o += TB * LB
        yb_t = region(o, TB * S).rearrange("p (c s) -> p c s", c=TB)
        o += TB * S
        lnc = region(o, 2 * D_C)
        o += 2 * D_C
        wsT = region(o, HC * P).rearrange("p (h i) -> p h i", h=HC)
        o += HC * P
        assert o <= 4 * KD * NC
        VAL, GATE, BG, CG, XB, U = 0, TA, 2 * TA, 2 * TA + TB, 2 * TA + 2 * TB, 2 * TA + 3 * TB

        with nc.Block() as block:
            @block.sync
            def _(sp):
                sp.dma_start(h[:, :, :], t["x"][0].rearrange("(t p) d -> p t d", p=P)).then_inc(first_in, 16)
                sp.dma_start(cst[:, :], t["consts"][:, :]).then_inc(first_in, 16)
                sp.dma_start(par[:, :], t["params"][:, :]).then_inc(first_in, 16)
                load_chunk(sp, 0)
                sp.dma_start(wsT[:, :, :], t["w_s_T"][:, :, :]).then_inc(first_in, 16)
                sp.dma_start(lnc[:, 0:D_C], t["ln_c_g"][0:1, :].to_broadcast([P, D_C])).then_inc(first_in, 16)
                sp.dma_start(lnc[:, D_C:2 * D_C], t["ln_c_b"][0:1, :].to_broadcast([P, D_C])).then_inc(first_in, 16)
                for c in range(1, 4):
                    load_chunk(sp, c)
                sp.wait_ge(first_in, 96)

        normalise(h, NT, 0, param("g_mix"), tok, aT)

        def copy_z(c, who):
            if who == "act":
                f = ACT.Sigmoid if GATE <= c < BG else ACT.Copy
                return lambda b: nc.scalar.activation(zT[:, c, :], bank[:, b, :], f)
            return lambda b: nc.vector.tensor_copy(zT[:, c, :], bank[:, b, :])

        jobs = []
        for c in range(15):
            who = "act" if GATE <= c < BG or c % 2 else "dve"
            jobs.append(t_job(C_IN + c * P // NC, c * P % NC, aT, S, who, copy_z(c, who)))
        for tt in range(NT):
            jobs.append(tok_job(C_IN + 4, 0, D_C, aT, tt, "dve",
                                lambda b, tt=tt: nc.vector.tensor_copy(vt[:, tt, :], bank[:, b, 0:D_C])))
        dense(jobs)

        v24 = vt[:, :, :].rearrange("p t (h c) -> p (t h) c", h=HC)
        sq24 = acc[:, :, :].rearrange("p c s -> p (c s)").rearrange("p (g c) -> p g c", c=HD)
        m24, s24, r24 = stat[:, 12:36], stat[:, 36:60], stat[:, 12:36]
        nG = NT * HC

        def over(x, n):
            return x.rearrange("p (g o) -> p g o", o=1).to_broadcast([P, x.shape[1], n])

        def over_t(x):
            return x.rearrange("p (o n) -> p o n", o=1).to_broadcast([P, NT, x.shape[1]])

        dv = steps("dve", ["vsum", "vmean", "vsub", "vvar", "vr", "vscale", "vg", "vb"]
                   + [("pad", c) for c in range(TA)] + [("glu", c) for c in range(TA)]
                   + [("tap", k, c) for k in range(WA) for c in range(TA)]
                   + [("u1", i) for i in range(TC)] + [("u2", i) for i in range(TC)]
                   + [("am", c) for c in range(TA)] + [("ar", c) for c in range(TA)]
                   + [("as", c) for c in range(TA)])
        ac = steps("act", ["vsq", "vsd"] + [("asq", c) for c in range(TA)] + [("asd", c) for c in range(TA)]
                   + [("silu", c) for c in range(TA)])
        pe = steps("pe", [("mix", i) for i in range(TC)] + [("am", c) for c in range(TA)] + [("av", c) for c in range(TA)])
        po = steps("pool", ["ws", "pad"] + [("g", c) for c in range(TB)]
                   + [("t", k, c) for k in range(WB) for c in range(TB)]
                   + [("s", k, c) for k in range(1, WB) for c in range(TB)] + [("out", c) for c in range(TB)])
        with nc.Block() as block:
            @block.scalar
            def _(eng):
                eng.wait_ge(dve_done, dv["vsub"])
                nc.scalar.activation(sq24, v24, ACT.Square).then_inc(act_done, 1)
                eng.wait_ge(dve_done, dv["vvar"])
                nc.scalar.activation(s24, s24, ACT.Sqrt, scale=1.0 / HD, bias=const("eps", 0, 1)).then_inc(act_done, 1)
                for c in range(TA):
                    eng.wait_ge(dve_done, dv["am", c])
                    nc.scalar.activation(zT[:, GATE + c, :], acc[:, c, :], ACT.Square).then_inc(act_done, 1)
                for c in range(TA):
                    eng.wait_ge(pe_done, pe["av", c])
                    nc.scalar.activation(zT[:, VAL + c, :], bank[:, 3 + c, :], ACT.Sqrt,
                                         bias=const("eps", 0, 1)).then_inc(act_done, 1)
                for c in range(TA):
                    eng.wait_ge(dve_done, dv["as", c])
                    nc.scalar.activation(mixT[:, c, :], acc[:, c, :], ACT.Silu, scale=param("ln_a_g", c, c + 1),
                                         bias=param("ln_a_b", c, c + 1)).then_inc(act_done, 1)

            @block.vector
            def _(eng):
                nc.vector.tensor_reduce(m24, v24, AX, ALU.add).then_inc(dve_done, 1)
                eng.wait_ge(dve_done, dv["vsum"])
                nc.vector.tensor_scalar(m24, m24, 1.0 / HD, None, ALU.mult).then_inc(dve_done, 1)
                eng.wait_ge(dve_done, dv["vmean"])
                nc.vector.tensor_tensor(v24, v24, over(m24, HD), ALU.subtract).then_inc(dve_done, 1)
                eng.wait_ge(act_done, ac["vsq"])
                nc.vector.tensor_reduce(s24, sq24, AX, ALU.add).then_inc(dve_done, 1)
                eng.wait_ge(act_done, ac["vsd"])
                nc.vector.reciprocal(r24, s24).then_inc(dve_done, 1)
                eng.wait_ge(dve_done, dv["vr"])
                nc.vector.tensor_tensor(v24, v24, over(r24, HD), ALU.mult).then_inc(dve_done, 1)
                eng.wait_ge(dve_done, dv["vscale"])
                nc.vector.tensor_tensor(vt[:, :, :], vt[:, :, :], over_t(lnc[:, 0:D_C]), ALU.mult).then_inc(dve_done, 1)
                eng.wait_ge(dve_done, dv["vg"])
                nc.vector.tensor_tensor(vt[:, :, :], vt[:, :, :], over_t(lnc[:, D_C:2 * D_C]), ALU.add).then_inc(dve_done, 1)
                for c in range(TA):
                    nc.vector.memset(ya_in[:, c, 0:WA - 1], 0.0).then_inc(dve_done, 1)
                for c in range(TA):
                    nc.vector.tensor_tensor(ya_in[:, c, WA - 1:LA], zT[:, VAL + c, :], zT[:, GATE + c, :],
                                            ALU.mult).then_inc(dve_done, 1)
                for k in range(WA):
                    for c in range(TA):
                        w = param("conv_a_w", c * WA + k, c * WA + k + 1)
                        if k == 0:
                            eng.wait_ge(dve_done, dv["glu", c])
                            ins = nc.vector.tensor_scalar(acc[:, c, :], ya_in[:, c, 0:S], w,
                                                          param("conv_a_b", c, c + 1), ALU.mult, ALU.add)
                        else:
                            eng.wait_ge(dve_done, dv["tap", k - 1, c])
                            ins = nc.vector.scalar_tensor_tensor(out=acc[:, c, :], in0=ya_in[:, c, k:k + S], scalar=w,
                                                                 in1=acc[:, c, :], op0=ALU.mult, op1=ALU.add)
                        ins.then_inc(dve_done, 1)
                for i in range(TC):
                    eng.wait_ge(pe_done, pe["mix", i])
                    mixed = mixT[:, TA + TB + i, :].rearrange("p (t i) -> p t i", t=NT)
                    nc.vector.tensor_tensor(mixed, bank[:, i, :].rearrange("p (t i) -> p t i", t=NT),
                                            over_t(param("b_s", i * P, (i + 1) * P)), ALU.add).then_inc(dve_done, 1)
                for i in range(TC):
                    eng.wait_ge(dve_done, dv["u1", i])
                    nc.vector.tensor_tensor(mixT[:, TA + TB + i, :], mixT[:, TA + TB + i, :], zT[:, U + i, :],
                                            ALU.mult).then_inc(dve_done, 1)
                for c in range(TA):
                    eng.wait_ge(pe_done, pe["am", c])
                    nc.vector.tensor_tensor(acc[:, c, :], acc[:, c, :], bank[:, 4 + c % 4, :], ALU.subtract).then_inc(dve_done, 1)
                for c in range(TA):
                    eng.wait_ge(act_done, ac["asd", c])
                    nc.vector.reciprocal(zT[:, VAL + c, :], zT[:, VAL + c, :]).then_inc(dve_done, 1)
                for c in range(TA):
                    eng.wait_ge(dve_done, dv["ar", c])
                    nc.vector.tensor_tensor(acc[:, c, :], acc[:, c, :], zT[:, VAL + c, :], ALU.mult).then_inc(dve_done, 1)

            @block.tensor
            def _(eng):
                eng.wait_ge(dve_done, dv["vb"])
                eng.wait_ge(pool_done, po["ws"])
                for i in range(TC):
                    for tt in range(NT):
                        for half in range(2):
                            hd = 2 * i + half
                            mm = nc.tensor.matmul(bank[half * HD:(half + 1) * HD, i, tt * P:(tt + 1) * P],
                                                  vt[:, tt, hd * HD:(hd + 1) * HD], wsT[:, hd, :],
                                                  start=True, stop=True)
                    mm.then_inc(pe_done, 1)
                for c in range(TA):
                    eng.wait_ge(dve_done, dv["tap", WA - 1, c])
                    nc.tensor.matmul(bank[:, 4 + c % 4, :], const("bones"), acc[:, c, :],
                                     start=True, stop=True).then_inc(pe_done, 1)
                for c in range(TA):
                    eng.wait_ge(act_done, ac["asq", c])
                    if c == 0:
                        eng.wait_ge(dve_done, dv["u1", TC - 1])
                        eng.wait_ge(dve_done, dv["am", TA - 1])
                    nc.tensor.matmul(bank[:, 3 + c, :], const("bones"), zT[:, GATE + c, :],
                                     start=True, stop=True).then_inc(pe_done, 1)

            @block.gpsimd
            def _(eng):
                eng.tensor_tensor(wsT[:, :, :], wsT[:, :, :],
                                  const("wsmask").rearrange("p (o i) -> p o i", o=1).to_broadcast([P, HC, P]),
                                  ALU.mult).then_inc(pool_done, 1)
                eng.memset(yb_in[:, :, 0:WB - 1], 0.0).then_inc(pool_done, 1)
                for c in range(TB):
                    eng.tensor_tensor(yb_in[:, c, WB - 1:LB], zT[:, CG + c, :], zT[:, XB + c, :], ALU.mult).then_inc(pool_done, 1)
                eng.wait_ge(pool_done, po["g", TB - 1])
                dst = [zT[:, CG:CG + TB, :], zT[:, XB:XB + TB, :], yb_t]
                for k in range(WB):
                    for c in range(TB):
                        w = param("conv_b_w", c * WB + k, c * WB + k + 1)
                        eng.tensor_scalar(dst[k][:, c, :], yb_in[:, c, k:k + S], w, None, ALU.mult).then_inc(pool_done, 1)
                for k in range(1, WB):
                    for c in range(TB):
                        eng.wait_ge(pool_done, po["t", k, c] if k == 1 else po["s", k - 1, c])
                        if k > 1:
                            eng.wait_ge(pool_done, po["t", k, c])
                        eng.tensor_tensor(dst[0][:, c, :], dst[0][:, c, :], dst[k][:, c, :], ALU.add).then_inc(pool_done, 1)
                for c in range(TB):
                    eng.wait_ge(pool_done, po["s", WB - 1, c])
                    eng.tensor_tensor(mixT[:, TA + c, :], dst[0][:, c, :], zT[:, BG + c, :], ALU.mult).then_inc(pool_done, 1)

        project_into_h(C_OUT, mixT)

        SC0 = 0
        scores = region(0, NT * HH * NK).rearrange("p (t g k) -> p t g k", t=NT, g=HH)
        qT = region(8192, 4 * S).rearrange("p (c s) -> p c s", c=4)
        keysT = region(10240, HH * NK).rearrange("p (g k) -> p g k", g=HH)
        at["late"] += 16
        keys_at = at["late"]
        normalise(h, NT, 0, None, tok, aT, row=grow, row_ap=t["g_ffn"][0:1, :],
                  sp_work=lambda sp: sp.dma_start(keysT[:, :, :], t["sub_keys_T"][:, :, :]).then_inc(late_in, 16))

        pe = steps("pe", [x for g in range(HH + 1) for x in ([("q", g)] if g < HH else []) + ([("s", g - 1)] if g else [])])
        ac = steps("act", [("q", g) for g in range(HH)])
        dv = steps("dve", [("s", g) for g in range(HH)])
        with nc.Block() as block:
            @block.sync
            def _(sp):
                for c in range(4):
                    sp.wait_ge(pe_done, pe["q", 4 * c + 3])
                    load_chunk(sp, C_Q + c + 4)

            @block.tensor
            def _(eng):
                eng.wait_ge(late_in, keys_at)
                for g in range(HH + 1):
                    if g < HH:
                        if g % 4 == 0:
                            wait_chunk(eng, C_Q + g // 4)
                        if g >= 4:
                            eng.wait_ge(act_done, ac["q", g - 4])
                        w = chunk_view(C_Q + g // 4)
                        for k in range(KD):
                            mm = nc.tensor.matmul(bank[:, g % 4, :], w[:, k, g % 4 * P:(g % 4 + 1) * P], aT[:, k, :],
                                                  start=k == 0, stop=k == KD - 1)
                        mm.then_inc(pe_done, 1)
                    if g:
                        s = g - 1
                        eng.wait_ge(act_done, ac["q", s])
                        if s >= 4:
                            eng.wait_ge(dve_done, dv["s", s - 4])
                        for tt in range(NT):
                            mm = nc.tensor.matmul(bank[:, 4 + s % 4, tt * NK:(tt + 1) * NK],
                                                  qT[:, s % 4, tt * P:(tt + 1) * P], keysT[:, s, :], start=True, stop=True)
                        mm.then_inc(pe_done, 1)

            @block.scalar
            def _(eng):
                for g in range(HH):
                    eng.wait_ge(pe_done, pe["q", g])
                    if g >= 4:
                        eng.wait_ge(pe_done, pe["s", g - 4])
                    nc.scalar.activation(qT[:, g % 4, :], bank[:, g % 4, :], ACT.Copy).then_inc(act_done, 1)

            @block.vector
            def _(eng):
                for g in range(HH):
                    eng.wait_ge(pe_done, pe["s", g])
                    nc.vector.tensor_copy(scores[:, :, g, :], bank[:, 4 + g % 4, :].rearrange("p (t k) -> p t k", t=NT))\
                      .then_inc(dve_done, 1)

        SW = region(8192, HH * NK).rearrange("p (g k) -> p g k", g=HH)
        cand = region(10240, PH * TOPK * TOPK).rearrange("p (h c) -> p h c", h=PH)
        hot = region(12288, PH * TOPK * TOPK)
        o = 14336
        kv = region(o, HH * TOPK).rearrange("p (g k) -> p g k", g=HH)
        ki = region(o + 256, HH * TOPK).bitcast(U32).rearrange("p (g k) -> p g k", g=HH)
        kf = region(o + 512, HH * TOPK).rearrange("p (g k) -> p g k", g=HH)
        cv = region(o + 768, PH * TOPK).rearrange("p (h k) -> p h k", h=PH)
        ci = region(o + 896, PH * TOPK).bitcast(U32)
        cq = region(o + 1024, 2 * PH * TOPK).bitcast(U32)
        cf = region(o + 1280, 2 * PH * TOPK)
        ef = region(o + 1536, 2 * PH * TOPK)
        sm = region(o + 1792, 2 * PH)
        ce = region(o + 1808, PH * TOPK).rearrange("p (h k) -> p h k", h=PH)
        GK = PH * TOPK
        gates = sb("gates", [P, NT * GK])
        eidx = sb("eidx", [P, NT * GK], I32)
        top = sem("top_steps")
        differ = sem("top_differ")
        exps = sem("top_exp")

        def top_program():
            prog = []

            def step(need, f):
                prog.append((need, f))
                return len(prog)

            def best(src, v, i, pre):
                a = step(pre, lambda: nc.vector.max(v[:, 0:8], src))
                b = step(a, lambda: nc.vector.max_index(i[:, 0:8], v[:, 0:8], src))
                c = step(b, lambda: nc.vector.match_replace(src, v[:, 0:8], src, LOWEST))
                d = step(c, lambda: nc.vector.max(v[:, 8:16], src))
                return step(d, lambda: nc.vector.max_index(i[:, 8:16], v[:, 8:16], src))
            return prog, step, best

        with nc.Block() as block:
            prog, step, best = top_program()
            first = step(0, None)
            last = first
            for g in range(HH):
                last = best(SW[:, g, :], kv[:, g, :], ki[:, g, :], first)
            a = step(last, lambda: nc.vector.tensor_copy(kf, ki))
            kv4 = kv.rearrange("p (h two) k -> p h two k", two=2)
            kf4 = kf.rearrange("p (h two) k -> p h two k", two=2)
            c4 = cand.rearrange("p h (i j) -> p h i j", i=TOPK)
            for hd in range(PH):
                s = step(last, lambda hd=hd: nc.vector.tensor_tensor(
                    c4[:, hd], kv4[:, hd, 0, :].rearrange("p (i o) -> p i o", o=1).to_broadcast([P, TOPK, TOPK]),
                    kv4[:, hd, 1, :].rearrange("p (o j) -> p o j", o=1).to_broadcast([P, TOPK, TOPK]), ALU.add))
            lastc = s
            for hd in range(PH):
                lastc = best(cand[:, hd, :], cv[:, hd, :], ci[:, hd * TOPK:(hd + 1) * TOPK], s)
            s1 = step(lastc, lambda: nc.vector.tensor_scalar(cq[:, 0:GK], ci, 4, None, ALU.logical_shift_right))
            s2 = step(lastc, lambda: nc.vector.tensor_scalar(cq[:, GK:2 * GK], ci, 15, None, ALU.bitwise_and))
            s3 = step(s2, lambda: nc.vector.tensor_copy(cf, cq))
            hot3 = hot.rearrange("p (c i) -> p c i", i=TOPK)
            hot4 = hot.rearrange("p (h c i) -> p h c i", h=PH, i=TOPK)
            iota16 = const("iota", 0, TOPK).rearrange("p (o i) -> p o i", o=1).to_broadcast([P, GK, TOPK])
            s6 = s3
            for half in range(2):
                s4 = step(s6, lambda half=half: nc.vector.tensor_tensor(
                    hot3, cf[:, half * GK:(half + 1) * GK].rearrange("p (c o) -> p c o", o=1).to_broadcast([P, GK, TOPK]),
                    iota16, ALU.is_equal))
                s5 = s4
                for hd in range(PH):
                    s5 = step(s4, lambda half=half, hd=hd: nc.vector.tensor_tensor(
                        hot4[:, hd], hot4[:, hd],
                        kf4[:, hd, half, :].rearrange("p (o i) -> p o i", o=1).to_broadcast([P, TOPK, TOPK]), ALU.mult))
                s6 = step(s5, lambda half=half: nc.vector.tensor_reduce(ef[:, half * GK:(half + 1) * GK], hot3, AX, ALU.add))
            IDX = step(s6, None)
            SUB = step(lastc, lambda: nc.vector.tensor_tensor(
                ce, cv, cv[:, :, 0:1].to_broadcast([P, PH, TOPK]), ALU.subtract))
            s7 = step(SUB, lambda: nc.vector.tensor_reduce(sm[:, 0:PH], ce, AX, ALU.add))
            s8 = step(s7, lambda: nc.vector.reciprocal(sm[:, PH:2 * PH], sm[:, 0:PH]))
            GAT = step(s8, None)
            NSTEP = len(prog)

            @block.vector
            def _(eng):
                with eng.Fori(0, NT) as tt:
                    for n, (need, f) in enumerate(prog):
                        if n + 1 == s7:
                            eng.wait_ge(exps, tt + 1)
                        elif need:
                            eng.wait_ge(top, need - (need > SUB))
                        if n + 1 == first:
                            ins = nc.vector.tensor_copy(SW, X[:, bass.ds(tt * (HH * NK), HH * NK)]
                                                        .rearrange("p (g k) -> p g k", g=HH))
                        elif n + 1 == IDX:
                            ins = nc.vector.scalar_tensor_tensor(
                                out=eidx[:, bass.ds(tt * GK, GK)], in0=ef[:, 0:GK], scalar=float(NK),
                                in1=ef[:, GK:2 * GK], op0=ALU.mult, op1=ALU.add)
                        elif n + 1 == GAT:
                            ins = nc.vector.tensor_tensor(
                                gates[:, bass.ds(tt * GK, GK)].rearrange("p (h k) -> p h k", h=PH), ce,
                                over(sm[:, PH:2 * PH], TOPK), ALU.mult)
                        else:
                            ins = f()
                        ins.then_inc(differ if n + 1 == SUB else top, 1)
                    eng.wait_ge(top, NSTEP - 1)
                    eng.sem_clear(top)

            @block.scalar
            def _(eng):
                with eng.Fori(0, NT) as tt:
                    eng.wait_ge(differ, tt + 1)
                    nc.scalar.activation(ce, ce, ACT.Exp).then_inc(exps, 1)

        slot = [region(j * D, D) for j in range(GRP)]
        o = GRP * D
        dots = region(o, GK)
        acts = region(o + GK, GK)
        diag = region(o + 2 * GK, 2 * P).rearrange("p (b m) -> p b m", b=2)
        cur = region(o + 2 * GK + 2 * P, 2 * GRP).bitcast(I32)
        row_in_slot = [sem(f"row_in_slot{j}") for j in range(GRP)]
        u_used = sem("u_used")
        v_used = sem("v_used")
        cur_ready = sem("cur_ready")
        pool_turn = sem("pool_turn")
        gelu_done = sem("gelu_done")
        acts_done = sem("acts_done")
        diag_done = sem("diag_done")
        acc_zero = sem("acc_zero")
        acc_free = sem("acc_free")
        u_rows, v_rows = t["expert_u"][0], t["expert_v"][0]
        NG = GK // GRP
        h2 = h[:, :, :].rearrange("p t d -> p (t d)")
        tok2 = tok[:, :, :].rearrange("p t d -> p (t d)")
        with nc.Block() as block:
            @block.gpsimd
            def _(eng):
                def gather(rows, tt, g, side, turn, free):
                    ix = cur[:, side * GRP:(side + 1) * GRP]
                    eng.tensor_copy(ix, eidx[:, bass.ds(tt * GK + g * GRP, GRP)]).then_inc(cur_ready, 1)
                    eng.wait_ge(cur_ready, turn)
                    eng.sem_inc(pool_turn, 1)
                    for j in range(GRP):
                        s, v = free(j)
                        eng.wait_ge(s, v)
                        eng.sem_inc(pool_turn, 1)
                        eng.indirect_dma_start(slot[j], None, rows, bass.IndirectOffsetOnAxis(ap=ix[:, j:j + 1], axis=0))\
                           .then_inc(row_in_slot[j], 16)

                def rest(rows, tt, turn, used, ahead):
                    def one(g, side):
                        gather(rows, tt, g, side, tt * (2 * NG) + g + (turn + 1),
                               lambda j: (used, tt * GK + g * GRP + (j + 1 - GRP + ahead)))
                    one(1, 1)
                    with eng.Fori(1, NG // 2) as pair:
                        one(pair * 2, 0)
                        one(pair * 2 + 1, 1)

                with eng.Fori(0, NT) as tt:
                    gather(u_rows, tt, 0, 0, tt * (2 * NG) + 1, lambda j: (v_used, tt * GK + (j + 1)))
                    rest(u_rows, tt, 0, u_used, 0)
                    gather(v_rows, tt, 0, 0, tt * (2 * NG) + (NG + 1), lambda j: (u_used, tt * GK + (GK - GRP + j + 1)))
                    rest(v_rows, tt, NG, v_used, GRP)

            @block.vector
            def _(eng):
                eng.sem_inc(acc_free, 1)
                with eng.Fori(0, NT) as tt:
                    with eng.Fori(0, NG) as g:
                        for j in range(GRP):
                            eng.wait_ge(row_in_slot[j], (tt * (2 * NG) + g + 1) * 16)
                            nc.vector.scalar_tensor_tensor(
                                out=slot[j], in0=slot[j], scalar=1.0, in1=tok2[:, bass.ds(tt * D, D)],
                                op0=ALU.mult, op1=ALU.mult, accum_out=dots[:, bass.ds(g * GRP + j, 1)]).then_inc(u_used, 1)
                    eng.wait_ge(gelu_done, tt + 1)
                    nc.vector.tensor_tensor(acts, acts, gates[:, bass.ds(tt * GK, GK)], ALU.mult).then_inc(acts_done, 1)
                    eng.wait_ge(v_used, (tt + 1) * GK + GRP)
                    hrow = h2[:, bass.ds(tt * D, D)]
                    nc.vector.tensor_tensor(hrow, hrow, bank[:, 0:2, :].rearrange("p b n -> p (b n)"), ALU.add)\
                      .then_inc(acc_free, 1)

            @block.scalar
            def _(eng):
                with eng.Fori(0, NT) as tt:
                    eng.wait_ge(u_used, (tt + 1) * GK)
                    nc.scalar.activation(acts, dots, ACT.Gelu_apprx_tanh).then_inc(gelu_done, 1)
                    with eng.Fori(0, NG) as g:
                        for j in range(GRP):
                            if j == 0:
                                eng.wait_ge(acts_done, tt + 1)
                            eng.wait_ge(v_used, tt * GK + g * GRP + (j + GRP - 1))
                            nc.scalar.activation(diag[:, j % 2, :], ident, ACT.Copy,
                                                 scale=acts[:, bass.ds(g * GRP + j, 1)]).then_inc(diag_done, 1)

            @block.tensor
            def _(eng):
                eng.sem_inc(v_used, GRP)
                with eng.Fori(0, NT) as tt:
                    eng.wait_ge(acc_free, tt + 1)
                    for n in range(2):
                        mm = nc.tensor.matmul(bank[:, n, :], const("zero"), tok[:, 0, n * NC:(n + 1) * NC],
                                              start=True, stop=False, skip_group_check=True)
                    mm.then_inc(acc_zero, 1)
                    with eng.Fori(0, NG) as g:
                        for j in range(GRP):
                            eng.wait_ge(diag_done, tt * GK + g * GRP + (j + 1))
                            eng.wait_ge(row_in_slot[j], (tt * (2 * NG) + g + (NG + 1)) * 16)
                            for n in range(2):
                                mm = nc.tensor.matmul(bank[:, n, :], diag[:, j % 2, :], slot[j][:, n * NC:(n + 1) * NC],
                                                      start=False, stop=False, skip_group_check=True)
                            mm.then_inc(v_used, 1)

        pT = region(0, 2 * S).rearrange("p (k s) -> p k s", k=2)
        gsb = region(2 * S, NT * D).rearrange("p (t d) -> p t d", t=NT)
        at["late"] += 16
        pT_at = at["late"]
        normalise(h, NT, 0, param("g_ple"), tok, aT,
                  sp_work=lambda sp: (sp.dma_start(pT[:, :, :], t["p_T"].rearrange("(k p) s -> p k s", p=P))
                                      .then_inc(late_in, 16), sp.wait_ge(late_in, pT_at)))
        jobs = [tok_job(C_PG + n, 0, NC, aT, tt, "act",
                        lambda b, tt=tt, n=n: nc.scalar.activation(gsb[:, tt, n * NC:(n + 1) * NC], bank[:, b, :], ACT.Sigmoid))
                for n in range(2) for tt in range(NT)]
        jobs += [tok_job(C_PE, n * NC, NC, pT, tt, "dve",
                         lambda b, tt=tt, n=n: nc.vector.tensor_tensor(gsb[:, tt, n * NC:(n + 1) * NC], bank[:, b, :],
                                                                      gsb[:, tt, n * NC:(n + 1) * NC], ALU.mult),
                         after=n * NT + tt)
                 for n in range(2) for tt in range(NT)]
        dense(jobs)
        dv = steps("dve", range(NT))
        with nc.Block() as block:
            @block.vector
            def _(eng):
                for tt in range(NT):
                    nc.vector.tensor_tensor(h[:, tt, :], h[:, tt, :], gsb[:, tt, :], ALU.add).then_inc(dve_done, 1)
        final_norm(h, 0, t["g_final"].rearrange("(o d) -> o d", o=1), h, tok)

        normalise(h, NT, 1, param("g_mix_2"), tok, aT)
        qk = region(0, 8 * S).rearrange("p (c s) -> p c s", c=8)
        v2 = region(4096, NT * S).rearrange("p (t n) -> p t n", t=NT)
        LU = S + PADU
        uT = region(6144, 4 * LU).rearrange("p (g s) -> p g s", g=4)
        jobs = []
        for c in range(4):
            jobs.append(t_job(C_IN2, c * P, aT, S, "act",
                              lambda b, c=c: nc.scalar.activation(qk[:, c, :], bank[:, b, :], ACT.Copy, scale=HD ** -0.5)))
        for c in range(4):
            jobs.append(t_job(C_IN2 + 1, c * P, aT, S, "dve",
                              lambda b, c=c: nc.vector.tensor_copy(qk[:, 4 + c, :], bank[:, b, :])))
        for tt in range(NT):
            jobs.append(tok_job(C_IN2 + 2, 0, NC, aT, tt, "act",
                                lambda b, tt=tt: nc.scalar.activation(v2[:, tt, :], bank[:, b, :], ACT.Copy)))
        for g in range(4):
            jobs.append(t_job(C_IN2 + 3, g * P, aT, S, "dve",
                              lambda b, g=g: nc.vector.tensor_copy(uT[:, g, PADU:LU], bank[:, b, :])))
        dense(jobs)

        OFF = [0, 512, 896, 1152]
        ZW = 1280
        ZB = [(0, 0), (1, 0), (2, 0), (1, 384)]
        zs = [region(8256 + i * ZW, ZW) for i in range(2)]
        sp_ = [region(8256 + (2 + i) * ZW, ZW) for i in range(2)]
        wt = [region(8256 + (4 + i) * ZW, ZW) for i in range(2)]
        pa = aT[:, 0:5, :].rearrange("p k s -> p (k s)")
        pl = [pa[:, i * LU:(i + 1) * LU] for i in range(2)]
        wpool = grow[:, 0:4 * P].rearrange("p (g e) -> p g e", g=4)
        at["row"] += 16
        row_at = at["row"]

        def zpart(b0, i):
            b, c = ZB[i]
            return bank[:, b0 + b, c:c + S - i * P]

        def seg(x, i):
            return x[:, OFF[i]:OFF[i] + S - i * P]

        nsum = [1, 2, 3, 4]
        pool_labels = []
        for g in range(4):
            pool_labels += [("win", g, i) for i in range(nsum[g])]
            pool_labels += [("mean", g), ("edge", g), ("less", g)]
        dv = steps("dve", [x for hd in range(SBH) for x in
                           [("z", hd, i) for i in range(4)] + [("sp", hd)] + [("mask", hd, i) for i in range(4)]
                           + [("t1", hd)] + [("t2", hd, i) for i in range(4)] + [("wmask", hd, i) for i in range(4)]
                           + [("o", hd)]]
                   + pool_labels + [("po", g) for g in range(4)]
                   + ["srec", "prec"] + [("sn", k) for k in range(8)])
        ac = steps("act", [x for hd in range(SBH) for x in
                           [("abs", hd), ("e", hd), ("l", hd), ("w", hd)]]
                   + [("sq", k) for k in range(8)] + ["ssd", "psd"])
        pe = steps("pe", [x for hd in range(SBH + 1) for x in
                          ([("z", hd)] if hd < SBH else []) + ([("a", hd - 1), ("o", hd - 1)] if hd else [])]
                   + [("pool", g) for g in range(4)] + ["ssum", "psum"])
        po = steps("pool", ["upad"])
        ZBANK, ABANK, OBANK = 0, 3, 6
        pooled = [sp_[0][:, 0:S], sp_[1][:, 0:S], zs[0][:, 0:S], zs[1][:, 0:S]]
        with nc.Block() as block:
            @block.sync
            def _(sp):
                sp.dma_start(wpool, t["w_pool_2"][0].rearrange("g c e -> c g e")).then_inc(row_in, 16)
                for i in range(LEAST_LIVE, NBP, NT):
                    sp.dma_start(y_dram[i * P:(i + NT) * P, :].rearrange("(t p) d -> p t d", p=P), h[:, :, :])\
                      .then_inc(rows_filled, 16)
                sp.wait_ge(rows_filled, 16 * (NBP - LEAST_LIVE) // NT)

            @block.gpsimd
            def _(eng):
                eng.memset(uT[:, :, 0:PADU], 0.0).then_inc(pool_done, 1)

            @block.tensor
            def _(eng):
                def z_of(hd):
                    if hd:
                        eng.wait_ge(dve_done, dv["z", hd - 1, 3])
                    r = hd % 2 * HD
                    for i in range(4):
                        mm = nc.tensor.matmul(zpart(ZBANK, i), qk[r:r + HD, 4 + hd // 2, i * P:(i + 1) * P],
                                              qk[r:r + HD, hd // 2, i * P:S], start=True, stop=True)
                    mm.then_inc(pe_done, 1)

                z_of(0)
                for hd in range(SBH):
                    if hd + 1 < SBH:
                        z_of(hd + 1)
                    eng.wait_ge(dve_done, dv["mask", hd, 3])
                    if hd:
                        eng.wait_ge(dve_done, dv["t2", hd - 1, 3])
                    for i in range(4):
                        n = 4 - i
                        for j in range(i, 4):
                            b, c = ZB[i]
                            dst = bank[:, ABANK + b, c + (j - i) * P:c + S - i * P]
                            mm = nc.tensor.matmul(dst, const("gt") if j == i else const("ones"), seg(sp_[hd % 2], j),
                                                  start=j == i, stop=j == 3, skip_group_check=True)
                    mm.then_inc(pe_done, 1)
                    eng.wait_ge(dve_done, dv["wmask", hd, 3])
                    if hd:
                        eng.wait_ge(dve_done, dv["o", hd - 1])
                    r = hd % 2 * HD
                    for i in range(4):
                        mm = nc.tensor.matmul(bank[r:r + HD, OBANK, i * P:S], v2[:, i, hd * HD:(hd + 1) * HD],
                                              seg(wt[hd % 2], i), start=i == 0, stop=i == 3, skip_group_check=True)
                    mm.then_inc(pe_done, 1)
                eng.wait_ge(row_in, row_at)
                for g in range(4):
                    eng.wait_ge(dve_done, dv["less", g])
                    nc.tensor.matmul(bank[:, g, :], wpool[:, g, :], pooled[g], start=True, stop=True).then_inc(pe_done, 1)
                for n, name in enumerate(("ssum", "psum")):
                    for k in range(4):
                        eng.wait_ge(act_done, ac["sq", 4 * n + k])
                        mm = nc.tensor.matmul(bank[:, 4 + n, :], const("ones"), qk[:, 4 * n + k, :],
                                              start=k == 0, stop=k == 3)
                    mm.then_inc(pe_done, 1)

            @block.scalar
            def _(eng):
                for hd in range(SBH):
                    s = hd % 2
                    eng.wait_ge(dve_done, dv["z", hd, 3])
                    if hd >= 2:
                        eng.wait_ge(pe_done, pe["a", hd - 2])
                    nc.scalar.activation(sp_[s], zs[s], ACT.Abs).then_inc(act_done, 1)
                    eng.wait_ge(act_done, ac["abs", hd])
                    nc.scalar.activation(sp_[s], sp_[s], ACT.Exp, scale=-1.0).then_inc(act_done, 1)
                    eng.wait_ge(act_done, ac["e", hd])
                    nc.scalar.activation(sp_[s], sp_[s], ACT.Ln, bias=const("ones", 0, 1)).then_inc(act_done, 1)
                    eng.wait_ge(dve_done, dv["t2", hd, 3])
                    nc.scalar.activation(wt[s], wt[s], ACT.Exp).then_inc(act_done, 1)
                for k in range(8):
                    if k < 4:
                        eng.wait_ge(dve_done, dv["o", 2 * k + 1])
                    else:
                        eng.wait_ge(dve_done, dv["po", k - 4])
                    if k == 0:
                        eng.wait_ge(pe_done, pe["o", SBH - 1])
                    nc.scalar.activation(qk[:, k, :], mixT[:, k, :], ACT.Square).then_inc(act_done, 1)
                for n, name in enumerate(("ssum", "psum")):
                    eng.wait_ge(pe_done, pe[name])
                    nc.scalar.activation(v2[:, n, :], bank[:, 4 + n, :], ACT.Sqrt, scale=1.0 / S,
                                         bias=const("eps", 1, 2)).then_inc(act_done, 1)

            @block.vector
            def _(eng):
                for hd in range(SBH):
                    s = hd % 2
                    eng.wait_ge(pe_done, pe["z", hd])
                    for i in range(4):
                        if hd >= 2:
                            eng.wait_ge(dve_done, dv["t1", hd - 2])
                        nc.vector.tensor_copy(seg(zs[s], i), zpart(ZBANK, i)).then_inc(dve_done, 1)
                    eng.wait_ge(act_done, ac["l", hd])
                    eng.wait_ge(dve_done, dv["z", hd, 3])
                    nc.vector.scalar_tensor_tensor(out=sp_[s], in0=zs[s], scalar=0.0, in1=sp_[s],
                                                   op0=ALU.max, op1=ALU.add).then_inc(dve_done, 1)
                    eng.wait_ge(dve_done, dv["sp", hd])
                    if hd >= 2:
                        eng.wait_ge(pe_done, pe["o", hd - 2])
                    for i in range(4):
                        d = sp_[s][:, OFF[i]:OFF[i] + P]
                        nc.vector.tensor_tensor(d, d, const("lt"), ALU.mult).then_inc(dve_done, 1)
                    eng.wait_ge(dve_done, dv["mask", hd, 3])
                    nc.vector.tensor_tensor(wt[s], zs[s], sp_[s], ALU.subtract).then_inc(dve_done, 1)
                    eng.wait_ge(dve_done, dv["t1", hd])
                    eng.wait_ge(pe_done, pe["a", hd])
                    for i in range(4):
                        nc.vector.tensor_tensor(seg(wt[s], i), seg(wt[s], i), zpart(ABANK, i), ALU.subtract).then_inc(dve_done, 1)
                    eng.wait_ge(act_done, ac["w", hd])
                    for i in range(4):
                        d = wt[s][:, OFF[i]:OFF[i] + P]
                        nc.vector.tensor_tensor(d, d, const("lt"), ALU.mult).then_inc(dve_done, 1)
                    eng.wait_ge(pe_done, pe["o", hd])
                    r = hd % 2 * HD
                    nc.vector.tensor_copy(mixT[r:r + HD, hd // 2, :], bank[r:r + HD, OBANK, :]).then_inc(dve_done, 1)
                eng.wait_ge(pool_done, po["upad"])
                prev = dv["o", SBH - 1]
                for g, win in enumerate(WINS):
                    src = uT[:, g, :]
                    step_ = 1
                    for i in range(nsum[g]):
                        dst = pl[i % 2]
                        lo = 2 * step_ - 1
                        eng.wait_ge(dve_done, prev)
                        nc.vector.tensor_tensor(dst[:, lo:LU], src[:, lo:LU], src[:, lo - step_:LU - step_], ALU.add)\
                          .then_inc(dve_done, 1)
                        prev = dv["win", g, i]
                        src = dst
                        step_ *= 2
                    dst = pooled[g]
                    eng.wait_ge(dve_done, prev)
                    nc.vector.tensor_scalar(dst[:, PADU:S], src[:, 2 * PADU:LU], 1.0 / win, None, ALU.mult).then_inc(dve_done, 1)
                    nc.vector.tensor_tensor(dst[:, 0:PADU], src[:, PADU:2 * PADU],
                                            const("rcount", g * PADU, (g + 1) * PADU), ALU.mult).then_inc(dve_done, 1)
                    eng.wait_ge(dve_done, dv["edge", g])
                    nc.vector.tensor_tensor(dst, dst, uT[:, g, PADU:LU], ALU.subtract).then_inc(dve_done, 1)
                    prev = dv["less", g]
                for g in range(4):
                    eng.wait_ge(pe_done, pe["pool", g])
                    nc.vector.tensor_scalar(mixT[:, 4 + g, :], bank[:, g, :], param("pool_scale", g, g + 1), None,
                                            ALU.mult).then_inc(dve_done, 1)
                for n, name in enumerate(("ssd", "psd")):
                    eng.wait_ge(act_done, ac[name])
                    nc.vector.reciprocal(v2[:, n, :], v2[:, n, :]).then_inc(dve_done, 1)
                for k in range(8):
                    eng.wait_ge(dve_done, dv["srec" if k < 4 else "prec"])
                    g = param("g_sb", k, k + 1) if k < 4 else param("g_pool", k - 4, k - 3)
                    nc.vector.scalar_tensor_tensor(out=mixT[:, k, :], in0=mixT[:, k, :], scalar=g, in1=v2[:, k // 4, :],
                                                   op0=ALU.mult, op1=ALU.mult).then_inc(dve_done, 1)

        project_into_h(C_OUT2, mixT)

        mem = region(0, TM * D).rearrange("p (t d) -> p t d", t=TM)
        memT = region(2048, KD * NMEM).rearrange("p (k m) -> p k m", k=KD)
        kmT = region(4096, KD * NMEM).rearrange("p (k m) -> p k m", k=KD)
        vm = region(6144, TM * D).rearrange("p (t d) -> p t d", t=TM)
        qm = region(8192, KD * S).rearrange("p (k s) -> p k s", k=KD)
        prob = region(12288, NT * MH * NMEM).rearrange("p (t h m) -> p t h m", t=NT, h=MH)
        at["late"] += 16
        mem_at = at["late"]
        with nc.Block() as block:
            @block.sync
            def _(sp):
                sp.dma_start(mem[:, :, :], t["mem_2"][0].rearrange("(t p) d -> p t d", p=P)).then_inc(late_in, 16)
                sp.wait_ge(late_in, mem_at)
        normalise(mem, TM, 1, param("g_mem_kv"), tok, memT)
        jobs = []
        for c in range(8):
            jobs.append(t_job(C_KV + c // 4, c % 4 * P, memT, NMEM, "act",
                              lambda b, c=c: nc.scalar.activation(kmT[:, c, :], bank[:, b, 0:NMEM], ACT.Copy)))
        for n in range(2):
            for mt in range(TM):
                jobs.append(tok_job(C_KV + 2 + n, 0, NC, memT, mt, "dve",
                                    lambda b, mt=mt, n=n: nc.vector.tensor_copy(vm[:, mt, n * NC:(n + 1) * NC], bank[:, b, :])))
        dense(jobs)
        normalise(h, NT, 1, param("g_mem_q"), tok, aT)
        dense([t_job(C_MQ + c // 4, c % 4 * P, aT, S, "act" if c % 2 else "dve",
                     (lambda b, c=c: nc.scalar.activation(qm[:, c, :], bank[:, b, :], ACT.Copy)) if c % 2 else
                     (lambda b, c=c: nc.vector.tensor_copy(qm[:, c, :], bank[:, b, :]))) for c in range(8)])

        dh = D // MH
        SCALE = dh ** -0.5
        units = [(tt, half) for tt in range(NT) for half in range(2)]
        pTt = aT[:, :, :].rearrange("p (h m) s -> p h m s", h=MH)
        mx, nmx, rs, ri = stat[:, 0:16], stat[:, 16:32], stat[:, 32:48], stat[:, 48:64]
        pe = steps("pe", [("s", u) for u in range(8)] + [("t", hd, mt) for hd in range(MH) for mt in range(TM)]
                   + [("o", c) for c in range(8)])
        dv = steps("dve", [x for u in range(8) for x in (("max", u), ("neg", u))] + ["rec"]
                   + [("p", u) for u in range(8)] + [("t", k) for k in range(0, 8, 2)] + [("o", c) for c in range(0, 8, 2)])
        ac = steps("act", [("e", u, j) for u in range(8) for j in range(2)]
                   + [("t", k) for k in range(1, 8, 2)] + [("o", c) for c in range(1, 8, 2)])
        with nc.Block() as block:
            @block.tensor
            def _(eng):
                for u, (tt, half) in enumerate(units):
                    for j in range(2):
                        hd = 2 * half + j
                        for k in range(2):
                            mm = nc.tensor.matmul(bank[:, u, j * NMEM:(j + 1) * NMEM],
                                                  qm[:, 2 * hd + k, tt * P:(tt + 1) * P], kmT[:, 2 * hd + k, :],
                                                  start=k == 0, stop=k == 1)
                    mm.then_inc(pe_done, 1)
                for hd in range(MH):
                    for mt in range(TM):
                        b = hd * TM + mt
                        for tt in range(NT):
                            eng.wait_ge(dve_done, dv["p", 7])
                            mm = nc.tensor.transpose(bank[:, b, tt * P:(tt + 1) * P], prob[:, tt, hd, mt * P:(mt + 1) * P], ident)
                        mm.then_inc(pe_done, 1)
                for c in range(8):
                    hd = c // 2
                    for mt in range(TM):
                        k = hd * TM + mt
                        eng.wait_ge(*((dve_done, dv["t", k]) if k % 2 == 0 else (act_done, ac["t", k])))
                    if c % 2 == 0:
                        eng.wait_ge(dve_done, dv["t", c])
                    else:
                        eng.wait_ge(act_done, ac["t", c])
                    for mt in range(TM):
                        mm = nc.tensor.matmul(bank[:, c, :], vm[:, mt, c * P:(c + 1) * P], pTt[:, hd, mt, :],
                                              start=mt == 0, stop=mt == TM - 1)
                    mm.then_inc(pe_done, 1)

            @block.vector
            def _(eng):
                for u, (tt, half) in enumerate(units):
                    eng.wait_ge(pe_done, pe["s", u])
                    nc.vector.tensor_reduce(mx[:, 2 * u:2 * u + 2], bank[:, u, :].rearrange("p (j m) -> p j m", j=2),
                                            AX, ALU.max).then_inc(dve_done, 1)
                    eng.wait_ge(dve_done, dv["max", u])
                    nc.vector.tensor_scalar(nmx[:, 2 * u:2 * u + 2], mx[:, 2 * u:2 * u + 2], -SCALE, None, ALU.mult)\
                      .then_inc(dve_done, 1)
                eng.wait_ge(act_done, ac["e", 7, 1])
                nc.vector.reciprocal(ri, rs).then_inc(dve_done, 1)
                eng.wait_ge(dve_done, dv["rec"])
                for u, (tt, half) in enumerate(units):
                    pr = prob[:, tt, 2 * half:2 * half + 2, :]
                    nc.vector.tensor_tensor(pr, pr, over(ri[:, 2 * u:2 * u + 2], NMEM), ALU.mult).then_inc(dve_done, 1)
                for k in range(0, 8, 2):
                    eng.wait_ge(pe_done, pe["t", k // TM, k % TM])
                    nc.vector.tensor_copy(pTt[:, k // TM, k % TM, :], bank[:, k, :]).then_inc(dve_done, 1)
                for c in range(0, 8, 2):
                    eng.wait_ge(pe_done, pe["o", c])
                    nc.vector.tensor_copy(mixT[:, c, :], bank[:, c, :]).then_inc(dve_done, 1)

            @block.scalar
            def _(eng):
                for u, (tt, half) in enumerate(units):
                    eng.wait_ge(dve_done, dv["neg", u])
                    for j in range(2):
                        nc.scalar.activation(prob[:, tt, 2 * half + j, :], bank[:, u, j * NMEM:(j + 1) * NMEM], ACT.Exp,
                                             scale=SCALE, bias=nmx[:, 2 * u + j:2 * u + j + 1],
                                             accum_out=rs[:, 2 * u + j:2 * u + j + 1]).then_inc(act_done, 1)
                for k in range(1, 8, 2):
                    eng.wait_ge(pe_done, pe["t", k // TM, k % TM])
                    nc.scalar.activation(pTt[:, k // TM, k % TM, :], bank[:, k, :], ACT.Copy).then_inc(act_done, 1)
                for c in range(1, 8, 2):
                    eng.wait_ge(pe_done, pe["o", c])
                    nc.scalar.activation(mixT[:, c, :], bank[:, c, :], ACT.Copy).then_inc(act_done, 1)

        project_into_h(C_MO, mixT)

        o = 0
        wr = region(o, KD * NE).rearrange("p (k e) -> p k e", k=KD)
        o += KD * NE
        br = region(o, NE)
        o += NE
        bexp = X[0:3 * NE, o:o + 3 * D]
        o += 3 * D
        at["late"] += 48 + 32
        r_at = at["late"]

        def router_loads(sp):
            sp.dma_start(wr[:, :, :], t["w_router_2"][0].rearrange("(k p) e -> p k e", p=P)).then_inc(late_in, 16)
            sp.dma_start(br[:, :], t["b_router_2"][0:1, :].to_broadcast([P, NE])).then_inc(late_in, 16)
            for i in range(3):
                sp.dma_start(bexp[i * NE:(i + 1) * NE, :], t["b_expert"][:, :]).then_inc(late_in, 16)
        normalise(h, NT, 1, None, tok, aT, row=grow, row_ap=t["g_ffn_2"][0:1, :], sp_work=router_loads)

        lg = region(o, NT * NE).rearrange("p (t e) -> p t e", t=NT)
        o += NT * NE
        tv = region(o, NT * 8).rearrange("p (t k) -> p t k", t=NT)
        o += NT * 8
        ti = region(o, NT * 8).bitcast(U32).rearrange("p (t k) -> p t k", t=NT)
        o += NT * 8
        tf = region(o, NT * 8).rearrange("p (t k) -> p t k", t=NT)
        o += NT * 8
        oh = region(o, NT * EK * NE).rearrange("p (t k e) -> p t k e", t=NT, k=EK)
        o += NT * EK * NE
        oh2 = region(o, NT * EK * NE).rearrange("p (t k e) -> p t k e", t=NT, k=EK)
        o += NT * EK * NE
        M = region(o, NT * NE).rearrange("p (t e) -> p t e", t=NT)
        o += NT * NE
        R = region(o, NT * NE)
        o += NT * NE
        q4 = region(o, NT * NE)
        o += NT * NE
        tq = region(o, NT * NE)
        o += NT * NE
        am = region(o, NT * NE)
        o += NT * NE
        ay = region(o, NT * NE)
        o += NT * NE
        nb = region(o, NE)
        o += NE
        nb2 = region(o, NE)
        o += NE
        bend = region(o, NE)
        o += NE
        bst = region(o, NE)
        o += NE
        cmpb = region(o, NBP * NE).rearrange("p (b e) -> p b e", b=NBP)
        o += NBP * NE
        bh = region(o, 3 * D // 2).bitcast(BF16)[0:3 * NE, :]
        o += 3 * D // 2
        assert o <= 4 * KD * NC
        gk = sb("gk", [P, NT * EK])
        smap = sb("smap", [P, NT * EK], I32)
        srow = sb("srow", [P, NT * EK], I32)
        blkf = sb("blkf", [P, NBP])
        blki = sb("blki", [P, NBP], I32)
        live = sb("live", [P, 1], I32)
        tki = sb("tki", [P, NT], I32)
        slots = sb("slots", [P, NBP], I32)
        b3 = sb("b3", [3 * NE, 3 * D], BF16)
        zero_i = slots

        def bc(x, shape):
            return x.to_broadcast(shape)

        dvl = ["lg"] + [("mx", i) for i in range(NT)] + [("ix", i) for i in range(NT)] + ["tf", "tsub"]
        dvl += ["esum", "erec", "gk"] + [("oh", i) for i in range(NT)] + ["M"]
        dvl += ["nb0", "nb1", "nb2", "nb3", "bend", "bst", "live", "cmp", "blkf", "blkm", "blki"]
        dvl += ["R", "q1", "q2", "q2a", "q3", "q3a", "p", "bq", "am", "ay"]
        dvl += ["selm", "fmap", "smap", "sely", "frow", "srow", "tki", "zero"]
        dvl += ["hi", "r1", "mid", "r2", "lo", "midc"]
        dv = steps("dve", dvl)
        ac = steps("act", ["exp"])
        pe = steps("pe", ["lg", "rank", "cnt"])
        ws = [wring[i][:, :] for i in range(4)] + [region(0, KD * NC), region(KD * NC, KD * NC)]
        w1s = [w.rearrange("p (k n) -> p k n", k=KD) for w in ws[0:4]]
        w2s = [w.rearrange("p (k n) -> p k n", k=4) for w in ws[4:6]]
        o = 2 * KD * NC
        xg = region(o, D)
        gsb_ = region(o + D, D)
        usb = region(o + 2 * D, D)
        act_ = region(o + 3 * D, D)
        ysb = region(o + 4 * D, D)
        ohb = X[0:3 * NE, o + 5 * D:o + 5 * D + P // 2].bitcast(BF16)
        curs = region(o + 5 * D + P, 1).bitcast(I32)
        xT = aT[:, 0:2, :].rearrange("p k s -> p (k s)").rearrange("p (k m) -> p k m", k=KD)
        hT = aT[:, 2:4, :].rearrange("p k s -> p (k s)").rearrange("p (k m) -> p k m", k=KD)
        w1_in = [sem(f"w1_in{i}") for i in range(4)]
        w2_in = [sem(f"w2_in{i}") for i in range(2)]
        rows_in = sem("rows_in")
        curs_ready = sem("curs_ready")
        x_t = sem("x_t")
        x_e = sem("x_e")
        oh_ready = sem("oh_ready")
        gu_done = sem("gu_done")
        gate_ok = sem("gate_ok")
        up_ok = sem("up_ok")
        sig_ok = sem("sig_ok")
        mul_ok = sem("mul_ok")
        act_ok = sem("act_ok")
        h_t = sem("h_t")
        h_e = sem("h_e")
        y_done = sem("y_done")
        y_out = sem("y_out")
        y_st = sem("y_st")
        all_stored = sem("all_stored")
        we1, we2 = t["w_expert_in_2"][0], t["w_expert_out_2"][0]
        GU = [0, 2 * 512, 512, 3 * 512]
        HB, GB, YB = 0, 2, 6


        def load_w1(sp, e, c):
            sp.dma_start(w1s[c], we1[bass.ds(e, 1), :, GU[c]:GU[c] + NC]
                         .rearrange("o (k p) n -> p (o k) n", p=P)).then_inc(w1_in[c], 16)

        def load_w2(sp, e, c):
            sp.dma_start(w2s[c], we2[bass.ds(e, 1), c * NC:(c + 1) * NC, :]
                         .rearrange("o (k p) n -> p (o k) n", p=P)).then_inc(w2_in[c], 16)

        map_zero, map_set, rows_out, map_in = sem("map_zero"), sem("map_set"), sem("rows_out"), sem("map_in")
        with nc.Block() as block:
            @block.sync
            def _(sp):
                sp.dma_start(xn_dram.rearrange("(t p) d -> p t d", p=P), tok[:, :, :]).then_inc(rows_out, 16)
                sp.wait_ge(dve_done, dv["zero"])
                sp.dma_start(tokmap_dram.rearrange("(p b) o -> p (b o)", p=P), zero_i[:, :]).then_inc(map_zero, 16)
                sp.wait_ge(dve_done, dv["blki"])
                e = sp.value_load(blki[0:1, 0:1], min_val=0, max_val=NE - 1)
                for c in range(4):
                    load_w1(sp, e, c)
                sp.wait_ge(map_set, 16 * NT * EK)
                sp.dma_start(slots[:, :], tokmap_dram.rearrange("(p b) o -> p (b o)", p=P)).then_inc(map_in, 16)
                sp.wait_ge(map_in, 16)
                sp.wait_ge(rows_out, 16)

            @block.tensor
            def _(eng):
                eng.wait_ge(late_in, r_at)
                for tt in range(NT):
                    for k in range(KD):
                        mm = nc.tensor.matmul(bank[:, 0, tt * NE:(tt + 1) * NE], aT[:, k, tt * P:(tt + 1) * P], wr[:, k, :],
                                              start=k == 0, stop=k == KD - 1)
                mm.then_inc(pe_done, 1)
                eng.wait_ge(dve_done, dv["M"])
                for tt in range(NT):
                    for j in range(tt + 1):
                        mm = nc.tensor.matmul(bank[:, 1, tt * NE:(tt + 1) * NE], const("lt") if j == tt else const("ones"),
                                              M[:, j, :], start=j == 0, stop=j == tt)
                mm.then_inc(pe_done, 1)
                for j in range(NT):
                    mm = nc.tensor.matmul(bank[:, 2, 0:NE], const("ones"), M[:, j, :], start=j == 0, stop=j == NT - 1)
                mm.then_inc(pe_done, 1)

            @block.scalar
            def _(eng):
                eng.wait_ge(dve_done, dv["tsub"])
                nc.scalar.activation(tv[:, :, EK:2 * EK], tv[:, :, EK:2 * EK], ACT.Exp).then_inc(act_done, 1)

            @block.vector
            def _(eng):
                eng.wait_ge(late_in, r_at)
                eng.wait_ge(pe_done, pe["lg"])
                nc.vector.tensor_tensor(lg, bank[:, 0, 0:NT * NE].rearrange("p (t e) -> p t e", t=NT),
                                        over_t(br[:, :]), ALU.add).then_inc(dve_done, 1)
                eng.wait_ge(dve_done, dv["lg"])
                for i in range(NT):
                    nc.vector.max(tv[:, i, :], lg[:, i, :]).then_inc(dve_done, 1)
                for i in range(NT):
                    eng.wait_ge(dve_done, dv["mx", i])
                    nc.vector.max_index(ti[:, i, :], tv[:, i, :], lg[:, i, :]).then_inc(dve_done, 1)
                eng.wait_ge(dve_done, dv["ix", NT - 1])
                nc.vector.tensor_copy(tf, ti).then_inc(dve_done, 1)
                nc.vector.tensor_tensor(tv[:, :, EK:2 * EK], tv[:, :, 0:EK], bc(tv[:, :, 0:1], [P, NT, EK]), ALU.subtract)\
                  .then_inc(dve_done, 1)
                eng.wait_ge(act_done, ac["exp"])
                nc.vector.tensor_reduce(nb[:, 0:NT], tv[:, :, EK:2 * EK], AX, ALU.add).then_inc(dve_done, 1)
                eng.wait_ge(dve_done, dv["esum"])
                nc.vector.reciprocal(nb[:, 4:4 + NT], nb[:, 0:NT]).then_inc(dve_done, 1)
                eng.wait_ge(dve_done, dv["erec"])
                nc.vector.tensor_tensor(gk[:, :].rearrange("p (t k) -> p t k", t=NT), tv[:, :, EK:2 * EK],
                                        over(nb[:, 4:4 + NT], EK), ALU.mult).then_inc(dve_done, 1)
                for i in range(NT):
                    nc.vector.tensor_tensor(oh[:, i, :, :], over(tf[:, i, 0:EK], NE),
                                            over_t(const("iota", 0, NE)), ALU.is_equal).then_inc(dve_done, 1)
                eng.wait_ge(dve_done, dv["oh", NT - 1])
                nc.vector.tensor_reduce(M, oh.rearrange("p t k e -> p t e k"), AX, ALU.add).then_inc(dve_done, 1)
                eng.wait_ge(pe_done, pe["cnt"])
                cnt = bank[:, 2, 0:NE]
                nc.vector.tensor_scalar(nb, cnt, 0.0, None, ALU.is_gt).then_inc(dve_done, 1)
                prev, a, b = "nb0", nb, nb2
                for j in range(1, 4):
                    eng.wait_ge(dve_done, dv[prev])
                    nc.vector.scalar_tensor_tensor(out=b, in0=cnt, scalar=float(P * j), in1=a, op0=ALU.is_gt, op1=ALU.add)\
                      .then_inc(dve_done, 1)
                    prev, a, b = f"nb{j}", b, a
                eng.wait_ge(dve_done, dv["nb3"])
                nc.vector.tensor_tensor_scan(out=bend, data0=const("ones", 0, NE), data1=a, initial=0.0,
                                             op0=ALU.mult, op1=ALU.add).then_inc(dve_done, 1)
                eng.wait_ge(dve_done, dv["bend"])
                nc.vector.tensor_tensor(bst, bend, a, ALU.subtract).then_inc(dve_done, 1)
                nc.vector.tensor_copy(live[:, :], bend[:, NE - 1:NE]).then_inc(dve_done, 1)
                nc.vector.tensor_tensor(cmpb, bend.rearrange("p (o e) -> p o e", o=1).to_broadcast([P, NBP, NE]),
                                        over(const("iota"), NE), ALU.is_le).then_inc(dve_done, 1)
                eng.wait_ge(dve_done, dv["cmp"])
                nc.vector.tensor_reduce(blkf[:, :], cmpb, AX, ALU.add).then_inc(dve_done, 1)
                eng.wait_ge(dve_done, dv["blkf"])
                nc.vector.tensor_scalar(blkf[:, :], blkf[:, :], float(NE - 1), None, ALU.min).then_inc(dve_done, 1)
                eng.wait_ge(dve_done, dv["blkm"])
                nc.vector.tensor_copy(blki[:, :], blkf[:, :]).then_inc(dve_done, 1)
                nc.vector.tensor_copy(R, bank[:, 1, 0:NT * NE]).then_inc(dve_done, 1)
                eng.wait_ge(dve_done, dv["R"])
                nc.vector.tensor_scalar(q4, R, float(P), None, ALU.is_ge).then_inc(dve_done, 1)
                eng.wait_ge(dve_done, dv["q1"])
                nc.vector.tensor_scalar(tq, R, float(2 * P), None, ALU.is_ge).then_inc(dve_done, 1)
                eng.wait_ge(dve_done, dv["q2"])
                nc.vector.tensor_tensor(q4, q4, tq, ALU.add).then_inc(dve_done, 1)
                eng.wait_ge(dve_done, dv["q2a"])
                nc.vector.tensor_scalar(tq, R, float(3 * P), None, ALU.is_ge).then_inc(dve_done, 1)
                eng.wait_ge(dve_done, dv["q3"])
                nc.vector.tensor_tensor(q4, q4, tq, ALU.add).then_inc(dve_done, 1)
                eng.wait_ge(dve_done, dv["q3a"])
                nc.vector.scalar_tensor_tensor(out=R, in0=q4, scalar=float(-P), in1=R, op0=ALU.mult, op1=ALU.add)\
                  .then_inc(dve_done, 1)
                nc.vector.tensor_tensor(q4.rearrange("p (t e) -> p t e", t=NT), q4.rearrange("p (t e) -> p t e", t=NT),
                                        over_t(bst), ALU.add).then_inc(dve_done, 1)
                eng.wait_ge(dve_done, dv["bq"])
                nc.vector.scalar_tensor_tensor(out=am, in0=R, scalar=float(NBP), in1=q4, op0=ALU.mult, op1=ALU.add)\
                  .then_inc(dve_done, 1)
                nc.vector.scalar_tensor_tensor(out=ay, in0=q4, scalar=float(P), in1=R, op0=ALU.mult, op1=ALU.add)\
                  .then_inc(dve_done, 1)
                eng.wait_ge(dve_done, dv["ay"])
                for src, dst, n, (l1, l2) in ((am, smap, 0, ("selm", "fmap")), (ay, srow, 1, ("sely", "frow"))):
                    s3 = src.rearrange("p (t o e) -> p t o e", t=NT, o=1).to_broadcast([P, NT, EK, NE])
                    if n:
                        eng.wait_ge(dve_done, dv["fmap"])
                    nc.vector.tensor_tensor(oh2, oh, s3, ALU.mult).then_inc(dve_done, 1)
                    eng.wait_ge(dve_done, dv[l1])
                    f = stat[:, n * 16:(n + 1) * 16]
                    nc.vector.tensor_reduce(f, oh2.rearrange("p t k e -> p (t k) e"), AX, ALU.add).then_inc(dve_done, 1)
                    eng.wait_ge(dve_done, dv[l2])
                    nc.vector.tensor_copy(dst[:, :], f).then_inc(dve_done, 1)
                nc.vector.tensor_copy(tki[:, :], const("tok")).then_inc(dve_done, 1)
                nc.vector.memset(zero_i[:, :], 0).then_inc(dve_done, 1)
                B = bexp
                nc.vector.tensor_copy(b3[:, :], B).then_inc(dve_done, 1)
                eng.wait_ge(dve_done, dv["hi"])
                nc.vector.tensor_tensor(B, B, b3[:, :], ALU.subtract).then_inc(dve_done, 1)
                eng.wait_ge(dve_done, dv["r1"])
                nc.vector.tensor_copy(bh, B).then_inc(dve_done, 1)
                eng.wait_ge(dve_done, dv["mid"])
                nc.vector.tensor_tensor(B, B, bh, ALU.subtract).then_inc(dve_done, 1)
                eng.wait_ge(dve_done, dv["r2"])
                nc.vector.tensor_copy(b3[2 * NE:3 * NE, :], B[2 * NE:3 * NE, :]).then_inc(dve_done, 1)
                nc.vector.tensor_copy(b3[NE:2 * NE, :], bh[NE:2 * NE, :]).then_inc(dve_done, 1)

            @block.gpsimd
            def _(eng):
                eng.wait_ge(map_zero, 16)
                eng.wait_ge(dve_done, dv["zero"])
                for j in range(NT * EK):
                    eng.indirect_dma_start(tokmap_dram, bass.IndirectOffsetOnAxis(ap=smap[:, j:j + 1], axis=0),
                                           tki[:, j // EK:j // EK + 1], None).then_inc(map_set, 16)
                eng.wait_ge(map_set, 16 * NT * EK)

        def each_block(eng, body, ahead=0):
            n = eng.value_load(live[0:1, 0:1], min_val=1, max_val=NBLK)
            with eng.Fori(0, NBLK - ahead) as b:
                with eng.If(b + ahead < n):
                    body(b)
                with eng.Else():
                    eng.nop()
            return n

        with nc.Block() as block:
            @block.sync
            def _(eng):
                e = eng.value_load(blki[0:1, 0:1], min_val=0, max_val=NE - 1)
                for c in range(2):
                    load_w2(eng, e, c)

                def body(b):
                    e = eng.value_load(blki[0:1, bass.ds(b + 1, 1)], min_val=0, max_val=NE - 1)
                    for c in range(4):
                        eng.wait_ge(gu_done, b * 4 + (c + 1))
                        load_w1(eng, e, c)
                    for c in range(2):
                        eng.wait_ge(y_done, b * 2 + (c + 1))
                        load_w2(eng, e, c)
                each_block(eng, body, ahead=1)

            @block.gpsimd
            def _(eng):
                def gather(col, turn):
                    eng.tensor_copy(curs, slots[:, col]).then_inc(curs_ready, 1)
                    eng.wait_ge(curs_ready, turn)
                    eng.sem_inc(pool_turn, 1)
                    eng.indirect_dma_start(xg, None, xn_dram, bass.IndirectOffsetOnAxis(ap=curs, axis=0))\
                       .then_inc(rows_in, 16)
                gather(slice(0, 1), 1)

                def body(b):
                    eng.wait_ge(x_t, b * 2 + 2)
                    eng.sem_inc(pool_turn, 1)
                    gather(bass.ds(b + 1, 1), b + 2)
                each_block(eng, body)

            @block.tensor
            def _(eng):
                def transpose_rows():
                    for half in range(2):
                        for k in range(4):
                            kk = half * 4 + k
                            mm = nc.tensor.transpose(bank[:, GB + half, k * P:(k + 1) * P], xg[:, kk * P:(kk + 1) * P], ident)
                        mm.then_inc(x_t, 1)

                def transpose_act(half):
                    for k in range(4):
                        kk = half * 4 + k
                        mm = nc.tensor.transpose(bank[:, HB + half, k * P:(k + 1) * P], act_[:, kk * P:(kk + 1) * P], ident)
                    mm.then_inc(h_t, 1)

                def down(half, ks):
                    for k in ks:
                        for n in range(2):
                            mm = nc.tensor.matmul(bank[:, YB + n, :], hT[:, half * 4 + k, :],
                                                  w2s[half][:, k, n * NC:(n + 1) * NC], start=False,
                                                  stop=half == 1 and k == 3, skip_group_check=True)
                    return mm

                eng.wait_ge(rows_in, 16)
                transpose_rows()

                def body(b):
                    for c in range(4):
                        eng.wait_ge(w1_in[c], b * 16 + 16)
                        if c == 0:
                            eng.wait_ge(x_e, b * 2 + 2)
                        for k in range(KD):
                            nc.tensor.matmul(bank[:, GB + c, :], xT[:, k, :], w1s[c][:, k, :], start=k == 0, stop=False)
                        if c == 0:
                            eng.wait_ge(oh_ready, b + 1)
                        nc.tensor.matmul(bank[:, GB + c, :], ohb, b3[:, GU[c]:GU[c] + NC],
                                         start=False, stop=True).then_inc(gu_done, 1)
                        if c == 2:
                            eng.wait_ge(act_ok, b * 2 + 1)
                            transpose_act(0)
                    eng.wait_ge(rows_in, b * 16 + 32)
                    transpose_rows()
                    eng.wait_ge(y_out, b * 2 + 2)
                    for n in range(2):
                        nc.tensor.matmul(bank[:, YB + n, :], ohb, b3[:, 2 * FF + n * NC:2 * FF + (n + 1) * NC],
                                         start=True, stop=False, skip_group_check=True)
                    eng.wait_ge(h_e, b * 2 + 1)
                    eng.wait_ge(w2_in[0], b * 16 + 16)
                    down(0, (0, 1))
                    eng.wait_ge(act_ok, b * 2 + 2)
                    transpose_act(1)
                    down(0, (2, 3)).then_inc(y_done, 1)
                    eng.wait_ge(h_e, b * 2 + 2)
                    eng.wait_ge(w2_in[1], b * 16 + 16)
                    down(1, range(4)).then_inc(y_done, 1)
                each_block(eng, body)

            @block.scalar
            def _(eng):
                eng.sem_inc(y_out, 1)

                def copy_rows(count):
                    eng.wait_ge(x_t, count)
                    nc.scalar.activation(xT[:, 4:8, :], bank[:, GB + 1, :].rearrange("p (k m) -> p k m", k=4), ACT.Copy)\
                      .then_inc(x_e, 1)
                copy_rows(2)

                def body(b):
                    for half in range(2):
                        eng.wait_ge(gate_ok, b * 2 + half + 1)
                        nc.scalar.activation(act_[:, half * NC:(half + 1) * NC], gsb_[:, half * NC:(half + 1) * NC],
                                             ACT.Sigmoid, scale=1.702).then_inc(sig_ok, 1)
                        if half:
                            copy_rows(b * 2 + 4)
                        eng.wait_ge(h_t, b * 2 + half + 1)
                        nc.scalar.activation(hT[:, half * 4:half * 4 + 4, :],
                                             bank[:, HB + half, :].rearrange("p (k m) -> p k m", k=4), ACT.Copy).then_inc(h_e, 1)
                    eng.wait_ge(y_done, b * 2 + 2)
                    eng.wait_ge(y_st, b * 16 + 16)
                    nc.scalar.activation(ysb[:, 0:NC], bank[:, YB, :], ACT.Copy).then_inc(y_out, 1)
                    eng.wait_ge(y_out, b * 2 + 4)
                    eng.dma_start(y_dram[bass.ds(b * P, P), :], ysb).then_inc(y_st, 16)
                n = each_block(eng, body)
                eng.wait_ge(y_st, n * 16 + 16)
                eng.sem_inc(all_stored, 1)

            @block.vector
            def _(eng):
                eng.sem_inc(y_out, 1)
                eng.sem_inc(y_st, 16)

                def pick(col):
                    nc.vector.tensor_scalar(ohb, cst[0:3 * NE, _C["emod"][0]:_C["emod"][0] + P],
                                            blkf[0:3 * NE, col], None, ALU.is_equal).then_inc(oh_ready, 1)

                def copy_rows(count):
                    eng.wait_ge(x_t, count)
                    nc.vector.tensor_copy(xT[:, 0:4, :], bank[:, GB, :].rearrange("p (k m) -> p k m", k=4)).then_inc(x_e, 1)
                pick(slice(0, 1))
                copy_rows(1)

                def body(b):
                    for half in range(2):
                        lo, hi = half * NC, (half + 1) * NC
                        eng.wait_ge(gu_done, b * 4 + 2 * half + 1)
                        nc.vector.tensor_scalar(gsb_[:, lo:hi], bank[:, GB + 2 * half, :], 7.0, None, ALU.min).then_inc(gate_ok, 1)
                        eng.wait_ge(gu_done, b * 4 + 2 * half + 2)
                        nc.vector.tensor_scalar(usb[:, lo:hi], bank[:, GB + 2 * half + 1, :], 7.0, -7.0, ALU.min, ALU.max)\
                          .then_inc(up_ok, 1)
                        eng.wait_ge(up_ok, b * 2 + half + 1)
                        nc.vector.scalar_tensor_tensor(out=usb[:, lo:hi], in0=usb[:, lo:hi], scalar=1.0, in1=gsb_[:, lo:hi],
                                                       op0=ALU.add, op1=ALU.mult).then_inc(mul_ok, 1)
                        eng.wait_ge(mul_ok, b * 2 + half + 1)
                        eng.wait_ge(sig_ok, b * 2 + half + 1)
                        nc.vector.tensor_tensor(act_[:, lo:hi], act_[:, lo:hi], usb[:, lo:hi], ALU.mult).then_inc(act_ok, 1)
                    copy_rows(b * 2 + 3)
                    eng.wait_ge(y_done, b * 2 + 2)
                    pick(bass.ds(b + 1, 1))
                    eng.wait_ge(y_st, b * 16 + 16)
                    nc.vector.tensor_copy(ysb[:, NC:D], bank[:, YB + 1, :]).then_inc(y_out, 1)
                each_block(eng, body)

        got = [region(j * D, D) for j in range(8)]
        got_in = [sem(f"got_in{j}") for j in range(8)]
        dv = steps("dve", [(k, tt) for k in range(EK) for tt in range(NT)])
        with nc.Block() as block:
            @block.gpsimd
            def _(eng):
                for n in range(NT * EK):
                    k, tt = n // NT, n % NT
                    if n >= 8:
                        eng.wait_ge(dve_done, dv[(n - 8) // NT, (n - 8) % NT])
                    eng.indirect_dma_start(got[n % 8], None, y_dram,
                                           bass.IndirectOffsetOnAxis(ap=srow[:, tt * EK + k:tt * EK + k + 1], axis=0))\
                       .then_inc(got_in[n % 8], 16)

            @block.vector
            def _(eng):
                for n in range(NT * EK):
                    k, tt = n // NT, n % NT
                    eng.wait_ge(got_in[n % 8], 16 * (n // 8 + 1))
                    if k:
                        eng.wait_ge(dve_done, dv[k - 1, tt])
                    nc.vector.scalar_tensor_tensor(out=h[:, tt, :], in0=got[n % 8], scalar=gk[:, tt * EK + k:tt * EK + k + 1],
                                                   in1=h[:, tt, :], op0=ALU.mult, op1=ALU.add).then_inc(dve_done, 1)

        stored = sem("stored")

        def store(sp, dv):
            for i in range(NT):
                sp.wait_ge(dve_done, dv["scale", i])
                sp.dma_start(out[0, i * P:(i + 1) * P, :], tok[:, i, :]).then_inc(stored, 16)
            sp.wait_ge(stored, 16 * NT)
        final_norm(h, 1, t["g_final_2"].rearrange("(o d) -> o d", o=1), tok, tok, done_sp=store)


_RAW = ["x", "w_in", "ln_c_g", "ln_c_b", "w_out", "g_ffn", "w_q", "expert_u", "expert_v", "w_pe", "w_pg", "g_final",
        "mem_2", "w_in_2", "w_pool_2", "w_out_2", "w_mem_q_2", "w_mem_kv_2", "w_mem_o_2", "g_ffn_2", "w_router_2",
        "b_router_2", "w_expert_in_2", "w_expert_out_2", "g_final_2"]


def _channels(a, tiles):
    a = np.asarray(a)
    a = a.reshape(tiles, P, -1)
    return np.ascontiguousarray(a.transpose(1, 0, 2)).reshape(P, -1)


def kernel(**inputs):
    import concourse.bacc as _bacc
    from concourse.bass_utils import run_bass_kernel_spmd as _run

    i = {k: np.asarray(v) for k, v in inputs.items()}
    arrays = {n: np.ascontiguousarray(i[n]) for n in _RAW}
    b_s = i["b_s"][0].reshape(TC, 2, P)
    parts = {
        "g_mix": _channels(i["g_mix"][0], KD), "conv_a_w": _channels(i["conv_a_w"][0].T, TA),
        "conv_a_b": _channels(i["conv_a_b"][0], TA), "ln_a_g": _channels(i["ln_a_g"][0], TA),
        "ln_a_b": _channels(i["ln_a_b"][0], TA), "conv_b_w": _channels(i["conv_b_w"][0].T, TB),
        "g_ple": _channels(i["g_ple"][0], KD), "g_mix_2": _channels(i["g_mix_2"][0], KD),
        "g_sb": _channels(i["g_sb_out_2"][0], 4), "g_pool": _channels(i["g_pool_out_2"][0], 4),
        "pool_scale": _channels(i["pool_scale_2"][0], 4), "g_mem_q": _channels(i["g_mem_q_2"][0], KD),
        "g_mem_kv": _channels(i["g_mem_kv_2"][0], KD),
        "b_s": np.repeat(b_s.transpose(1, 0, 2).reshape(2, TC * P), HD, axis=0),
    }
    arrays["params"] = np.ascontiguousarray(np.concatenate([parts[n] for n in _Q], axis=1))
    arrays["consts"] = constants()
    arrays["w_s_T"] = np.ascontiguousarray(i["w_s"][0].transpose(2, 0, 1))
    arrays["sub_keys_T"] = np.ascontiguousarray(i["sub_keys"][0].reshape(HH, NK, P).transpose(2, 0, 1))
    arrays["p_T"] = np.ascontiguousarray(i["p"][0, 0].T)
    arrays["b_expert"] = np.ascontiguousarray(np.concatenate([i["b_expert_in_2"][0], i["b_expert_out_2"][0]], axis=1))

    nc = _bacc.Bacc("TRN2", target_bir_lowering=False, num_devices=1)
    t = {n: nc.dram_tensor(f"in_{n}", a.shape, mybir.dt.from_np(a.dtype), kind="ExternalInput").ap()
         for n, a in arrays.items()}
    out = nc.dram_tensor("out_0", (1, S, D), F32, kind="ExternalOutput").ap()
    build(nc, t, out)
    r = _run(nc, [{f"in_{n}": a for n, a in arrays.items()}], core_ids=[0])
    return r.results[0]["out_0"]
```

```python
from contextlib import ExitStack

import numpy as np

import concourse.bass as bass
from concourse import mybir

ALU = mybir.AluOpType
ACT = mybir.ActivationFunctionType
F32 = mybir.dt.float32
BF16 = mybir.dt.bfloat16
I32 = mybir.dt.int32
U32 = mybir.dt.uint32
AX = mybir.AxisListType.X

P = 128
S = 512
D = 1024
NT = S // P
KD = D // P
NC = 512
D_A, D_B, D_C = 384, 256, 384
TA, TB, TC = D_A // P, D_B // P, D_C // P
IN_COLS = 2 * D_A + 3 * D_B + 2 * D_C
WA, WB = 31, 3
HC = 6
HH = 16
PH = 8
NK = 128
TOPK = 16
PLE = 256
SBH = 8
HD = 64
WINS = (2, 4, 8, 16)
PADU = 16
NMEM = 256
TM = NMEM // P
MH = 4
NE = 32
EK = 4
FF = 1024
EPS1, EPS2 = 1e-6, 1e-5
NBLK = 47
NBP = 48
LEAST_LIVE = S * EK // P
GRP = 8
LOWEST = -3.0e38

_C = {}
_n = 0
for _name, _w in (("ident", P), ("lt", P), ("gt", P), ("ones", P), ("bones", P), ("wsmask", P),
                  ("iota", NBP), ("tok", NT), ("emod", P), ("rcount", 4 * PADU), ("zero", P), ("eps", 2)):
    _C[_name] = (_n, _w)
    _n += _w
NCONST = _n

_Q = {}
_n = 0
for _name, _w in (("g_mix", KD), ("conv_a_w", TA * WA), ("conv_a_b", TA), ("ln_a_g", TA), ("ln_a_b", TA),
                  ("conv_b_w", TB * WB), ("g_ple", KD), ("g_mix_2", KD), ("g_sb", 4), ("g_pool", 4),
                  ("pool_scale", 4), ("g_mem_q", KD), ("g_mem_kv", KD), ("b_s", TC * P)):
    _Q[_name] = (_n, _w)
    _n += _w
NPAR = _n


def constants():
    c = np.zeros((P, NCONST), np.float32)
    p = np.arange(P)[:, None]
    m = np.arange(P)[None, :]

    def put(name, a):
        o, w = _C[name]
        c[:, o:o + w] = a

    put("ident", p == m)
    put("lt", p < m)
    put("gt", p > m)
    put("ones", 1.0)
    put("bones", (p // HD == m // HD) / HD)
    put("wsmask", p // HD <= m // HD)
    put("iota", np.arange(NBP)[None, :])
    put("tok", p + P * np.arange(NT)[None, :])
    put("emod", p % NE + 0 * m)
    t = np.arange(PADU)
    put("rcount", np.concatenate([1.0 / np.minimum(t + 1, w) for w in WINS])[None, :])
    put("eps", np.array([[EPS1, EPS2]]))
    return c


class Steps:

    def __init__(self, start, labels):
        self.start, self.labels = start, list(labels)
        self.at = {label: start + i + 1 for i, label in enumerate(self.labels)}

    def __getitem__(self, label):
        return self.at[label]

    def end(self):
        return self.start + len(self.labels)


def build(nc, t, out):
    ctx = ExitStack()
    with ctx:
        def sb(name, shape, dt=F32):
            return ctx.enter_context(nc.sbuf_tensor(name, shape, dt))

        def sem(name):
            return ctx.enter_context(nc.semaphore(name))

        wring = [sb(f"wring{i}", [P, KD * NC]) for i in range(4)]
        X = sb("work", [P, 4 * KD * NC])
        h = sb("h", [P, NT, D])
        aT = sb("aT", [P, KD, S])
        tok = sb("tok", [P, NT, D])
        mixT = tok[:, :, :].rearrange("p t d -> p (t d)").rearrange("p (k s) -> p k s", k=KD)
        cst = sb("cst", [P, NCONST])
        par = sb("par", [P, NPAR])
        grow = sb("grow", [P, D])
        stat = sb("stat", [P, 64])
        bank = ctx.enter_context(nc.psum_tensor("banks", [P, 8, NC], F32))

        def const(name, lo=0, hi=None):
            o, w = _C[name]
            return cst[:, o + lo:o + (w if hi is None else hi)]

        def param(name, lo=0, hi=None):
            o, w = _Q[name]
            return par[:, o + lo:o + (w if hi is None else hi)]

        ident = const("ident")

        xn_dram = nc.dram_tensor("ffn_rows", (S, D), F32).ap()
        tokmap_dram = nc.dram_tensor("slot_tokens", (P * NBP, 1), I32).ap()
        y_dram = nc.dram_tensor("expert_rows", (NBP * P, D), F32).ap()

        pe_done = sem("pe_done")
        dve_done = sem("dve_done")
        act_done = sem("act_done")
        pool_done = sem("pool_done")
        first_in = sem("first_in")
        late_in = sem("late_in")
        rows_filled = sem("rows_filled")
        row_in = sem("row_in")
        chunk_in = [sem(f"chunk_in{i}") for i in range(4)]
        at = {"pe": 0, "dve": 0, "act": 0, "pool": 0, "late": 0, "row": 0}

        def steps(eng, labels):
            s = Steps(at[eng], labels)
            at[eng] = s.end()
            return s

        def cols(w, lo, n=NC, k=KD):
            return w.rearrange("(k p) n -> p k n", p=P)[:, 0:k, lo:lo + n], k, n

        w_in, w_in2 = t["w_in"][0], t["w_in_2"][0]
        chunks = [cols(w_in, c) for c in (0, 512, 1024)] + [cols(w_in, 1536, D_C), cols(w_in, 1536 + D_C, D_C)]
        chunks += [cols(t["w_out"][0], c) for c in (0, 512)]
        chunks += [cols(t["w_q"][0], c) for c in (0, 512, 1024, 1536)]
        chunks += [cols(t["w_pg"][0], c) for c in (0, 512)]
        chunks += [cols(t["w_pe"][0], 0, D, PLE // P)]
        chunks += [cols(w_in2, c) for c in (0, 512, 1024, 1536)]
        chunks += [cols(t["w_out_2"][0], c) for c in (0, 512)]
        chunks += [cols(t["w_mem_kv_2"][0], c) for c in (0, 512, 1024, 1536)]
        chunks += [cols(t["w_mem_q_2"][0], c) for c in (0, 512)]
        chunks += [cols(t["w_mem_o_2"][0], c) for c in (0, 512)]
        (C_IN, C_OUT, C_Q, C_PG, C_PE, C_IN2, C_OUT2, C_KV, C_MQ, C_MO) = (0, 5, 7, 11, 13, 14, 18, 20, 24, 26)

        def chunk_view(i):
            _, k, n = chunks[i]
            return wring[i % 4][:, 0:k * n].rearrange("p (k n) -> p k n", k=k)

        def load_chunk(sp, i):
            if i < len(chunks):
                sp.dma_start(chunk_view(i), chunks[i][0]).then_inc(chunk_in[i % 4], 16)

        def wait_chunk(eng, i):
            eng.wait_ge(chunk_in[i % 4], 16 * (i // 4 + 1))

        def dense(jobs, before_sp=None, after_dve=None):
            pe = steps("pe", range(len(jobs)))
            dv = steps("dve", [j for j, job in enumerate(jobs) if job[3] == "dve"])
            ac = steps("act", [j for j, job in enumerate(jobs) if job[3] == "act"])

            def evacuated(j):
                return (dve_done, dv[j]) if jobs[j][3] == "dve" else (act_done, ac[j])

            last_of = {}
            for j, job in enumerate(jobs):
                last_of[job[0]] = j
            with nc.Block() as block:
                @block.sync
                def _(sp):
                    if before_sp:
                        before_sp(sp)
                    for c, j in last_of.items():
                        sp.wait_ge(pe_done, pe[j])
                        load_chunk(sp, c + 4)

                @block.tensor
                def _(eng):
                    seen = set()
                    for j, (c, mms, _, _, _, _) in enumerate(jobs):
                        if c not in seen:
                            wait_chunk(eng, c)
                            seen.add(c)
                        if j >= 8:
                            eng.wait_ge(*evacuated(j - 8))
                        for i, (dst, lhsT, rhs, start, stop) in enumerate(mms):
                            mm = nc.tensor.matmul(dst(j % 8), lhsT, rhs, start=start, stop=stop)
                        mm.then_inc(pe_done, 1)

                def evacuate(eng, which, s, done):
                    for j, job in enumerate(jobs):
                        if job[3] != which:
                            continue
                        eng.wait_ge(pe_done, pe[j])
                        if job[5] is not None:
                            eng.wait_ge(*evacuated(job[5]))
                        job[4](j % 8).then_inc(done, 1)

                @block.vector
                def _(eng):
                    evacuate(eng, "dve", dv, dve_done)

                @block.scalar
                def _(eng):
                    evacuate(eng, "act", ac, act_done)

        def whole(n=NC, rows=P):
            return lambda b: bank[0:rows, b, 0:n]

        def t_job(c, col, src, n, who, evac, after=None, m=P):
            w = chunk_view(c)
            k = chunks[c][1]
            mms = [(whole(n), w[:, i, col:col + m], src[:, i, 0:n], i == 0, i == k - 1) for i in range(k)]
            return (c, mms, m, who, evac, after)

        def tok_job(c, col, n, src, tt, who, evac, after=None):
            w = chunk_view(c)
            k = chunks[c][1]
            mms = [(whole(n), src[:, i, tt * P:(tt + 1) * P], w[:, i, col:col + n], i == 0, i == k - 1)
                   for i in range(k)]
            return (c, mms, P, who, evac, after)

        def normalise(src, ntt, eps_col, gain, dst, dstT, row=None, row_ap=None, sp_work=None):
            ac = steps("act", [("sq", i) for i in range(ntt)] + ["sd"] + [("out", k) for k in range(1, KD, 2)])
            dv = steps("dve", ["rstd"] + [("scale", i) for i in range(ntt)] + [("out", k) for k in range(0, KD, 2)])
            pe = steps("pe", range(KD))
            ss, sd, rstd = stat[:, 0:ntt], stat[:, 4:4 + ntt], stat[:, 8:8 + ntt]
            if row_ap is not None:
                at["row"] += 16
            row_at = at["row"]
            with nc.Block() as block:
                @block.sync
                def _(sp):
                    if row_ap is not None:
                        sp.dma_start(grow[:, :], row_ap.to_broadcast([P, D])).then_inc(row_in, 16)
                    if sp_work:
                        sp_work(sp)

                @block.scalar
                def _(eng):
                    for i in range(ntt):
                        nc.scalar.activation(dst[:, i, :], src[:, i, :], ACT.Square,
                                             accum_out=ss[:, i:i + 1]).then_inc(act_done, 1)
                    eng.wait_ge(act_done, ac["sq", ntt - 1])
                    nc.scalar.activation(sd, ss, ACT.Sqrt, scale=1.0 / D,
                                         bias=const("eps", eps_col, eps_col + 1)).then_inc(act_done, 1)
                    for k in range(1, KD, 2):
                        eng.wait_ge(pe_done, pe[k])
                        g = 1.0 if gain is None else gain[:, k:k + 1]
                        nc.scalar.activation(dstT[:, k, 0:ntt * P], bank[:, k, 0:ntt * P], ACT.Copy,
                                             scale=g).then_inc(act_done, 1)

                @block.vector
                def _(eng):
                    eng.wait_ge(act_done, ac["sd"])
                    nc.vector.reciprocal(rstd, sd).then_inc(dve_done, 1)
                    eng.wait_ge(dve_done, dv["rstd"])
                    if row is not None:
                        eng.wait_ge(row_in, row_at)
                    for i in range(ntt):
                        if row is None:
                            ins = nc.vector.tensor_scalar(dst[:, i, :], src[:, i, :], rstd[:, i:i + 1], None, ALU.mult)
                        else:
                            ins = nc.vector.scalar_tensor_tensor(out=dst[:, i, :], in0=src[:, i, :],
                                                                 scalar=rstd[:, i:i + 1], in1=row[:, :],
                                                                 op0=ALU.mult, op1=ALU.mult)
                        ins.then_inc(dve_done, 1)
                    for k in range(0, KD, 2):
                        eng.wait_ge(pe_done, pe[k])
                        if gain is None:
                            ins = nc.vector.tensor_copy(dstT[:, k, 0:ntt * P], bank[:, k, 0:ntt * P])
                        else:
                            ins = nc.vector.tensor_scalar(dstT[:, k, 0:ntt * P], bank[:, k, 0:ntt * P],
                                                          gain[:, k:k + 1], None, ALU.mult)
                        ins.then_inc(dve_done, 1)

                @block.tensor
                def _(eng):
                    for k in range(KD):
                        for i in range(ntt):
                            if k == 0:
                                eng.wait_ge(dve_done, dv["scale", i])
                            mm = nc.tensor.transpose(bank[:, k, i * P:(i + 1) * P], dst[:, i, k * P:(k + 1) * P], ident)
                        mm.then_inc(pe_done, 1)

        def final_norm(src, eps_col, row_ap, dst, junk, done_sp=None):
            ac = steps("act", [("sq", i) for i in range(NT)] + ["sd"])
            dv = steps("dve", ["rstd"] + [("scale", i) for i in range(NT)])
            ss, sd, rstd = stat[:, 0:NT], stat[:, 4:4 + NT], stat[:, 8:8 + NT]
            at["row"] += 16
            row_at = at["row"]
            with nc.Block() as block:
                @block.sync
                def _(sp):
                    sp.dma_start(grow[:, :], row_ap.to_broadcast([P, D])).then_inc(row_in, 16)
                    if done_sp:
                        done_sp(sp, dv)

                @block.scalar
                def _(eng):
                    for i in range(NT):
                        nc.scalar.activation(junk[:, i, :], src[:, i, :], ACT.Square,
                                             accum_out=ss[:, i:i + 1]).then_inc(act_done, 1)
                    eng.wait_ge(act_done, ac["sq", NT - 1])
                    nc.scalar.activation(sd, ss, ACT.Sqrt, scale=1.0 / D,
                                         bias=const("eps", eps_col, eps_col + 1)).then_inc(act_done, 1)

                @block.vector
                def _(eng):
                    eng.wait_ge(act_done, ac["sd"])
                    nc.vector.reciprocal(rstd, sd).then_inc(dve_done, 1)
                    eng.wait_ge(dve_done, dv["rstd"])
                    eng.wait_ge(row_in, row_at)
                    for i in range(NT):
                        nc.vector.scalar_tensor_tensor(out=dst[:, i, :], in0=src[:, i, :], scalar=rstd[:, i:i + 1],
                                                       in1=grow[:, :], op0=ALU.mult, op1=ALU.mult).then_inc(dve_done, 1)

        def add_to_h(tt, lo, n=NC):
            def evac(b):
                return nc.vector.tensor_tensor(h[:, tt, lo:lo + n], h[:, tt, lo:lo + n], bank[:, b, 0:n], ALU.add)
            return evac

        def project_into_h(c0, src):
            dense([tok_job(c0 + n, 0, NC, src, tt, "dve", add_to_h(tt, n * NC)) for n in range(2) for tt in range(NT)])

        def region(lo, n):
            return X[:, lo:lo + n]

        o = 0
        zT = region(o, 15 * S).rearrange("p (c s) -> p c s", c=15)
        o += 15 * S
        vt = region(o, NT * D_C).rearrange("p (t n) -> p t n", t=NT)
        o += NT * D_C
        LA = S + WA - 1
        ya_in = region(o, TA * LA).rearrange("p (c s) -> p c s", c=TA)
        o += TA * LA
        acc = region(o, TA * S).rearrange("p (c s) -> p c s", c=TA)
        o += TA * S
        LB = S + WB - 1
        yb_in = region(o, TB * LB).rearrange("p (c s) -> p c s", c=TB)
        o += TB * LB
        yb_t = region(o, TB * S).rearrange("p (c s) -> p c s", c=TB)
        o += TB * S
        lnc = region(o, 2 * D_C)
        o += 2 * D_C
        wsT = region(o, HC * P).rearrange("p (h i) -> p h i", h=HC)
        o += HC * P
        assert o <= 4 * KD * NC
        VAL, GATE, BG, CG, XB, U = 0, TA, 2 * TA, 2 * TA + TB, 2 * TA + 2 * TB, 2 * TA + 3 * TB

        with nc.Block() as block:
            @block.sync
            def _(sp):
                sp.dma_start(h[:, :, :], t["x"][0].rearrange("(t p) d -> p t d", p=P)).then_inc(first_in, 16)
                sp.dma_start(cst[:, :], t["consts"][:, :]).then_inc(first_in, 16)
                sp.dma_start(par[:, :], t["params"][:, :]).then_inc(first_in, 16)
                load_chunk(sp, 0)
                sp.dma_start(wsT[:, :, :], t["w_s_T"][:, :, :]).then_inc(first_in, 16)
                sp.dma_start(lnc[:, 0:D_C], t["ln_c_g"][0:1, :].to_broadcast([P, D_C])).then_inc(first_in, 16)
                sp.dma_start(lnc[:, D_C:2 * D_C], t["ln_c_b"][0:1, :].to_broadcast([P, D_C])).then_inc(first_in, 16)
                for c in range(1, 4):
                    load_chunk(sp, c)
                sp.wait_ge(first_in, 96)

        normalise(h, NT, 0, param("g_mix"), tok, aT)

        def copy_z(c, who):
            if who == "act":
                f = ACT.Sigmoid if GATE <= c < BG else ACT.Copy
                return lambda b: nc.scalar.activation(zT[:, c, :], bank[:, b, :], f)
            return lambda b: nc.vector.tensor_copy(zT[:, c, :], bank[:, b, :])

        jobs = []
        for c in range(15):
            who = "act" if GATE <= c < BG or c % 2 else "dve"
            jobs.append(t_job(C_IN + c * P // NC, c * P % NC, aT, S, who, copy_z(c, who)))
        for tt in range(NT):
            jobs.append(tok_job(C_IN + 4, 0, D_C, aT, tt, "dve",
                                lambda b, tt=tt: nc.vector.tensor_copy(vt[:, tt, :], bank[:, b, 0:D_C])))
        dense(jobs)

        v24 = vt[:, :, :].rearrange("p t (h c) -> p (t h) c", h=HC)
        sq24 = acc[:, :, :].rearrange("p c s -> p (c s)").rearrange("p (g c) -> p g c", c=HD)
        m24, s24, r24 = stat[:, 12:36], stat[:, 36:60], stat[:, 12:36]
        nG = NT * HC

        def over(x, n):
            return x.rearrange("p (g o) -> p g o", o=1).to_broadcast([P, x.shape[1], n])

        def over_t(x):
            return x.rearrange("p (o n) -> p o n", o=1).to_broadcast([P, NT, x.shape[1]])

        dv = steps("dve", ["vsum", "vmean", "vsub", "vvar", "vr", "vscale", "vg", "vb"]
                   + [("pad", c) for c in range(TA)] + [("glu", c) for c in range(TA)]
                   + [("tap", k, c) for k in range(WA) for c in range(TA)]
                   + [("u1", i) for i in range(TC)] + [("u2", i) for i in range(TC)]
                   + [("am", c) for c in range(TA)] + [("ar", c) for c in range(TA)]
                   + [("as", c) for c in range(TA)])
        ac = steps("act", ["vsq", "vsd"] + [("asq", c) for c in range(TA)] + [("asd", c) for c in range(TA)]
                   + [("silu", c) for c in range(TA)])
        pe = steps("pe", [("mix", i) for i in range(TC)] + [("am", c) for c in range(TA)] + [("av", c) for c in range(TA)])
        po = steps("pool", ["ws", "pad"] + [("g", c) for c in range(TB)]
                   + [("t", k, c) for k in range(WB) for c in range(TB)]
                   + [("s", k, c) for k in range(1, WB) for c in range(TB)] + [("out", c) for c in range(TB)])
        with nc.Block() as block:
            @block.scalar
            def _(eng):
                eng.wait_ge(dve_done, dv["vsub"])
                nc.scalar.activation(sq24, v24, ACT.Square).then_inc(act_done, 1)
                eng.wait_ge(dve_done, dv["vvar"])
                nc.scalar.activation(s24, s24, ACT.Sqrt, scale=1.0 / HD, bias=const("eps", 0, 1)).then_inc(act_done, 1)
                for c in range(TA):
                    eng.wait_ge(dve_done, dv["am", c])
                    nc.scalar.activation(zT[:, GATE + c, :], acc[:, c, :], ACT.Square).then_inc(act_done, 1)
                for c in range(TA):
                    eng.wait_ge(pe_done, pe["av", c])
                    nc.scalar.activation(zT[:, VAL + c, :], bank[:, 3 + c, :], ACT.Sqrt,
                                         bias=const("eps", 0, 1)).then_inc(act_done, 1)
                for c in range(TA):
                    eng.wait_ge(dve_done, dv["as", c])
                    nc.scalar.activation(mixT[:, c, :], acc[:, c, :], ACT.Silu, scale=param("ln_a_g", c, c + 1),
                                         bias=param("ln_a_b", c, c + 1)).then_inc(act_done, 1)

            @block.vector
            def _(eng):
                nc.vector.tensor_reduce(m24, v24, AX, ALU.add).then_inc(dve_done, 1)
                eng.wait_ge(dve_done, dv["vsum"])
                nc.vector.tensor_scalar(m24, m24, 1.0 / HD, None, ALU.mult).then_inc(dve_done, 1)
                eng.wait_ge(dve_done, dv["vmean"])
                nc.vector.tensor_tensor(v24, v24, over(m24, HD), ALU.subtract).then_inc(dve_done, 1)
                eng.wait_ge(act_done, ac["vsq"])
                nc.vector.tensor_reduce(s24, sq24, AX, ALU.add).then_inc(dve_done, 1)
                eng.wait_ge(act_done, ac["vsd"])
                nc.vector.reciprocal(r24, s24).then_inc(dve_done, 1)
                eng.wait_ge(dve_done, dv["vr"])
                nc.vector.tensor_tensor(v24, v24, over(r24, HD), ALU.mult).then_inc(dve_done, 1)
                eng.wait_ge(dve_done, dv["vscale"])
                nc.vector.tensor_tensor(vt[:, :, :], vt[:, :, :], over_t(lnc[:, 0:D_C]), ALU.mult).then_inc(dve_done, 1)
                eng.wait_ge(dve_done, dv["vg"])
                nc.vector.tensor_tensor(vt[:, :, :], vt[:, :, :], over_t(lnc[:, D_C:2 * D_C]), ALU.add).then_inc(dve_done, 1)
                for c in range(TA):
                    nc.vector.memset(ya_in[:, c, 0:WA - 1], 0.0).then_inc(dve_done, 1)
                for c in range(TA):
                    nc.vector.tensor_tensor(ya_in[:, c, WA - 1:LA], zT[:, VAL + c, :], zT[:, GATE + c, :],
                                            ALU.mult).then_inc(dve_done, 1)
                for k in range(WA):
                    for c in range(TA):
                        w = param("conv_a_w", c * WA + k, c * WA + k + 1)
                        if k == 0:
                            eng.wait_ge(dve_done, dv["glu", c])
                            ins = nc.vector.tensor_scalar(acc[:, c, :], ya_in[:, c, 0:S], w,
                                                          param("conv_a_b", c, c + 1), ALU.mult, ALU.add)
                        else:
                            eng.wait_ge(dve_done, dv["tap", k - 1, c])
                            ins = nc.vector.scalar_tensor_tensor(out=acc[:, c, :], in0=ya_in[:, c, k:k + S], scalar=w,
                                                                 in1=acc[:, c, :], op0=ALU.mult, op1=ALU.add)
                        ins.then_inc(dve_done, 1)
                for i in range(TC):
                    eng.wait_ge(pe_done, pe["mix", i])
                    mixed = mixT[:, TA + TB + i, :].rearrange("p (t i) -> p t i", t=NT)
                    nc.vector.tensor_tensor(mixed, bank[:, i, :].rearrange("p (t i) -> p t i", t=NT),
                                            over_t(param("b_s", i * P, (i + 1) * P)), ALU.add).then_inc(dve_done, 1)
                for i in range(TC):
                    eng.wait_ge(dve_done, dv["u1", i])
                    nc.vector.tensor_tensor(mixT[:, TA + TB + i, :], mixT[:, TA + TB + i, :], zT[:, U + i, :],
                                            ALU.mult).then_inc(dve_done, 1)
                for c in range(TA):
                    eng.wait_ge(pe_done, pe["am", c])
                    nc.vector.tensor_tensor(acc[:, c, :], acc[:, c, :], bank[:, 4 + c % 4, :], ALU.subtract).then_inc(dve_done, 1)
                for c in range(TA):
                    eng.wait_ge(act_done, ac["asd", c])
                    nc.vector.reciprocal(zT[:, VAL + c, :], zT[:, VAL + c, :]).then_inc(dve_done, 1)
                for c in range(TA):
                    eng.wait_ge(dve_done, dv["ar", c])
                    nc.vector.tensor_tensor(acc[:, c, :], acc[:, c, :], zT[:, VAL + c, :], ALU.mult).then_inc(dve_done, 1)

            @block.tensor
            def _(eng):
                eng.wait_ge(dve_done, dv["vb"])
                eng.wait_ge(pool_done, po["ws"])
                for i in range(TC):
                    for tt in range(NT):
                        for half in range(2):
                            hd = 2 * i + half
                            mm = nc.tensor.matmul(bank[half * HD:(half + 1) * HD, i, tt * P:(tt + 1) * P],
                                                  vt[:, tt, hd * HD:(hd + 1) * HD], wsT[:, hd, :],
                                                  start=True, stop=True)
                    mm.then_inc(pe_done, 1)
                for c in range(TA):
                    eng.wait_ge(dve_done, dv["tap", WA - 1, c])
                    nc.tensor.matmul(bank[:, 4 + c % 4, :], const("bones"), acc[:, c, :],
                                     start=True, stop=True).then_inc(pe_done, 1)
                for c in range(TA):
                    eng.wait_ge(act_done, ac["asq", c])
                    if c == 0:
                        eng.wait_ge(dve_done, dv["u1", TC - 1])
                        eng.wait_ge(dve_done, dv["am", TA - 1])
                    nc.tensor.matmul(bank[:, 3 + c, :], const("bones"), zT[:, GATE + c, :],
                                     start=True, stop=True).then_inc(pe_done, 1)

            @block.gpsimd
            def _(eng):
                eng.tensor_tensor(wsT[:, :, :], wsT[:, :, :],
                                  const("wsmask").rearrange("p (o i) -> p o i", o=1).to_broadcast([P, HC, P]),
                                  ALU.mult).then_inc(pool_done, 1)
                eng.memset(yb_in[:, :, 0:WB - 1], 0.0).then_inc(pool_done, 1)
                for c in range(TB):
                    eng.tensor_tensor(yb_in[:, c, WB - 1:LB], zT[:, CG + c, :], zT[:, XB + c, :], ALU.mult).then_inc(pool_done, 1)
                eng.wait_ge(pool_done, po["g", TB - 1])
                dst = [zT[:, CG:CG + TB, :], zT[:, XB:XB + TB, :], yb_t]
                for k in range(WB):
                    for c in range(TB):
                        w = param("conv_b_w", c * WB + k, c * WB + k + 1)
                        eng.tensor_scalar(dst[k][:, c, :], yb_in[:, c, k:k + S], w, None, ALU.mult).then_inc(pool_done, 1)
                for k in range(1, WB):
                    for c in range(TB):
                        eng.wait_ge(pool_done, po["t", k, c] if k == 1 else po["s", k - 1, c])
                        if k > 1:
                            eng.wait_ge(pool_done, po["t", k, c])
                        eng.tensor_tensor(dst[0][:, c, :], dst[0][:, c, :], dst[k][:, c, :], ALU.add).then_inc(pool_done, 1)
                for c in range(TB):
                    eng.wait_ge(pool_done, po["s", WB - 1, c])
                    eng.tensor_tensor(mixT[:, TA + c, :], dst[0][:, c, :], zT[:, BG + c, :], ALU.mult).then_inc(pool_done, 1)

        project_into_h(C_OUT, mixT)

        SC0 = 0
        scores = region(0, NT * HH * NK).rearrange("p (t g k) -> p t g k", t=NT, g=HH)
        qT = region(8192, 4 * S).rearrange("p (c s) -> p c s", c=4)
        keysT = region(10240, HH * NK).rearrange("p (g k) -> p g k", g=HH)
        at["late"] += 16
        keys_at = at["late"]
        normalise(h, NT, 0, None, tok, aT, row=grow, row_ap=t["g_ffn"][0:1, :],
                  sp_work=lambda sp: sp.dma_start(keysT[:, :, :], t["sub_keys_T"][:, :, :]).then_inc(late_in, 16))

        pe = steps("pe", [x for g in range(HH + 1) for x in ([("q", g)] if g < HH else []) + ([("s", g - 1)] if g else [])])
        ac = steps("act", [("q", g) for g in range(HH)])
        dv = steps("dve", [("s", g) for g in range(HH)])
        with nc.Block() as block:
            @block.sync
            def _(sp):
                for c in range(2):
                    sp.wait_ge(pe_done, pe["q", 4 * c + 3])
                    load_chunk(sp, C_Q + c + 4)

            @block.tensor
            def _(eng):
                eng.wait_ge(late_in, keys_at)
                for g in range(HH + 1):
                    if g < HH:
                        if g % 4 == 0:
                            wait_chunk(eng, C_Q + g // 4)
                        if g >= 4:
                            eng.wait_ge(act_done, ac["q", g - 4])
                        w = chunk_view(C_Q + g // 4)
                        for k in range(KD):
                            mm = nc.tensor.matmul(bank[:, g % 4, :], w[:, k, g % 4 * P:(g % 4 + 1) * P], aT[:, k, :],
                                                  start=k == 0, stop=k == KD - 1)
                        mm.then_inc(pe_done, 1)
                    if g:
                        s = g - 1
                        eng.wait_ge(act_done, ac["q", s])
                        if s >= 4:
                            eng.wait_ge(dve_done, dv["s", s - 4])
                        for tt in range(NT):
                            mm = nc.tensor.matmul(bank[:, 4 + s % 4, tt * NK:(tt + 1) * NK],
                                                  qT[:, s % 4, tt * P:(tt + 1) * P], keysT[:, s, :], start=True, stop=True)
                        mm.then_inc(pe_done, 1)

            @block.scalar
            def _(eng):
                for g in range(HH):
                    eng.wait_ge(pe_done, pe["q", g])
                    if g >= 4:
                        eng.wait_ge(pe_done, pe["s", g - 4])
                    nc.scalar.activation(qT[:, g % 4, :], bank[:, g % 4, :], ACT.Copy).then_inc(act_done, 1)

            @block.vector
            def _(eng):
                for g in range(HH):
                    eng.wait_ge(pe_done, pe["s", g])
                    nc.vector.tensor_copy(scores[:, :, g, :], bank[:, 4 + g % 4, :].rearrange("p (t k) -> p t k", t=NT))\
                      .then_inc(dve_done, 1)

        SW = region(NT * HH * NK, HH * NK).rearrange("p (g k) -> p g k", g=HH)
        cand = region(10240, PH * TOPK * TOPK).rearrange("p (h c) -> p h c", h=PH)
        hot = region(12288, PH * TOPK * TOPK)
        o = 14336
        kv = region(o, HH * TOPK).rearrange("p (g k) -> p g k", g=HH)
        ki = region(o + 256, HH * TOPK).bitcast(U32).rearrange("p (g k) -> p g k", g=HH)
        kf = region(o + 512, HH * TOPK).rearrange("p (g k) -> p g k", g=HH)
        cv = region(o + 768, PH * TOPK).rearrange("p (h k) -> p h k", h=PH)
        ci = region(o + 896, PH * TOPK).bitcast(U32)
        cq = region(o + 1024, 2 * PH * TOPK).bitcast(U32)
        cf = region(o + 1280, 2 * PH * TOPK)
        ef = region(o + 1536, 2 * PH * TOPK)
        sm = region(o + 1792, 2 * PH)
        ce = region(o + 1808, PH * TOPK).rearrange("p (h k) -> p h k", h=PH)
        GK = PH * TOPK
        gates = sb("gates", [P, (NT + 1) * GK])
        eidx = sb("eidx", [P, (NT + 1) * GK], I32)
        top = sem("top_steps")
        differ = sem("top_differ")
        exps = sem("top_exp")
        picked = sem("picked")

        def top_program():
            prog = []

            def step(need, f):
                prog.append((need, f))
                return len(prog)

            def best(src, v, i, pre):
                a = step(pre, lambda: nc.vector.max(v[:, 0:8], src))
                b = step(a, lambda: nc.vector.max_index(i[:, 0:8], v[:, 0:8], src))
                c = step(b, lambda: nc.vector.match_replace(src, v[:, 0:8], src, LOWEST))
                d = step(c, lambda: nc.vector.max(v[:, 8:16], src))
                return step(d, lambda: nc.vector.max_index(i[:, 8:16], v[:, 8:16], src))
            return prog, step, best

        prog, step, best = top_program()
        first = step(0, None)
        last = first
        for g in range(HH):
            last = best(SW[:, g, :], kv[:, g, :], ki[:, g, :], first)
        a = step(last, lambda: nc.vector.tensor_copy(kf, ki))
        kv4 = kv.rearrange("p (h two) k -> p h two k", two=2)
        kf4 = kf.rearrange("p (h two) k -> p h two k", two=2)
        c4 = cand.rearrange("p h (i j) -> p h i j", i=TOPK)
        for hd in range(PH):
            s = step(last, lambda hd=hd: nc.vector.tensor_tensor(
                c4[:, hd], kv4[:, hd, 0, :].rearrange("p (i o) -> p i o", o=1).to_broadcast([P, TOPK, TOPK]),
                kv4[:, hd, 1, :].rearrange("p (o j) -> p o j", o=1).to_broadcast([P, TOPK, TOPK]), ALU.add))
        lastc = s
        for hd in range(PH):
            lastc = best(cand[:, hd, :], cv[:, hd, :], ci[:, hd * TOPK:(hd + 1) * TOPK], s)
        s1 = step(lastc, lambda: nc.vector.tensor_scalar(cq[:, 0:GK], ci, 4, None, ALU.logical_shift_right))
        s2 = step(lastc, lambda: nc.vector.tensor_scalar(cq[:, GK:2 * GK], ci, 15, None, ALU.bitwise_and))
        s3 = step(s2, lambda: nc.vector.tensor_copy(cf, cq))
        hot3 = hot.rearrange("p (c i) -> p c i", i=TOPK)
        hot4 = hot.rearrange("p (h c i) -> p h c i", h=PH, i=TOPK)
        iota16 = const("iota", 0, TOPK).rearrange("p (o i) -> p o i", o=1).to_broadcast([P, GK, TOPK])
        s6 = s3
        for half in range(2):
            s4 = step(s6, lambda half=half: nc.vector.tensor_tensor(
                hot3, cf[:, half * GK:(half + 1) * GK].rearrange("p (c o) -> p c o", o=1).to_broadcast([P, GK, TOPK]),
                iota16, ALU.is_equal))
            s5 = s4
            for hd in range(PH):
                s5 = step(s4, lambda half=half, hd=hd: nc.vector.tensor_tensor(
                    hot4[:, hd], hot4[:, hd],
                    kf4[:, hd, half, :].rearrange("p (o i) -> p o i", o=1).to_broadcast([P, TOPK, TOPK]), ALU.mult))
            s6 = step(s5, lambda half=half: nc.vector.tensor_reduce(ef[:, half * GK:(half + 1) * GK], hot3, AX, ALU.add))
        IDX = step(s6, None)
        SUB = step(lastc, lambda: nc.vector.tensor_tensor(
            ce, cv, cv[:, :, 0:1].to_broadcast([P, PH, TOPK]), ALU.subtract))
        s7 = step(SUB, lambda: nc.vector.tensor_reduce(sm[:, 0:PH], ce, AX, ALU.add))
        s8 = step(s7, lambda: nc.vector.reciprocal(sm[:, PH:2 * PH], sm[:, 0:PH]))
        GAT = step(s8, None)
        NSTEP = len(prog)

        def pick_best(eng, tile):
            for n, (need, f) in enumerate(prog):
                if n + 1 == s7:
                    eng.wait_ge(exps, tile + 1)
                elif need:
                    eng.wait_ge(top, need - (need > SUB))
                if n + 1 == first:
                    ins = nc.vector.tensor_copy(SW, X[:, bass.ds(tile * (HH * NK), HH * NK)]
                                                .rearrange("p (g k) -> p g k", g=HH))
                elif n + 1 == IDX:
                    ins = nc.vector.scalar_tensor_tensor(
                        out=eidx[:, bass.ds(tile * GK, GK)], in0=ef[:, 0:GK], scalar=float(NK),
                        in1=ef[:, GK:2 * GK], op0=ALU.mult, op1=ALU.add)
                elif n + 1 == GAT:
                    ins = nc.vector.tensor_tensor(
                        gates[:, bass.ds(tile * GK, GK)].rearrange("p (h k) -> p h k", h=PH), ce,
                        over(sm[:, PH:2 * PH], TOPK), ALU.mult)
                else:
                    ins = f()
                ins.then_inc(differ if n + 1 == SUB else top, 1)
            eng.wait_ge(top, NSTEP - 1)
            eng.sem_clear(top)
            eng.sem_inc(picked, 1)

        def exponentials(eng, tile):
            eng.wait_ge(differ, tile + 1)
            nc.scalar.activation(ce, ce, ACT.Exp).then_inc(exps, 1)

        with nc.Block() as block:
            @block.vector
            def _(eng):
                pick_best(eng, 0)

            @block.scalar
            def _(eng):
                exponentials(eng, 0)

        slot = [wring[C_PE % 4 + j // 4][:, j % 4 * D:(j % 4 + 1) * D] for j in range(GRP)]
        assert (C_PG % 4, (C_PG + 1) % 4, C_PE % 4) == (3, 0, 1) and GRP == 8
        work = aT[:, :, :].rearrange("p k s -> p (k s)")
        o = 0
        dots = work[:, o:o + GK]
        o += GK
        acts = work[:, o:o + GK]
        o += GK
        diag = work[:, o:o + GRP * P].rearrange("p (b m) -> p b m", b=GRP)
        o += GRP * P
        vsum = work[:, o:o + D]
        o += D
        cur = work[:, o:o + 2 * GRP].bitcast(I32)
        row_in_slot = [sem(f"row_in_slot{j}") for j in range(GRP)]
        slot_used = [sem(f"slot_used{j}") for j in range(GRP)]
        cur_ready = sem("cur_ready")
        pool_turn = sem("pool_turn")
        gelu_done = sem("gelu_done")
        acts_done = sem("acts_done")
        diag_done = sem("diag_done")
        vsum_step = sem("vsum_step")
        h_added = sem("h_added")
        dve_turn, act_turn = sem("dve_turn"), sem("act_turn")
        acc_zero = sem("acc_zero")
        acc_free = sem("acc_free")
        u_rows, v_rows = t["expert_u"][0], t["expert_v"][0]
        NG = GK // GRP
        NA = 5
        BY_DVE = (1, 4, 7)
        BY_PE = tuple(j for j in range(GRP) if j not in BY_DVE)
        PE_ROWS = NA * GRP + (NG - NA) * len(BY_PE)
        DVE_ROWS = (NG - NA) * len(BY_DVE)
        h2 = h[:, :, :].rearrange("p t d -> p (t d)")
        tok2 = tok[:, :, :].rearrange("p t d -> p (t d)")

        def turn(tt, g, v):
            return tt * (2 * NG) + g + (NG if v else 0)

        with nc.Block() as block:
            @block.gpsimd
            def _(eng):
                def gather(rows, tt, g, side, v):
                    ix = cur[:, side * GRP:(side + 1) * GRP]
                    eng.tensor_copy(ix, eidx[:, bass.ds(tt * GK + g * GRP, GRP)]).then_inc(cur_ready, 1)
                    eng.wait_ge(cur_ready, turn(tt, g, v) + 1)
                    eng.sem_inc(pool_turn, 1)
                    for j in range(GRP):
                        eng.wait_ge(slot_used[j], turn(tt, g, v) + 1)
                        eng.sem_inc(pool_turn, 1)
                        eng.indirect_dma_start(slot[j], None, rows, bass.IndirectOffsetOnAxis(ap=ix[:, j:j + 1], axis=0))\
                           .then_inc(row_in_slot[j], 16)

                with eng.Fori(0, NT) as tt:
                    eng.wait_ge(picked, tt + 1)
                    eng.sem_inc(pool_turn, 1)
                    for v, rows in enumerate((u_rows, v_rows)):
                        with eng.Fori(0, NG // 2) as pair:
                            gather(rows, tt, pair * 2, 0, v)
                            gather(rows, tt, pair * 2 + 1, 1, v)

            @block.vector
            def _(eng):
                eng.sem_inc(acc_free, 1)
                for j in range(GRP):
                    eng.sem_inc(slot_used[j], 1)
                with eng.Fori(0, NT) as tt:
                    nc.vector.memset(vsum, 0.0).then_inc(vsum_step, 1)
                    with eng.Fori(0, NG) as g:
                        for j in range(GRP):
                            eng.wait_ge(row_in_slot[j], (turn(tt, g, 0) + 1) * 16)
                            nc.vector.scalar_tensor_tensor(
                                out=slot[j], in0=slot[j], scalar=1.0, in1=tok2[:, bass.ds(tt * D, D)], op0=ALU.mult,
                                op1=ALU.mult, accum_out=dots[:, bass.ds(g * GRP + j, 1)]).then_inc(slot_used[j], 1)
                    eng.wait_ge(gelu_done, tt + 1)
                    nc.vector.tensor_tensor(acts, acts, gates[:, bass.ds(tt * GK, GK)], ALU.mult).then_inc(acts_done, 1)
                    with eng.If(tt < NT - 1):
                        pick_best(eng, tt + 1)
                    with eng.Else():
                        eng.nop()
                    eng.wait_ge(acts_done, tt + 1)
                    eng.sem_inc(dve_turn, 1)
                    with eng.Fori(0, NG - NA) as g:
                        for n, j in enumerate(BY_DVE):
                            eng.wait_ge(row_in_slot[j], (turn(tt, g + NA, 1) + 1) * 16)
                            eng.wait_ge(vsum_step, tt * (DVE_ROWS + 1) + g * len(BY_DVE) + (n + 1))
                            eng.sem_inc(dve_turn, 1)
                            nc.vector.scalar_tensor_tensor(out=vsum, in0=slot[j], scalar=acts[:, bass.ds((g + NA) * GRP + j, 1)],
                                                           in1=vsum, op0=ALU.mult, op1=ALU.add).then_inc(vsum_step, 1)
                            eng.wait_ge(vsum_step, tt * (DVE_ROWS + 1) + g * len(BY_DVE) + (n + 2))
                            eng.sem_inc(slot_used[j], 1)
                    hrow = h2[:, bass.ds(tt * D, D)]
                    for j in range(GRP):
                        eng.wait_ge(slot_used[j], turn(tt, 0, 0) + (2 * NG + 1))
                    eng.sem_inc(dve_turn, 1)
                    nc.vector.tensor_tensor(hrow, hrow, bank[:, 0:2, :].rearrange("p b n -> p (b n)"), ALU.add)\
                      .then_inc(acc_free, 1)
                    eng.wait_ge(acc_free, tt + 2)
                    nc.vector.tensor_tensor(hrow, hrow, vsum, ALU.add).then_inc(h_added, 1)
                    eng.wait_ge(h_added, tt + 1)
                    eng.sem_inc(dve_turn, 1)

            @block.scalar
            def _(eng):
                def diagonal(tt, g, j):
                    eng.wait_ge(slot_used[j], turn(tt, g, 1) + 1)
                    nc.scalar.activation(diag[:, j, :], ident, ACT.Copy,
                                         scale=acts[:, bass.ds(g * GRP + j, 1)]).then_inc(diag_done, 1)

                with eng.Fori(0, NT) as tt:
                    for j in range(GRP):
                        eng.wait_ge(slot_used[j], turn(tt, 0, 1) + 1)
                    nc.scalar.activation(acts, dots, ACT.Gelu_apprx_tanh).then_inc(gelu_done, 1)
                    eng.wait_ge(acts_done, tt + 1)
                    eng.sem_inc(act_turn, 1)
                    with eng.Fori(0, NA) as g:
                        for j in range(GRP):
                            diagonal(tt, g, j)
                    with eng.If(tt < NT - 1):
                        exponentials(eng, tt + 1)
                    with eng.Else():
                        eng.nop()
                    with eng.Fori(NA, NG) as g:
                        for j in BY_PE:
                            diagonal(tt, g, j)

            @block.tensor
            def _(eng):
                def add_row(tt, g, j, rows):
                    eng.wait_ge(diag_done, tt * PE_ROWS + rows)
                    eng.wait_ge(row_in_slot[j], (turn(tt, g, 1) + 1) * 16)
                    for n in range(2):
                        mm = nc.tensor.matmul(bank[:, n, :], diag[:, j, :], slot[j][:, n * NC:(n + 1) * NC],
                                              start=False, stop=False, skip_group_check=True)
                    mm.then_inc(slot_used[j], 1)

                with eng.Fori(0, NT) as tt:
                    eng.wait_ge(acc_free, tt + 1)
                    for n in range(2):
                        mm = nc.tensor.matmul(bank[:, n, :], const("zero"), tok[:, 0, n * NC:(n + 1) * NC],
                                              start=True, stop=False, skip_group_check=True)
                    mm.then_inc(acc_zero, 1)
                    with eng.Fori(0, NA) as g:
                        for j in range(GRP):
                            add_row(tt, g, j, g * GRP + (j + 1))
                    with eng.Fori(0, NG - NA) as g:
                        for n, j in enumerate(BY_PE):
                            add_row(tt, g + NA, j, g * len(BY_PE) + (NA * GRP + n + 1))

        pT = region(0, 2 * S).rearrange("p (k s) -> p k s", k=2)
        gsb = region(2 * S, NT * D).rearrange("p (t d) -> p t d", t=NT)
        at["late"] += 16
        pT_at = at["late"]

        def ple_loads(sp):
            load_chunk(sp, C_PE)
            load_chunk(sp, C_PE + 1)
            sp.dma_start(pT[:, :, :], t["p_T"].rearrange("(k p) s -> p k s", p=P)).then_inc(late_in, 16)
            sp.wait_ge(late_in, pT_at)
        normalise(h, NT, 0, param("g_ple"), tok, aT,
                  sp_work=ple_loads)
        jobs = [tok_job(C_PG + n, 0, NC, aT, tt, "act",
                        lambda b, tt=tt, n=n: nc.scalar.activation(gsb[:, tt, n * NC:(n + 1) * NC], bank[:, b, :], ACT.Sigmoid))
                for n in range(2) for tt in range(NT)]
        jobs += [tok_job(C_PE, n * NC, NC, pT, tt, "dve",
                         lambda b, tt=tt, n=n: nc.vector.tensor_tensor(gsb[:, tt, n * NC:(n + 1) * NC], bank[:, b, :],
                                                                      gsb[:, tt, n * NC:(n + 1) * NC], ALU.mult),
                         after=n * NT + tt)
                 for n in range(2) for tt in range(NT)]
        dense(jobs)
        dv = steps("dve", range(NT))
        with nc.Block() as block:
            @block.vector
            def _(eng):
                for tt in range(NT):
                    nc.vector.tensor_tensor(h[:, tt, :], h[:, tt, :], gsb[:, tt, :], ALU.add).then_inc(dve_done, 1)
        final_norm(h, 0, t["g_final"].rearrange("(o d) -> o d", o=1), h, tok)

        normalise(h, NT, 1, param("g_mix_2"), tok, aT)
        qk = region(0, 8 * S).rearrange("p (c s) -> p c s", c=8)
        v2 = region(4096, NT * S).rearrange("p (t n) -> p t n", t=NT)
        LU = S + PADU
        uT = region(6144, 4 * LU).rearrange("p (g s) -> p g s", g=4)
        jobs = []
        for c in range(4):
            jobs.append(t_job(C_IN2, c * P, aT, S, "act",
                              lambda b, c=c: nc.scalar.activation(qk[:, c, :], bank[:, b, :], ACT.Copy, scale=HD ** -0.5)))
        for c in range(4):
            jobs.append(t_job(C_IN2 + 1, c * P, aT, S, "dve",
                              lambda b, c=c: nc.vector.tensor_copy(qk[:, 4 + c, :], bank[:, b, :])))
        for tt in range(NT):
            jobs.append(tok_job(C_IN2 + 2, 0, NC, aT, tt, "act",
                                lambda b, tt=tt: nc.scalar.activation(v2[:, tt, :], bank[:, b, :], ACT.Copy)))
        for g in range(4):
            jobs.append(t_job(C_IN2 + 3, g * P, aT, S, "dve",
                              lambda b, g=g: nc.vector.tensor_copy(uT[:, g, PADU:LU], bank[:, b, :])))
        dense(jobs)

        OFF = [0, NC, 2 * NC, 2 * NC - P]
        ZW = 10 * P
        zs = [region(8256 + i * ZW, ZW) for i in range(2)]
        sp_ = [region(8256 + (2 + i) * ZW, ZW) for i in range(2)]
        wt = [region(8256 + (4 + i) * ZW, ZW) for i in range(2)]
        pa = aT[:, :, :].rearrange("p k s -> p (k s)")
        pl = [pa[:, i * LU:(i + 1) * LU] for i in range(2)]
        pooled = [pa[:, 2 * LU + g * S:2 * LU + (g + 1) * S] for g in range(4)]
        wpool = grow[:, 0:4 * P].rearrange("p (g e) -> p g e", g=4)
        sqs = [uT[:, k, 0:S] for k in range(4)] + pooled
        at["row"] += 16
        row_at = at["row"]
        ZBANK, ABANK, OBANK, GBANK = 0, 3, 6, 7

        def flat(b0):
            return bank[:, b0:b0 + 3, :].rearrange("p b n -> p (b n)")[:, 0:ZW]

        def seg(x, i):
            return x[:, OFF[i]:OFF[i] + S - i * P]

        def zpart(b0, i):
            return bank[:, b0 + OFF[i] // NC, OFF[i] % NC:OFF[i] % NC + S - i * P]

        def diagonals(x):
            return (x[:, 0:2 * NC].rearrange("p (j n) -> p j n", j=2)[:, :, 0:P],
                    x[:, OFF[3]:OFF[3] + 2 * P].rearrange("p (j n) -> p j n", j=2))
        below = const("lt").rearrange("p (o n) -> p o n", o=1).to_broadcast([P, 2, P])

        nsum = [1, 2, 3, 4]
        POOL_AT = 2
        dvl = [("z", 0), ("sp", 0), ("mask", 0, 0), ("mask", 0, 1)]
        acl = [("abs", 0), ("e", 0), ("l", 0)]
        pel = [("z", 0)]
        for it in range(SBH + 1):
            nxt, here = it + 1 < SBH, it < SBH
            dvl += ([("z", it + 1)] if nxt else []) + ([("t1", it), ("t2", it)] if here else [])
            dvl += [("sp", it + 1), ("mask", it + 1, 0), ("mask", it + 1, 1)] if nxt else []
            dvl += [("wmask", it, 0), ("wmask", it, 1)] if here else ["prec"] + [("sn", k) for k in range(4, 8)]
            dvl += [("o", it - 1)] if it else []
            acl += [("sq", (it - 3) // 2)] if it in (3, 5, 7) else []
            acl += [("abs", it + 1), ("e", it + 1), ("l", it + 1)] if nxt else []
            acl += [("w", it)] if here else ["psd"]
            acl += [("po", it - POOL_AT), ("sq", 4 + it - POOL_AT)] if 0 <= it - POOL_AT < 4 else []
            pel += ([("z", it + 1)] if nxt else []) + ([("a", it)] if here else []) + ([("o", it - 1)] if it else [])
            pel += [("pool", it - POOL_AT)] if 0 <= it - POOL_AT < 4 else []
            pel += ["psum"] if it == SBH - 1 else []
        dv = steps("dve", dvl + ["srec"] + [("sn", k) for k in range(4)])
        ac = steps("act", acl + [("sq", 3), "ssd"])
        pe = steps("pe", pel + ["ssum"])
        pool_labels = []
        for g in range(4):
            pool_labels += [("win", g, i) for i in range(nsum[g])] + [("mean", g), ("edge", g), ("less", g)]
        po = steps("pool", ["upad"] + pool_labels)
        with nc.Block() as block:
            @block.sync
            def _(sp):
                sp.dma_start(wpool, t["w_pool_2"][0].rearrange("g c e -> c g e")).then_inc(row_in, 16)
                for i in range(LEAST_LIVE, NBP, NT):
                    sp.dma_start(y_dram[i * P:(i + NT) * P, :].rearrange("(t p) d -> p t d", p=P), h[:, :, :])\
                      .then_inc(rows_filled, 16)
                sp.wait_ge(rows_filled, 16 * (NBP - LEAST_LIVE) // NT)

            @block.gpsimd
            def _(eng):
                eng.memset(uT[:, :, 0:PADU], 0.0).then_inc(pool_done, 1)
                prev = po["upad"]
                for g, win in enumerate(WINS):
                    src = uT[:, g, :]
                    step_ = 1
                    for i in range(nsum[g]):
                        dst = pl[i % 2]
                        lo = 2 * step_ - 1
                        eng.wait_ge(pool_done, prev)
                        eng.tensor_tensor(dst[:, lo:LU], src[:, lo:LU], src[:, lo - step_:LU - step_], ALU.add)\
                           .then_inc(pool_done, 1)
                        prev = po["win", g, i]
                        src = dst
                        step_ *= 2
                    dst = pooled[g]
                    eng.wait_ge(pool_done, prev)
                    eng.tensor_scalar(dst[:, PADU:S], src[:, 2 * PADU:LU], 1.0 / win, None, ALU.mult).then_inc(pool_done, 1)
                    eng.tensor_tensor(dst[:, 0:PADU], src[:, PADU:2 * PADU],
                                      const("rcount", g * PADU, (g + 1) * PADU), ALU.mult).then_inc(pool_done, 1)
                    eng.wait_ge(pool_done, po["edge", g])
                    eng.tensor_tensor(dst, dst, uT[:, g, PADU:LU], ALU.subtract).then_inc(pool_done, 1)
                    prev = po["less", g]

            @block.tensor
            def _(eng):
                def z_of(hd):
                    if hd:
                        eng.wait_ge(dve_done, dv["z", hd - 1])
                    r = hd % 2 * HD
                    for i in range(4):
                        mm = nc.tensor.matmul(zpart(ZBANK, i), qk[r:r + HD, 4 + hd // 2, i * P:(i + 1) * P],
                                              qk[r:r + HD, hd // 2, i * P:S], start=True, stop=True)
                    mm.then_inc(pe_done, 1)

                def sums_of(hd):
                    eng.wait_ge(dve_done, dv["mask", hd, 1])
                    if hd:
                        eng.wait_ge(dve_done, dv["t2", hd - 1])
                    for i in range(4):
                        for j in range(i, 4):
                            dst = zpart(ABANK, i)[:, (j - i) * P:]
                            mm = nc.tensor.matmul(dst, const("gt") if j == i else const("ones"), seg(sp_[hd % 2], j),
                                                  start=j == i, stop=j == 3, skip_group_check=True)
                    mm.then_inc(pe_done, 1)

                def result_of(hd):
                    eng.wait_ge(dve_done, dv["wmask", hd, 1])
                    if hd:
                        eng.wait_ge(dve_done, dv["o", hd - 1])
                    r = hd % 2 * HD
                    for i in range(4):
                        mm = nc.tensor.matmul(bank[r:r + HD, OBANK, i * P:S], v2[:, i, hd * HD:(hd + 1) * HD],
                                              seg(wt[hd % 2], i), start=i == 0, stop=i == 3, skip_group_check=True)
                    mm.then_inc(pe_done, 1)

                def squares(b, ks):
                    for k in ks:
                        eng.wait_ge(act_done, ac["sq", k])
                        mm = nc.tensor.matmul(bank[:, b, :], const("ones"), sqs[k], start=k % 4 == 0, stop=k % 4 == 3)
                    mm.then_inc(pe_done, 1)

                z_of(0)
                for it in range(SBH + 1):
                    if it + 1 < SBH:
                        z_of(it + 1)
                    if it < SBH:
                        sums_of(it)
                    if it:
                        result_of(it - 1)
                    g = it - POOL_AT
                    if 0 <= g < 4:
                        if g == 0:
                            eng.wait_ge(row_in, row_at)
                        else:
                            eng.wait_ge(act_done, ac["po", g - 1])
                        eng.wait_ge(pool_done, po["less", g])
                        nc.tensor.matmul(bank[:, GBANK, :], wpool[:, g, :], pooled[g], start=True, stop=True)\
                          .then_inc(pe_done, 1)
                    if it == SBH - 1:
                        squares(GBANK, range(4, 8))
                squares(ZBANK, range(4))

            @block.scalar
            def _(eng):
                def softplus(hd):
                    s = hd % 2
                    eng.wait_ge(dve_done, dv["z", hd])
                    if hd >= 2:
                        eng.wait_ge(pe_done, pe["a", hd - 2])
                    nc.scalar.activation(sp_[s], zs[s], ACT.Abs).then_inc(act_done, 1)
                    eng.wait_ge(act_done, ac["abs", hd])
                    nc.scalar.activation(sp_[s], sp_[s], ACT.Exp, scale=-1.0).then_inc(act_done, 1)
                    eng.wait_ge(act_done, ac["e", hd])
                    nc.scalar.activation(sp_[s], sp_[s], ACT.Ln, bias=const("ones", 0, 1)).then_inc(act_done, 1)

                def square(k):
                    if k < 4:
                        eng.wait_ge(pool_done, po["less", 3])
                        eng.wait_ge(dve_done, dv["o", 2 * k + 1])
                    else:
                        eng.wait_ge(act_done, ac["po", k - 4])
                    nc.scalar.activation(sqs[k], mixT[:, k, :], ACT.Square).then_inc(act_done, 1)

                def deviation(n, b, name):
                    eng.wait_ge(pe_done, pe[name])
                    if n == 0:
                        eng.wait_ge(pe_done, pe["o", SBH - 1])
                    dst = v2[:, 0, :] if n == 0 else qk[:, 0, :]
                    nc.scalar.activation(dst, bank[:, b, :], ACT.Sqrt, scale=1.0 / S,
                                         bias=const("eps", 1, 2)).then_inc(act_done, 1)

                softplus(0)
                for it in range(SBH + 1):
                    if it in (3, 5, 7):
                        square((it - 3) // 2)
                    if it + 1 < SBH:
                        softplus(it + 1)
                    if it < SBH:
                        eng.wait_ge(dve_done, dv["t2", it])
                        nc.scalar.activation(wt[it % 2], wt[it % 2], ACT.Exp).then_inc(act_done, 1)
                    else:
                        deviation(1, GBANK, "psum")
                    g = it - POOL_AT
                    if 0 <= g < 4:
                        eng.wait_ge(pe_done, pe["pool", g])
                        nc.scalar.activation(mixT[:, 4 + g, :], bank[:, GBANK, :], ACT.Copy,
                                             scale=param("pool_scale", g, g + 1)).then_inc(act_done, 1)
                        square(4 + g)
                square(3)
                deviation(0, ZBANK, "ssum")

            @block.vector
            def _(eng):
                def logits(hd):
                    eng.wait_ge(pe_done, pe["z", hd])
                    if hd >= 2:
                        eng.wait_ge(dve_done, dv["t1", hd - 2])
                    nc.vector.tensor_copy(zs[hd % 2], flat(ZBANK)).then_inc(dve_done, 1)

                def mask(x):
                    for d in diagonals(x):
                        nc.vector.tensor_tensor(d, d, below, ALU.mult).then_inc(dve_done, 1)

                def softplus(hd):
                    s = hd % 2
                    eng.wait_ge(act_done, ac["l", hd])
                    eng.wait_ge(dve_done, dv["z", hd])
                    nc.vector.scalar_tensor_tensor(out=sp_[s], in0=zs[s], scalar=0.0, in1=sp_[s],
                                                   op0=ALU.max, op1=ALU.add).then_inc(dve_done, 1)
                    eng.wait_ge(dve_done, dv["sp", hd])
                    mask(sp_[s])

                def normed(ks, recip, dev):
                    for k in ks:
                        eng.wait_ge(dve_done, dv[recip])
                        g = param("g_sb", k, k + 1) if k < 4 else param("g_pool", k - 4, k - 3)
                        nc.vector.scalar_tensor_tensor(out=mixT[:, k, :], in0=mixT[:, k, :], scalar=g, in1=dev,
                                                       op0=ALU.mult, op1=ALU.mult).then_inc(dve_done, 1)

                logits(0)
                softplus(0)
                for it in range(SBH + 1):
                    s = it % 2
                    if it + 1 < SBH:
                        logits(it + 1)
                    if it < SBH:
                        eng.wait_ge(dve_done, dv["mask", it, 1])
                        if it >= 2:
                            eng.wait_ge(pe_done, pe["o", it - 2])
                        nc.vector.tensor_tensor(wt[s], zs[s], sp_[s], ALU.subtract).then_inc(dve_done, 1)
                        eng.wait_ge(dve_done, dv["t1", it])
                        eng.wait_ge(pe_done, pe["a", it])
                        nc.vector.tensor_tensor(wt[s], wt[s], flat(ABANK), ALU.subtract).then_inc(dve_done, 1)
                    if it + 1 < SBH:
                        softplus(it + 1)
                    if it < SBH:
                        eng.wait_ge(act_done, ac["w", it])
                        mask(wt[s])
                    else:
                        eng.wait_ge(act_done, ac["psd"])
                        nc.vector.reciprocal(qk[:, 0, :], qk[:, 0, :]).then_inc(dve_done, 1)
                        normed(range(4, 8), "prec", qk[:, 0, :])
                    if it:
                        hd = it - 1
                        eng.wait_ge(pe_done, pe["o", hd])
                        r = hd % 2 * HD
                        nc.vector.tensor_copy(mixT[r:r + HD, hd // 2, :], bank[r:r + HD, OBANK, :]).then_inc(dve_done, 1)
                eng.wait_ge(act_done, ac["ssd"])
                nc.vector.reciprocal(v2[:, 0, :], v2[:, 0, :]).then_inc(dve_done, 1)
                normed(range(4), "srec", v2[:, 0, :])

        project_into_h(C_OUT2, mixT)

        mem = region(0, TM * D).rearrange("p (t d) -> p t d", t=TM)
        memT = region(2048, KD * NMEM).rearrange("p (k m) -> p k m", k=KD)
        kmT = region(4096, KD * NMEM).rearrange("p (k m) -> p k m", k=KD)
        vm = region(6144, TM * D).rearrange("p (t d) -> p t d", t=TM)
        qm = region(8192, KD * S).rearrange("p (k s) -> p k s", k=KD)
        prob = region(12288, NT * MH * NMEM).rearrange("p (t h m) -> p t h m", t=NT, h=MH)
        at["late"] += 16
        mem_at = at["late"]
        with nc.Block() as block:
            @block.sync
            def _(sp):
                sp.dma_start(mem[:, :, :], t["mem_2"][0].rearrange("(t p) d -> p t d", p=P)).then_inc(late_in, 16)
                sp.wait_ge(late_in, mem_at)
        normalise(mem, TM, 1, param("g_mem_kv"), tok, memT)
        jobs = []
        for c in range(8):
            jobs.append(t_job(C_KV + c // 4, c % 4 * P, memT, NMEM, "act",
                              lambda b, c=c: nc.scalar.activation(kmT[:, c, :], bank[:, b, 0:NMEM], ACT.Copy)))
        for n in range(2):
            for mt in range(TM):
                jobs.append(tok_job(C_KV + 2 + n, 0, NC, memT, mt, "dve",
                                    lambda b, mt=mt, n=n: nc.vector.tensor_copy(vm[:, mt, n * NC:(n + 1) * NC], bank[:, b, :])))
        dense(jobs)
        normalise(h, NT, 1, param("g_mem_q"), tok, aT)
        dense([t_job(C_MQ + c // 4, c % 4 * P, aT, S, "act" if c % 2 else "dve",
                     (lambda b, c=c: nc.scalar.activation(qm[:, c, :], bank[:, b, :], ACT.Copy)) if c % 2 else
                     (lambda b, c=c: nc.vector.tensor_copy(qm[:, c, :], bank[:, b, :]))) for c in range(8)])

        dh = D // MH
        SCALE = dh ** -0.5
        units = [(tt, half) for tt in range(NT) for half in range(2)]
        pTt = aT[:, :, :].rearrange("p (h m) s -> p h m s", h=MH)
        mx, nmx, rs, ri = stat[:, 0:16], stat[:, 16:32], stat[:, 32:48], stat[:, 48:64]
        pe = steps("pe", [("s", u) for u in range(8)] + [("t", hd, mt) for hd in range(MH) for mt in range(TM)]
                   + [("o", c) for c in range(8)])
        dv = steps("dve", [x for u in range(8) for x in (("max", u), ("neg", u))] + ["rec"]
                   + [("p", u) for u in range(8)] + [("t", k) for k in range(0, 8, 2)] + [("o", c) for c in range(0, 8, 2)])
        ac = steps("act", [("e", u, j) for u in range(8) for j in range(2)]
                   + [("t", k) for k in range(1, 8, 2)] + [("o", c) for c in range(1, 8, 2)])
        with nc.Block() as block:
            @block.tensor
            def _(eng):
                for u, (tt, half) in enumerate(units):
                    for j in range(2):
                        hd = 2 * half + j
                        for k in range(2):
                            mm = nc.tensor.matmul(bank[:, u, j * NMEM:(j + 1) * NMEM],
                                                  qm[:, 2 * hd + k, tt * P:(tt + 1) * P], kmT[:, 2 * hd + k, :],
                                                  start=k == 0, stop=k == 1)
                    mm.then_inc(pe_done, 1)
                for hd in range(MH):
                    for mt in range(TM):
                        b = hd * TM + mt
                        for tt in range(NT):
                            eng.wait_ge(dve_done, dv["p", 7])
                            mm = nc.tensor.transpose(bank[:, b, tt * P:(tt + 1) * P], prob[:, tt, hd, mt * P:(mt + 1) * P], ident)
                        mm.then_inc(pe_done, 1)
                for c in range(8):
                    hd = c // 2
                    for mt in range(TM):
                        k = hd * TM + mt
                        eng.wait_ge(*((dve_done, dv["t", k]) if k % 2 == 0 else (act_done, ac["t", k])))
                    if c % 2 == 0:
                        eng.wait_ge(dve_done, dv["t", c])
                    else:
                        eng.wait_ge(act_done, ac["t", c])
                    for mt in range(TM):
                        mm = nc.tensor.matmul(bank[:, c, :], vm[:, mt, c * P:(c + 1) * P], pTt[:, hd, mt, :],
                                              start=mt == 0, stop=mt == TM - 1)
                    mm.then_inc(pe_done, 1)

            @block.vector
            def _(eng):
                for u, (tt, half) in enumerate(units):
                    eng.wait_ge(pe_done, pe["s", u])
                    nc.vector.tensor_reduce(mx[:, 2 * u:2 * u + 2], bank[:, u, :].rearrange("p (j m) -> p j m", j=2),
                                            AX, ALU.max).then_inc(dve_done, 1)
                    eng.wait_ge(dve_done, dv["max", u])
                    nc.vector.tensor_scalar(nmx[:, 2 * u:2 * u + 2], mx[:, 2 * u:2 * u + 2], -SCALE, None, ALU.mult)\
                      .then_inc(dve_done, 1)
                eng.wait_ge(act_done, ac["e", 7, 1])
                nc.vector.reciprocal(ri, rs).then_inc(dve_done, 1)
                eng.wait_ge(dve_done, dv["rec"])
                for u, (tt, half) in enumerate(units):
                    pr = prob[:, tt, 2 * half:2 * half + 2, :]
                    nc.vector.tensor_tensor(pr, pr, over(ri[:, 2 * u:2 * u + 2], NMEM), ALU.mult).then_inc(dve_done, 1)
                for k in range(0, 8, 2):
                    eng.wait_ge(pe_done, pe["t", k // TM, k % TM])
                    nc.vector.tensor_copy(pTt[:, k // TM, k % TM, :], bank[:, k, :]).then_inc(dve_done, 1)
                for c in range(0, 8, 2):
                    eng.wait_ge(pe_done, pe["o", c])
                    nc.vector.tensor_copy(mixT[:, c, :], bank[:, c, :]).then_inc(dve_done, 1)

            @block.scalar
            def _(eng):
                for u, (tt, half) in enumerate(units):
                    eng.wait_ge(dve_done, dv["neg", u])
                    for j in range(2):
                        nc.scalar.activation(prob[:, tt, 2 * half + j, :], bank[:, u, j * NMEM:(j + 1) * NMEM], ACT.Exp,
                                             scale=SCALE, bias=nmx[:, 2 * u + j:2 * u + j + 1],
                                             accum_out=rs[:, 2 * u + j:2 * u + j + 1]).then_inc(act_done, 1)
                for k in range(1, 8, 2):
                    eng.wait_ge(pe_done, pe["t", k // TM, k % TM])
                    nc.scalar.activation(pTt[:, k // TM, k % TM, :], bank[:, k, :], ACT.Copy).then_inc(act_done, 1)
                for c in range(1, 8, 2):
                    eng.wait_ge(pe_done, pe["o", c])
                    nc.scalar.activation(mixT[:, c, :], bank[:, c, :], ACT.Copy).then_inc(act_done, 1)

        project_into_h(C_MO, mixT)

        o = 0
        wr = region(o, KD * NE).rearrange("p (k e) -> p k e", k=KD)
        o += KD * NE
        br = region(o, NE)
        o += NE
        bexp = X[0:3 * NE, o:o + 3 * D]
        o += 3 * D
        at["late"] += 48 + 32
        r_at = at["late"]

        def router_loads(sp):
            sp.dma_start(wr[:, :, :], t["w_router_2"][0].rearrange("(k p) e -> p k e", p=P)).then_inc(late_in, 16)
            sp.dma_start(br[:, :], t["b_router_2"][0:1, :].to_broadcast([P, NE])).then_inc(late_in, 16)
            for i in range(3):
                sp.dma_start(bexp[i * NE:(i + 1) * NE, :], t["b_expert"][:, :]).then_inc(late_in, 16)
        normalise(h, NT, 1, None, tok, aT, row=grow, row_ap=t["g_ffn_2"][0:1, :], sp_work=router_loads)

        lg = region(o, NT * NE).rearrange("p (t e) -> p t e", t=NT)
        o += NT * NE
        tv = region(o, NT * 8).rearrange("p (t k) -> p t k", t=NT)
        o += NT * 8
        ti = region(o, NT * 8).bitcast(U32).rearrange("p (t k) -> p t k", t=NT)
        o += NT * 8
        tf = region(o, NT * 8).rearrange("p (t k) -> p t k", t=NT)
        o += NT * 8
        oh = region(o, NT * EK * NE).rearrange("p (t k e) -> p t k e", t=NT, k=EK)
        o += NT * EK * NE
        oh2 = region(o, NT * EK * NE).rearrange("p (t k e) -> p t k e", t=NT, k=EK)
        o += NT * EK * NE
        M = region(o, NT * NE).rearrange("p (t e) -> p t e", t=NT)
        o += NT * NE
        R = region(o, NT * NE)
        o += NT * NE
        q4 = region(o, NT * NE)
        o += NT * NE
        tq = region(o, NT * NE)
        o += NT * NE
        am = region(o, NT * NE)
        o += NT * NE
        ay = region(o, NT * NE)
        o += NT * NE
        nb = region(o, NE)
        o += NE
        nb2 = region(o, NE)
        o += NE
        bend = region(o, NE)
        o += NE
        bst = region(o, NE)
        o += NE
        cmpb = region(o, NBP * NE).rearrange("p (b e) -> p b e", b=NBP)
        o += NBP * NE
        bh = region(o, 3 * D // 2).bitcast(BF16)[0:3 * NE, :]
        o += 3 * D // 2
        assert o <= 4 * KD * NC
        gk = sb("gk", [P, NT * EK])
        smap = sb("smap", [P, NT * EK], I32)
        srow = sb("srow", [P, NT * EK], I32)
        blkf = sb("blkf", [P, NBP])
        blki = sb("blki", [P, NBP], I32)
        live = sb("live", [P, 1], I32)
        tki = sb("tki", [P, NT], I32)
        slots = sb("slots", [P, NBP], I32)
        b3 = sb("b3", [3 * NE, 3 * D], BF16)
        zero_i = slots

        def bc(x, shape):
            return x.to_broadcast(shape)

        dvl = ["lg"] + [("mx", i) for i in range(NT)] + [("ix", i) for i in range(NT)] + ["tf", "tsub"]
        dvl += ["esum", "erec", "gk"] + [("oh", i) for i in range(NT)] + ["M"]
        dvl += ["nb0", "nb1", "nb2", "nb3", "bend", "bst", "live", "cmp", "blkf", "blkm", "blki"]
        dvl += ["R", "q1", "q2", "q2a", "q3", "q3a", "p", "bq", "am", "ay"]
        dvl += ["selm", "fmap", "smap", "sely", "frow", "srow", "tki", "zero"]
        dvl += ["hi", "r1", "mid", "r2", "lo", "midc"]
        dv = steps("dve", dvl)
        ac = steps("act", ["exp"])
        pe = steps("pe", ["lg", "rank", "cnt"])
        ws = [wring[i][:, :] for i in range(4)] + [region(0, KD * NC), region(KD * NC, KD * NC)]
        w1s = [w.rearrange("p (k n) -> p k n", k=KD) for w in ws[0:4]]
        w2s = [w.rearrange("p (k n) -> p k n", k=4) for w in ws[4:6]]
        o = 2 * KD * NC
        xg = region(o, D)
        gsb_ = region(o + D, D)
        usb = region(o + 2 * D, D)
        act_ = region(o + 3 * D, D)
        ysb = region(o + 4 * D, D)
        ohb = X[0:3 * NE, o + 5 * D:o + 5 * D + P // 2].bitcast(BF16)
        curs = region(o + 5 * D + P, 1).bitcast(I32)
        xT = aT[:, 0:2, :].rearrange("p k s -> p (k s)").rearrange("p (k m) -> p k m", k=KD)
        hT = aT[:, 2:4, :].rearrange("p k s -> p (k s)").rearrange("p (k m) -> p k m", k=KD)
        w1_in = [sem(f"w1_in{i}") for i in range(4)]
        w2_in = [sem(f"w2_in{i}") for i in range(2)]
        rows_in = sem("rows_in")
        curs_ready = sem("curs_ready")
        x_t = sem("x_t")
        x_e = sem("x_e")
        oh_ready = sem("oh_ready")
        gu_done = sem("gu_done")
        gate_ok = sem("gate_ok")
        up_ok = sem("up_ok")
        sig_ok = sem("sig_ok")
        mul_ok = sem("mul_ok")
        act_ok = sem("act_ok")
        h_t = sem("h_t")
        h_e = sem("h_e")
        y_done = sem("y_done")
        y_out = sem("y_out")
        y_st = sem("y_st")
        all_stored = sem("all_stored")
        we1, we2 = t["w_expert_in_2"][0], t["w_expert_out_2"][0]
        GU = [0, 2 * 512, 512, 3 * 512]
        HB, GB, YB = 0, 2, 6


        def load_w1(sp, e, c):
            sp.dma_start(w1s[c], we1[bass.ds(e, 1), :, GU[c]:GU[c] + NC]
                         .rearrange("o (k p) n -> p (o k) n", p=P)).then_inc(w1_in[c], 16)

        def load_w2(sp, e, c):
            sp.dma_start(w2s[c], we2[bass.ds(e, 1), c * NC:(c + 1) * NC, :]
                         .rearrange("o (k p) n -> p (o k) n", p=P)).then_inc(w2_in[c], 16)

        map_zero, map_set, rows_out, map_in = sem("map_zero"), sem("map_set"), sem("rows_out"), sem("map_in")
        with nc.Block() as block:
            @block.sync
            def _(sp):
                sp.dma_start(xn_dram.rearrange("(t p) d -> p t d", p=P), tok[:, :, :]).then_inc(rows_out, 16)
                sp.wait_ge(dve_done, dv["zero"])
                sp.dma_start(tokmap_dram.rearrange("(p b) o -> p (b o)", p=P), zero_i[:, :]).then_inc(map_zero, 16)
                sp.wait_ge(dve_done, dv["blki"])
                e = sp.value_load(blki[0:1, 0:1], min_val=0, max_val=NE - 1)
                for c in range(4):
                    load_w1(sp, e, c)
                sp.wait_ge(map_set, 16 * NT * EK)
                sp.dma_start(slots[:, :], tokmap_dram.rearrange("(p b) o -> p (b o)", p=P)).then_inc(map_in, 16)
                sp.wait_ge(map_in, 16)
                sp.wait_ge(rows_out, 16)

            @block.tensor
            def _(eng):
                eng.wait_ge(late_in, r_at)
                for tt in range(NT):
                    for k in range(KD):
                        mm = nc.tensor.matmul(bank[:, 0, tt * NE:(tt + 1) * NE], aT[:, k, tt * P:(tt + 1) * P], wr[:, k, :],
                                              start=k == 0, stop=k == KD - 1)
                mm.then_inc(pe_done, 1)
                eng.wait_ge(dve_done, dv["M"])
                for tt in range(NT):
                    for j in range(tt + 1):
                        mm = nc.tensor.matmul(bank[:, 1, tt * NE:(tt + 1) * NE], const("lt") if j == tt else const("ones"),
                                              M[:, j, :], start=j == 0, stop=j == tt)
                mm.then_inc(pe_done, 1)
                for j in range(NT):
                    mm = nc.tensor.matmul(bank[:, 2, 0:NE], const("ones"), M[:, j, :], start=j == 0, stop=j == NT - 1)
                mm.then_inc(pe_done, 1)

            @block.scalar
            def _(eng):
                eng.wait_ge(dve_done, dv["tsub"])
                nc.scalar.activation(tv[:, :, EK:2 * EK], tv[:, :, EK:2 * EK], ACT.Exp).then_inc(act_done, 1)

            @block.vector
            def _(eng):
                eng.wait_ge(late_in, r_at)
                eng.wait_ge(pe_done, pe["lg"])
                nc.vector.tensor_tensor(lg, bank[:, 0, 0:NT * NE].rearrange("p (t e) -> p t e", t=NT),
                                        over_t(br[:, :]), ALU.add).then_inc(dve_done, 1)
                eng.wait_ge(dve_done, dv["lg"])
                for i in range(NT):
                    nc.vector.max(tv[:, i, :], lg[:, i, :]).then_inc(dve_done, 1)
                for i in range(NT):
                    eng.wait_ge(dve_done, dv["mx", i])
                    nc.vector.max_index(ti[:, i, :], tv[:, i, :], lg[:, i, :]).then_inc(dve_done, 1)
                eng.wait_ge(dve_done, dv["ix", NT - 1])
                nc.vector.tensor_copy(tf, ti).then_inc(dve_done, 1)
                nc.vector.tensor_tensor(tv[:, :, EK:2 * EK], tv[:, :, 0:EK], bc(tv[:, :, 0:1], [P, NT, EK]), ALU.subtract)\
                  .then_inc(dve_done, 1)
                eng.wait_ge(act_done, ac["exp"])
                nc.vector.tensor_reduce(nb[:, 0:NT], tv[:, :, EK:2 * EK], AX, ALU.add).then_inc(dve_done, 1)
                eng.wait_ge(dve_done, dv["esum"])
                nc.vector.reciprocal(nb[:, 4:4 + NT], nb[:, 0:NT]).then_inc(dve_done, 1)
                eng.wait_ge(dve_done, dv["erec"])
                nc.vector.tensor_tensor(gk[:, :].rearrange("p (t k) -> p t k", t=NT), tv[:, :, EK:2 * EK],
                                        over(nb[:, 4:4 + NT], EK), ALU.mult).then_inc(dve_done, 1)
                for i in range(NT):
                    nc.vector.tensor_tensor(oh[:, i, :, :], over(tf[:, i, 0:EK], NE),
                                            over_t(const("iota", 0, NE)), ALU.is_equal).then_inc(dve_done, 1)
                eng.wait_ge(dve_done, dv["oh", NT - 1])
                nc.vector.tensor_reduce(M, oh.rearrange("p t k e -> p t e k"), AX, ALU.add).then_inc(dve_done, 1)
                eng.wait_ge(pe_done, pe["cnt"])
                cnt = bank[:, 2, 0:NE]
                nc.vector.tensor_scalar(nb, cnt, 0.0, None, ALU.is_gt).then_inc(dve_done, 1)
                prev, a, b = "nb0", nb, nb2
                for j in range(1, 4):
                    eng.wait_ge(dve_done, dv[prev])
                    nc.vector.scalar_tensor_tensor(out=b, in0=cnt, scalar=float(P * j), in1=a, op0=ALU.is_gt, op1=ALU.add)\
                      .then_inc(dve_done, 1)
                    prev, a, b = f"nb{j}", b, a
                eng.wait_ge(dve_done, dv["nb3"])
                nc.vector.tensor_tensor_scan(out=bend, data0=const("ones", 0, NE), data1=a, initial=0.0,
                                             op0=ALU.mult, op1=ALU.add).then_inc(dve_done, 1)
                eng.wait_ge(dve_done, dv["bend"])
                nc.vector.tensor_tensor(bst, bend, a, ALU.subtract).then_inc(dve_done, 1)
                nc.vector.tensor_copy(live[:, :], bend[:, NE - 1:NE]).then_inc(dve_done, 1)
                nc.vector.tensor_tensor(cmpb, bend.rearrange("p (o e) -> p o e", o=1).to_broadcast([P, NBP, NE]),
                                        over(const("iota"), NE), ALU.is_le).then_inc(dve_done, 1)
                eng.wait_ge(dve_done, dv["cmp"])
                nc.vector.tensor_reduce(blkf[:, :], cmpb, AX, ALU.add).then_inc(dve_done, 1)
                eng.wait_ge(dve_done, dv["blkf"])
                nc.vector.tensor_scalar(blkf[:, :], blkf[:, :], float(NE - 1), None, ALU.min).then_inc(dve_done, 1)
                eng.wait_ge(dve_done, dv["blkm"])
                nc.vector.tensor_copy(blki[:, :], blkf[:, :]).then_inc(dve_done, 1)
                nc.vector.tensor_copy(R, bank[:, 1, 0:NT * NE]).then_inc(dve_done, 1)
                eng.wait_ge(dve_done, dv["R"])
                nc.vector.tensor_scalar(q4, R, float(P), None, ALU.is_ge).then_inc(dve_done, 1)
                eng.wait_ge(dve_done, dv["q1"])
                nc.vector.tensor_scalar(tq, R, float(2 * P), None, ALU.is_ge).then_inc(dve_done, 1)
                eng.wait_ge(dve_done, dv["q2"])
                nc.vector.tensor_tensor(q4, q4, tq, ALU.add).then_inc(dve_done, 1)
                eng.wait_ge(dve_done, dv["q2a"])
                nc.vector.tensor_scalar(tq, R, float(3 * P), None, ALU.is_ge).then_inc(dve_done, 1)
                eng.wait_ge(dve_done, dv["q3"])
                nc.vector.tensor_tensor(q4, q4, tq, ALU.add).then_inc(dve_done, 1)
                eng.wait_ge(dve_done, dv["q3a"])
                nc.vector.scalar_tensor_tensor(out=R, in0=q4, scalar=float(-P), in1=R, op0=ALU.mult, op1=ALU.add)\
                  .then_inc(dve_done, 1)
                nc.vector.tensor_tensor(q4.rearrange("p (t e) -> p t e", t=NT), q4.rearrange("p (t e) -> p t e", t=NT),
                                        over_t(bst), ALU.add).then_inc(dve_done, 1)
                eng.wait_ge(dve_done, dv["bq"])
                nc.vector.scalar_tensor_tensor(out=am, in0=R, scalar=float(NBP), in1=q4, op0=ALU.mult, op1=ALU.add)\
                  .then_inc(dve_done, 1)
                nc.vector.scalar_tensor_tensor(out=ay, in0=q4, scalar=float(P), in1=R, op0=ALU.mult, op1=ALU.add)\
                  .then_inc(dve_done, 1)
                eng.wait_ge(dve_done, dv["ay"])
                for src, dst, n, (l1, l2) in ((am, smap, 0, ("selm", "fmap")), (ay, srow, 1, ("sely", "frow"))):
                    s3 = src.rearrange("p (t o e) -> p t o e", t=NT, o=1).to_broadcast([P, NT, EK, NE])
                    if n:
                        eng.wait_ge(dve_done, dv["fmap"])
                    nc.vector.tensor_tensor(oh2, oh, s3, ALU.mult).then_inc(dve_done, 1)
                    eng.wait_ge(dve_done, dv[l1])
                    f = stat[:, n * 16:(n + 1) * 16]
                    nc.vector.tensor_reduce(f, oh2.rearrange("p t k e -> p (t k) e"), AX, ALU.add).then_inc(dve_done, 1)
                    eng.wait_ge(dve_done, dv[l2])
                    nc.vector.tensor_copy(dst[:, :], f).then_inc(dve_done, 1)
                nc.vector.tensor_copy(tki[:, :], const("tok")).then_inc(dve_done, 1)
                nc.vector.memset(zero_i[:, :], 0).then_inc(dve_done, 1)
                B = bexp
                nc.vector.tensor_copy(b3[:, :], B).then_inc(dve_done, 1)
                eng.wait_ge(dve_done, dv["hi"])
                nc.vector.tensor_tensor(B, B, b3[:, :], ALU.subtract).then_inc(dve_done, 1)
                eng.wait_ge(dve_done, dv["r1"])
                nc.vector.tensor_copy(bh, B).then_inc(dve_done, 1)
                eng.wait_ge(dve_done, dv["mid"])
                nc.vector.tensor_tensor(B, B, bh, ALU.subtract).then_inc(dve_done, 1)
                eng.wait_ge(dve_done, dv["r2"])
                nc.vector.tensor_copy(b3[2 * NE:3 * NE, :], B[2 * NE:3 * NE, :]).then_inc(dve_done, 1)
                nc.vector.tensor_copy(b3[NE:2 * NE, :], bh[NE:2 * NE, :]).then_inc(dve_done, 1)

            @block.gpsimd
            def _(eng):
                eng.wait_ge(map_zero, 16)
                eng.wait_ge(dve_done, dv["zero"])
                for j in range(NT * EK):
                    eng.indirect_dma_start(tokmap_dram, bass.IndirectOffsetOnAxis(ap=smap[:, j:j + 1], axis=0),
                                           tki[:, j // EK:j // EK + 1], None).then_inc(map_set, 16)
                eng.wait_ge(map_set, 16 * NT * EK)

        def each_block(eng, body, ahead=0):
            n = eng.value_load(live[0:1, 0:1], min_val=1, max_val=NBLK)
            with eng.Fori(0, NBLK - ahead) as b:
                with eng.If(b + ahead < n):
                    body(b)
                with eng.Else():
                    eng.nop()
            return n

        with nc.Block() as block:
            @block.sync
            def _(eng):
                e = eng.value_load(blki[0:1, 0:1], min_val=0, max_val=NE - 1)
                for c in range(2):
                    load_w2(eng, e, c)

                def body(b):
                    e = eng.value_load(blki[0:1, bass.ds(b + 1, 1)], min_val=0, max_val=NE - 1)
                    for c in range(4):
                        eng.wait_ge(gu_done, b * 4 + (c + 1))
                        load_w1(eng, e, c)
                    for c in range(2):
                        eng.wait_ge(y_done, b * 2 + (c + 1))
                        load_w2(eng, e, c)
                each_block(eng, body, ahead=1)

            @block.gpsimd
            def _(eng):
                def gather(col, turn):
                    eng.tensor_copy(curs, slots[:, col]).then_inc(curs_ready, 1)
                    eng.wait_ge(curs_ready, turn)
                    eng.sem_inc(pool_turn, 1)
                    eng.indirect_dma_start(xg, None, xn_dram, bass.IndirectOffsetOnAxis(ap=curs, axis=0))\
                       .then_inc(rows_in, 16)
                gather(slice(0, 1), 1)

                def body(b):
                    eng.wait_ge(x_t, b * 2 + 2)
                    eng.sem_inc(pool_turn, 1)
                    gather(bass.ds(b + 1, 1), b + 2)
                each_block(eng, body)

            @block.tensor
            def _(eng):
                def transpose_rows():
                    for half in range(2):
                        for k in range(4):
                            kk = half * 4 + k
                            mm = nc.tensor.transpose(bank[:, GB + half, k * P:(k + 1) * P], xg[:, kk * P:(kk + 1) * P], ident)
                        mm.then_inc(x_t, 1)

                def transpose_act(half):
                    for k in range(4):
                        kk = half * 4 + k
                        mm = nc.tensor.transpose(bank[:, HB + half, k * P:(k + 1) * P], act_[:, kk * P:(kk + 1) * P], ident)
                    mm.then_inc(h_t, 1)

                def down(half, ks):
                    for k in ks:
                        for n in range(2):
                            mm = nc.tensor.matmul(bank[:, YB + n, :], hT[:, half * 4 + k, :],
                                                  w2s[half][:, k, n * NC:(n + 1) * NC], start=False,
                                                  stop=half == 1 and k == 3, skip_group_check=True)
                    return mm

                eng.wait_ge(rows_in, 16)
                transpose_rows()

                def body(b):
                    for c in range(4):
                        eng.wait_ge(w1_in[c], b * 16 + 16)
                        if c == 0:
                            eng.wait_ge(x_e, b * 2 + 2)
                        for k in range(KD):
                            nc.tensor.matmul(bank[:, GB + c, :], xT[:, k, :], w1s[c][:, k, :], start=k == 0, stop=False)
                        if c == 0:
                            eng.wait_ge(oh_ready, b + 1)
                        nc.tensor.matmul(bank[:, GB + c, :], ohb, b3[:, GU[c]:GU[c] + NC],
                                         start=False, stop=True).then_inc(gu_done, 1)
                        if c == 2:
                            eng.wait_ge(act_ok, b * 2 + 1)
                            transpose_act(0)
                    eng.wait_ge(rows_in, b * 16 + 32)
                    transpose_rows()
                    eng.wait_ge(y_out, b * 2 + 2)
                    for n in range(2):
                        nc.tensor.matmul(bank[:, YB + n, :], ohb, b3[:, 2 * FF + n * NC:2 * FF + (n + 1) * NC],
                                         start=True, stop=False, skip_group_check=True)
                    eng.wait_ge(h_e, b * 2 + 1)
                    eng.wait_ge(w2_in[0], b * 16 + 16)
                    down(0, (0, 1))
                    eng.wait_ge(act_ok, b * 2 + 2)
                    transpose_act(1)
                    down(0, (2, 3)).then_inc(y_done, 1)
                    eng.wait_ge(h_e, b * 2 + 2)
                    eng.wait_ge(w2_in[1], b * 16 + 16)
                    down(1, range(4)).then_inc(y_done, 1)
                each_block(eng, body)

            @block.scalar
            def _(eng):
                eng.sem_inc(y_out, 1)

                def copy_rows(count):
                    eng.wait_ge(x_t, count)
                    nc.scalar.activation(xT[:, 4:8, :], bank[:, GB + 1, :].rearrange("p (k m) -> p k m", k=4), ACT.Copy)\
                      .then_inc(x_e, 1)
                copy_rows(2)

                def body(b):
                    for half in range(2):
                        eng.wait_ge(gate_ok, b * 2 + half + 1)
                        nc.scalar.activation(act_[:, half * NC:(half + 1) * NC], gsb_[:, half * NC:(half + 1) * NC],
                                             ACT.Sigmoid, scale=1.702).then_inc(sig_ok, 1)
                        if half:
                            copy_rows(b * 2 + 4)
                        eng.wait_ge(h_t, b * 2 + half + 1)
                        nc.scalar.activation(hT[:, half * 4:half * 4 + 4, :],
                                             bank[:, HB + half, :].rearrange("p (k m) -> p k m", k=4), ACT.Copy).then_inc(h_e, 1)
                    eng.wait_ge(y_done, b * 2 + 2)
                    eng.wait_ge(y_st, b * 16 + 16)
                    nc.scalar.activation(ysb[:, 0:NC], bank[:, YB, :], ACT.Copy).then_inc(y_out, 1)
                    eng.wait_ge(y_out, b * 2 + 4)
                    eng.dma_start(y_dram[bass.ds(b * P, P), :], ysb).then_inc(y_st, 16)
                n = each_block(eng, body)
                eng.wait_ge(y_st, n * 16 + 16)
                eng.sem_inc(all_stored, 1)

            @block.vector
            def _(eng):
                eng.sem_inc(y_out, 1)
                eng.sem_inc(y_st, 16)

                def pick(col):
                    nc.vector.tensor_scalar(ohb, cst[0:3 * NE, _C["emod"][0]:_C["emod"][0] + P],
                                            blkf[0:3 * NE, col], None, ALU.is_equal).then_inc(oh_ready, 1)

                def copy_rows(count):
                    eng.wait_ge(x_t, count)
                    nc.vector.tensor_copy(xT[:, 0:4, :], bank[:, GB, :].rearrange("p (k m) -> p k m", k=4)).then_inc(x_e, 1)
                pick(slice(0, 1))
                copy_rows(1)

                def body(b):
                    for half in range(2):
                        lo, hi = half * NC, (half + 1) * NC
                        eng.wait_ge(gu_done, b * 4 + 2 * half + 1)
                        nc.vector.tensor_scalar(gsb_[:, lo:hi], bank[:, GB + 2 * half, :], 7.0, None, ALU.min).then_inc(gate_ok, 1)
                        eng.wait_ge(gu_done, b * 4 + 2 * half + 2)
                        nc.vector.tensor_scalar(usb[:, lo:hi], bank[:, GB + 2 * half + 1, :], 7.0, -7.0, ALU.min, ALU.max)\
                          .then_inc(up_ok, 1)
                        eng.wait_ge(up_ok, b * 2 + half + 1)
                        nc.vector.scalar_tensor_tensor(out=usb[:, lo:hi], in0=usb[:, lo:hi], scalar=1.0, in1=gsb_[:, lo:hi],
                                                       op0=ALU.add, op1=ALU.mult).then_inc(mul_ok, 1)
                        eng.wait_ge(mul_ok, b * 2 + half + 1)
                        eng.wait_ge(sig_ok, b * 2 + half + 1)
                        nc.vector.tensor_tensor(act_[:, lo:hi], act_[:, lo:hi], usb[:, lo:hi], ALU.mult).then_inc(act_ok, 1)
                    copy_rows(b * 2 + 3)
                    eng.wait_ge(y_done, b * 2 + 2)
                    pick(bass.ds(b + 1, 1))
                    eng.wait_ge(y_st, b * 16 + 16)
                    nc.vector.tensor_copy(ysb[:, NC:D], bank[:, YB + 1, :]).then_inc(y_out, 1)
                each_block(eng, body)

        got = [region(j * D, D) for j in range(8)]
        got_in = [sem(f"got_in{j}") for j in range(8)]
        dv = steps("dve", [(k, tt) for k in range(EK) for tt in range(NT)])
        with nc.Block() as block:
            @block.gpsimd
            def _(eng):
                for n in range(NT * EK):
                    k, tt = n // NT, n % NT
                    if n >= 8:
                        eng.wait_ge(dve_done, dv[(n - 8) // NT, (n - 8) % NT])
                    eng.indirect_dma_start(got[n % 8], None, y_dram,
                                           bass.IndirectOffsetOnAxis(ap=srow[:, tt * EK + k:tt * EK + k + 1], axis=0))\
                       .then_inc(got_in[n % 8], 16)

            @block.vector
            def _(eng):
                for n in range(NT * EK):
                    k, tt = n // NT, n % NT
                    eng.wait_ge(got_in[n % 8], 16 * (n // 8 + 1))
                    if k:
                        eng.wait_ge(dve_done, dv[k - 1, tt])
                    nc.vector.scalar_tensor_tensor(out=h[:, tt, :], in0=got[n % 8], scalar=gk[:, tt * EK + k:tt * EK + k + 1],
                                                   in1=h[:, tt, :], op0=ALU.mult, op1=ALU.add).then_inc(dve_done, 1)

        stored = sem("stored")

        def store(sp, dv):
            for i in range(NT):
                sp.wait_ge(dve_done, dv["scale", i])
                sp.dma_start(out[0, i * P:(i + 1) * P, :], tok[:, i, :]).then_inc(stored, 16)
            sp.wait_ge(stored, 16 * NT)
        final_norm(h, 1, t["g_final_2"].rearrange("(o d) -> o d", o=1), tok, tok, done_sp=store)


_RAW = ["x", "w_in", "ln_c_g", "ln_c_b", "w_out", "g_ffn", "w_q", "expert_u", "expert_v", "w_pe", "w_pg", "g_final",
        "mem_2", "w_in_2", "w_pool_2", "w_out_2", "w_mem_q_2", "w_mem_kv_2", "w_mem_o_2", "g_ffn_2", "w_router_2",
        "b_router_2", "w_expert_in_2", "w_expert_out_2", "g_final_2"]


def _channels(a, tiles):
    a = np.asarray(a)
    a = a.reshape(tiles, P, -1)
    return np.ascontiguousarray(a.transpose(1, 0, 2)).reshape(P, -1)


def kernel(**inputs):
    import concourse.bacc as _bacc
    from concourse.bass_utils import run_bass_kernel_spmd as _run

    i = {k: np.asarray(v) for k, v in inputs.items()}
    arrays = {n: np.ascontiguousarray(i[n]) for n in _RAW}
    b_s = i["b_s"][0].reshape(TC, 2, P)
    parts = {
        "g_mix": _channels(i["g_mix"][0], KD), "conv_a_w": _channels(i["conv_a_w"][0].T, TA),
        "conv_a_b": _channels(i["conv_a_b"][0], TA), "ln_a_g": _channels(i["ln_a_g"][0], TA),
        "ln_a_b": _channels(i["ln_a_b"][0], TA), "conv_b_w": _channels(i["conv_b_w"][0].T, TB),
        "g_ple": _channels(i["g_ple"][0], KD), "g_mix_2": _channels(i["g_mix_2"][0], KD),
        "g_sb": _channels(i["g_sb_out_2"][0], 4), "g_pool": _channels(i["g_pool_out_2"][0], 4),
        "pool_scale": _channels(i["pool_scale_2"][0], 4), "g_mem_q": _channels(i["g_mem_q_2"][0], KD),
        "g_mem_kv": _channels(i["g_mem_kv_2"][0], KD),
        "b_s": np.repeat(b_s.transpose(1, 0, 2).reshape(2, TC * P), HD, axis=0),
    }
    arrays["params"] = np.ascontiguousarray(np.concatenate([parts[n] for n in _Q], axis=1))
    arrays["consts"] = constants()
    arrays["w_s_T"] = np.ascontiguousarray(i["w_s"][0].transpose(2, 0, 1))
    arrays["sub_keys_T"] = np.ascontiguousarray(i["sub_keys"][0].reshape(HH, NK, P).transpose(2, 0, 1))
    arrays["p_T"] = np.ascontiguousarray(i["p"][0, 0].T)
    arrays["b_expert"] = np.ascontiguousarray(np.concatenate([i["b_expert_in_2"][0], i["b_expert_out_2"][0]], axis=1))

    nc = _bacc.Bacc("TRN2", target_bir_lowering=False, num_devices=1)
    t = {n: nc.dram_tensor(f"in_{n}", a.shape, mybir.dt.from_np(a.dtype), kind="ExternalInput").ap()
         for n, a in arrays.items()}
    out = nc.dram_tensor("out_0", (1, S, D), F32, kind="ExternalOutput").ap()
    build(nc, t, out)
    r = _run(nc, [{f"in_{n}": a for n, a in arrays.items()}], core_ids=[0])
    return r.results[0]["out_0"]
```

```python
from contextlib import ExitStack

import numpy as np

import concourse.bass as bass
from concourse import mybir

ALU = mybir.AluOpType
ACT = mybir.ActivationFunctionType
F32 = mybir.dt.float32
BF16 = mybir.dt.bfloat16
I32 = mybir.dt.int32
U32 = mybir.dt.uint32
AX = mybir.AxisListType.X

P = 128
S = 512
D = 1024
NT = S // P
KD = D // P
NC = 512
D_A, D_B, D_C = 384, 256, 384
TA, TB, TC = D_A // P, D_B // P, D_C // P
IN_COLS = 2 * D_A + 3 * D_B + 2 * D_C
WA, WB = 31, 3
HC = 6
HH = 16
PH = 8
NK = 128
TOPK = 16
PLE = 256
SBH = 8
HD = 64
WINS = (2, 4, 8, 16)
PADU = 16
NMEM = 256
TM = NMEM // P
MH = 4
NE = 32
EK = 4
FF = 1024
EPS1, EPS2 = 1e-6, 1e-5
NBLK = 47
NBP = 48
BATCH = 16
LEAST_LIVE = S * EK // P
GRP = 8
LOWEST = -3.0e38

_C = {}
_n = 0
for _name, _w in (("ident", P), ("lt", P), ("gt", P), ("ones", P), ("bones", P), ("wsmask", P),
                  ("iota", P), ("tok", NT), ("emod", P), ("rcount", 4 * PADU), ("zero", P), ("eps", 2)):
    _C[_name] = (_n, _w)
    _n += _w
NCONST = _n

_Q = {}
_n = 0
for _name, _w in (("g_mix", KD), ("conv_a_w", TA * WA), ("conv_a_b", TA), ("ln_a_g", TA), ("ln_a_b", TA),
                  ("conv_b_w", TB * WB), ("g_ple", KD), ("g_mix_2", KD), ("g_sb", 4), ("g_pool", 4),
                  ("pool_scale", 4), ("g_mem_q", KD), ("g_mem_kv", KD), ("b_s", TC * P)):
    _Q[_name] = (_n, _w)
    _n += _w
NPAR = _n


def constants():
    c = np.zeros((P, NCONST), np.float32)
    p = np.arange(P)[:, None]
    m = np.arange(P)[None, :]

    def put(name, a):
        o, w = _C[name]
        c[:, o:o + w] = a

    put("ident", p == m)
    put("lt", p < m)
    put("gt", p > m)
    put("ones", 1.0)
    put("bones", (p // HD == m // HD) / HD)
    put("wsmask", p // HD <= m // HD)
    put("iota", m)
    put("tok", p + P * np.arange(NT)[None, :])
    put("emod", p % NE + 0 * m)
    t = np.arange(PADU)
    put("rcount", np.concatenate([1.0 / np.minimum(t + 1, w) for w in WINS])[None, :])
    put("eps", np.array([[EPS1, EPS2]]))
    return c


class Steps:

    def __init__(self, start, labels):
        self.start, self.labels = start, list(labels)
        self.at = {label: start + i + 1 for i, label in enumerate(self.labels)}

    def __getitem__(self, label):
        return self.at[label]

    def end(self):
        return self.start + len(self.labels)


def build(nc, t, out):
    ctx = ExitStack()
    with ctx:
        def sb(name, shape, dt=F32):
            return ctx.enter_context(nc.sbuf_tensor(name, shape, dt))

        def sem(name):
            return ctx.enter_context(nc.semaphore(name))

        wring = [sb(f"wring{i}", [P, KD * NC]) for i in range(4)]
        X = sb("work", [P, 4 * KD * NC])
        h = sb("h", [P, NT, D])
        aT = sb("aT", [P, KD, S])
        tok = sb("tok", [P, NT, D])
        mixT = tok[:, :, :].rearrange("p t d -> p (t d)").rearrange("p (k s) -> p k s", k=KD)
        cst = sb("cst", [P, NCONST])
        par = sb("par", [P, NPAR])
        grow = sb("grow", [P, D])
        stat = sb("stat", [P, 64])
        bank = ctx.enter_context(nc.psum_tensor("banks", [P, 8, NC], F32))

        def const(name, lo=0, hi=None):
            o, w = _C[name]
            return cst[:, o + lo:o + (w if hi is None else hi)]

        def param(name, lo=0, hi=None):
            o, w = _Q[name]
            return par[:, o + lo:o + (w if hi is None else hi)]

        ident = const("ident")

        xn_dram = nc.dram_tensor("ffn_rows", (S, D), F32).ap()
        y_dram = nc.dram_tensor("expert_rows", (NBP * P, D), F32).ap()

        pe_done = sem("pe_done")
        dve_done = sem("dve_done")
        act_done = sem("act_done")
        pool_done = sem("pool_done")
        first_in = sem("first_in")
        late_in = sem("late_in")
        rows_filled = sem("rows_filled")
        row_in = sem("row_in")
        chunk_in = [sem(f"chunk_in{i}") for i in range(4)]
        at = {"pe": 0, "dve": 0, "act": 0, "pool": 0, "late": 0, "row": 0}

        def steps(eng, labels):
            s = Steps(at[eng], labels)
            at[eng] = s.end()
            return s

        def cols(w, lo, n=NC, k=KD):
            return w.rearrange("(k p) n -> p k n", p=P)[:, 0:k, lo:lo + n], k, n

        w_in, w_in2 = t["w_in"][0], t["w_in_2"][0]
        chunks = [cols(w_in, 0), cols(w_in, 512), cols(w_in, 1536 + D_C, D_C), cols(w_in, 1024), cols(w_in, 1536, D_C)]
        chunks += [cols(t["w_out"][0], c) for c in (0, 512)]
        chunks += [cols(t["w_q"][0], c) for c in (0, 512, 1024, 1536)]
        chunks += [cols(t["w_pg"][0], c) for c in (0, 512)]
        chunks += [cols(t["w_pe"][0], 0, D, PLE // P)]
        chunks += [cols(w_in2, c) for c in (0, 512, 1024, 1536)]
        chunks += [cols(t["w_out_2"][0], c) for c in (0, 512)]
        chunks += [cols(t["w_mem_kv_2"][0], c) for c in (0, 512, 1024, 1536)]
        chunks += [cols(t["w_mem_q_2"][0], c) for c in (0, 512)]
        chunks += [cols(t["w_mem_o_2"][0], c) for c in (0, 512)]
        (C_IN, C_OUT, C_Q, C_PG, C_PE, C_IN2, C_OUT2, C_KV, C_MQ, C_MO) = (0, 5, 7, 11, 13, 14, 18, 20, 24, 26)

        def chunk_view(i):
            _, k, n = chunks[i]
            return wring[i % 4][:, 0:k * n].rearrange("p (k n) -> p k n", k=k)

        def load_chunk(sp, i):
            if i < len(chunks):
                sp.dma_start(chunk_view(i), chunks[i][0]).then_inc(chunk_in[i % 4], 16)

        def wait_chunk(eng, i):
            eng.wait_ge(chunk_in[i % 4], 16 * (i // 4 + 1))

        def dense(jobs, before_sp=None, after_dve=None):
            pe = steps("pe", range(len(jobs)))
            dv = steps("dve", [j for j, job in enumerate(jobs) if job[3] == "dve"])
            ac = steps("act", [j for j, job in enumerate(jobs) if job[3] == "act"])

            def evacuated(j):
                return (dve_done, dv[j]) if jobs[j][3] == "dve" else (act_done, ac[j])

            last_of = {}
            for j, job in enumerate(jobs):
                last_of[job[0]] = j
            with nc.Block() as block:
                @block.sync
                def _(sp):
                    if before_sp:
                        before_sp(sp)
                    for c, j in last_of.items():
                        sp.wait_ge(pe_done, pe[j])
                        load_chunk(sp, c + 4)

                @block.tensor
                def _(eng):
                    seen = set()
                    for j, (c, mms, _, _, _, _) in enumerate(jobs):
                        if c not in seen:
                            wait_chunk(eng, c)
                            seen.add(c)
                        if j >= 8:
                            eng.wait_ge(*evacuated(j - 8))
                        for i, (dst, lhsT, rhs, start, stop) in enumerate(mms):
                            mm = nc.tensor.matmul(dst(j % 8), lhsT, rhs, start=start, stop=stop)
                        mm.then_inc(pe_done, 1)

                def evacuate(eng, which, s, done):
                    for j, job in enumerate(jobs):
                        if job[3] != which:
                            continue
                        eng.wait_ge(pe_done, pe[j])
                        if job[5] is not None:
                            eng.wait_ge(*evacuated(job[5]))
                        job[4](j % 8).then_inc(done, 1)

                @block.vector
                def _(eng):
                    evacuate(eng, "dve", dv, dve_done)

                @block.scalar
                def _(eng):
                    evacuate(eng, "act", ac, act_done)

        def whole(n=NC, rows=P):
            return lambda b: bank[0:rows, b, 0:n]

        def t_job(c, col, src, n, who, evac, after=None, m=P):
            w = chunk_view(c)
            k = chunks[c][1]
            mms = [(whole(n), w[:, i, col:col + m], src[:, i, 0:n], i == 0, i == k - 1) for i in range(k)]
            return (c, mms, m, who, evac, after)

        def tok_job(c, col, n, src, tt, who, evac, after=None):
            w = chunk_view(c)
            k = chunks[c][1]
            mms = [(whole(n), src[:, i, tt * P:(tt + 1) * P], w[:, i, col:col + n], i == 0, i == k - 1)
                   for i in range(k)]
            return (c, mms, P, who, evac, after)

        def normalise(src, ntt, eps_col, gain, dst, dstT, sp_work=None):
            ac = steps("act", [("sq", i) for i in range(ntt)] + ["sd"] + [("out", k) for k in range(1, KD, 2)])
            dv = steps("dve", ["rstd"] + [("scale", i) for i in range(ntt)] + [("out", k) for k in range(0, KD, 2)])
            pe = steps("pe", range(KD))
            ss, sd, rstd = stat[:, 0:ntt], stat[:, 4:4 + ntt], stat[:, 8:8 + ntt]
            with nc.Block() as block:
                @block.sync
                def _(sp):
                    if sp_work:
                        sp_work(sp)

                @block.scalar
                def _(eng):
                    for i in range(ntt):
                        nc.scalar.activation(dst[:, i, :], src[:, i, :], ACT.Square,
                                             accum_out=ss[:, i:i + 1]).then_inc(act_done, 1)
                    eng.wait_ge(act_done, ac["sq", ntt - 1])
                    nc.scalar.activation(sd, ss, ACT.Sqrt, scale=1.0 / D,
                                         bias=const("eps", eps_col, eps_col + 1)).then_inc(act_done, 1)
                    for k in range(1, KD, 2):
                        eng.wait_ge(pe_done, pe[k])
                        nc.scalar.activation(dstT[:, k, 0:ntt * P], bank[:, k, 0:ntt * P], ACT.Copy,
                                             scale=gain[:, k:k + 1]).then_inc(act_done, 1)

                @block.vector
                def _(eng):
                    eng.wait_ge(act_done, ac["sd"])
                    nc.vector.reciprocal(rstd, sd).then_inc(dve_done, 1)
                    eng.wait_ge(dve_done, dv["rstd"])
                    for i in range(ntt):
                        nc.vector.tensor_scalar(dst[:, i, :], src[:, i, :], rstd[:, i:i + 1], None, ALU.mult)\
                          .then_inc(dve_done, 1)
                    for k in range(0, KD, 2):
                        eng.wait_ge(pe_done, pe[k])
                        nc.vector.tensor_scalar(dstT[:, k, 0:ntt * P], bank[:, k, 0:ntt * P],
                                                gain[:, k:k + 1], None, ALU.mult).then_inc(dve_done, 1)

                @block.tensor
                def _(eng):
                    for k in range(KD):
                        for i in range(ntt):
                            if k == 0:
                                eng.wait_ge(dve_done, dv["scale", i])
                            mm = nc.tensor.transpose(bank[:, k, i * P:(i + 1) * P], dst[:, i, k * P:(k + 1) * P], ident)
                        mm.then_inc(pe_done, 1)

        def over(x, n):
            return x.rearrange("p (g o) -> p g o", o=1).to_broadcast([P, x.shape[1], n])

        def add_to_h(tt, lo, n=NC):
            def evac(b):
                return nc.vector.tensor_tensor(h[:, tt, lo:lo + n], h[:, tt, lo:lo + n], bank[:, b, 0:n], ALU.add)
            return evac

        def project_and_normalise(c0, src, rows, eps_col, gain, dstT, row_ap=None, sp_work=None, pool_work=None,
                                  aside=()):
            todo = [(h[:, i, :], rows[:, i, :], gain, dstT[:, :, i * P:(i + 1) * P]) for i in range(NT)]
            tiles = [(i, *todo[i]) for i in range(2)] + [(None, *x) for x in aside] + [(i, *todo[i]) for i in range(2, NT)]
            n_t = len(tiles)
            late_at = at["late"]
            pel, dvl = [], []
            for i in range(n_t + 1):
                if i < n_t and tiles[i][0] is not None:
                    pel += [("p", i, 0), ("p", i, 1)]
                    dvl += [("add", i, 0), ("add", i, 1)]
                if i:
                    pel += [("t", i - 1, 0), ("t", i - 1, 1)]
                    dvl += [("out", i - 1, 0), ("out", i - 1, 1)]
                if i < n_t:
                    dvl += [("rstd", i), ("scale", i)]
            pe, dv = steps("pe", pel), steps("dve", dvl)
            ac = steps("act", [x for i in range(n_t) for x in (("sq", i), ("sd", i))])
            if row_ap is not None:
                at["row"] += 16
            row_at = at["row"]

            def banks(i, n):
                return 4 + (2 * i + n) % 4
            order = [i for i in range(n_t) if tiles[i][0] is not None]

            with nc.Block() as block:
                @block.sync
                def _(sp):
                    if row_ap is not None:
                        sp.dma_start(grow[:, :], row_ap.to_broadcast([P, D])).then_inc(row_in, 16)
                    if sp_work:
                        sp_work(sp)
                    for n in range(2):
                        sp.wait_ge(pe_done, pe["p", n_t - 1, n])
                        load_chunk(sp, c0 + n + 4)

                @block.tensor
                def _(eng):
                    for n in range(2):
                        wait_chunk(eng, c0 + n)
                    for i in range(n_t + 1):
                        if i < n_t and tiles[i][0] is not None:
                            tt = tiles[i][0]
                            for n in range(2):
                                if tt >= 2:
                                    eng.wait_ge(dve_done, dv["add", order[tt - 2], n])
                                for k in range(KD):
                                    mm = nc.tensor.matmul(bank[:, (2 * tt + n) % 4, :], src[:, k, tt * P:(tt + 1) * P],
                                                          chunk_view(c0 + n)[:, k, :], start=k == 0, stop=k == KD - 1)
                                mm.then_inc(pe_done, 1)
                        if i:
                            eng.wait_ge(dve_done, dv["scale", i - 1])
                            for n in range(2):
                                if i >= 3:
                                    eng.wait_ge(dve_done, dv["out", i - 3, n])
                                for k in range(4):
                                    kk = 4 * n + k
                                    mm = nc.tensor.transpose(bank[:, banks(i - 1, n), k * P:(k + 1) * P],
                                                             tiles[i - 1][2][:, kk * P:(kk + 1) * P], ident)
                                mm.then_inc(pe_done, 1)

                @block.scalar
                def _(eng):
                    for i, (tt, source, scaled, _, _) in enumerate(tiles):
                        if tt is None:
                            eng.wait_ge(late_in, late_at)
                        else:
                            eng.wait_ge(dve_done, dv["add", i, 1])
                        nc.scalar.activation(scaled, source, ACT.Square, accum_out=stat[:, i:i + 1]).then_inc(act_done, 1)
                        eng.wait_ge(act_done, ac["sq", i])
                        nc.scalar.activation(stat[:, 8 + i:9 + i], stat[:, i:i + 1], ACT.Sqrt, scale=1.0 / D,
                                             bias=const("eps", eps_col, eps_col + 1)).then_inc(act_done, 1)

                @block.vector
                def _(eng):
                    if row_ap is not None:
                        eng.wait_ge(row_in, row_at)
                    for i in range(n_t + 1):
                        if i < n_t and tiles[i][0] is not None:
                            tt = tiles[i][0]
                            for n in range(2):
                                eng.wait_ge(pe_done, pe["p", i, n])
                                add_to_h(tt, n * NC)((2 * tt + n) % 4).then_inc(dve_done, 1)
                        if i:
                            _, _, _, g, dT = tiles[i - 1]
                            for n in range(2):
                                eng.wait_ge(pe_done, pe["t", i - 1, n])
                                b4 = bank[:, banks(i - 1, n), :].rearrange("p (k m) -> p k m", k=4)
                                d4 = dT[:, 4 * n:4 * n + 4, :]
                                if g is None:
                                    ins = nc.vector.tensor_copy(d4, b4)
                                else:
                                    ins = nc.vector.tensor_tensor(d4, b4, over(g[:, 4 * n:4 * n + 4], P), ALU.mult)
                                ins.then_inc(dve_done, 1)
                        if i < n_t:
                            _, source, scaled, _, _ = tiles[i]
                            rstd = stat[:, 16 + i:17 + i]
                            eng.wait_ge(act_done, ac["sd", i])
                            nc.vector.reciprocal(rstd, stat[:, 8 + i:9 + i]).then_inc(dve_done, 1)
                            eng.wait_ge(dve_done, dv["rstd", i])
                            if row_ap is None:
                                ins = nc.vector.tensor_scalar(scaled, source, rstd, None, ALU.mult)
                            else:
                                ins = nc.vector.scalar_tensor_tensor(out=scaled, in0=source, scalar=rstd, in1=grow[:, :],
                                                                     op0=ALU.mult, op1=ALU.mult)
                            ins.then_inc(dve_done, 1)

                if pool_work:
                    @block.gpsimd
                    def _(eng):
                        pool_work(eng)

        def region(lo, n):
            return X[:, lo:lo + n]

        o = 0
        zT = region(o, 15 * S).rearrange("p (c s) -> p c s", c=15)
        o += 15 * S
        vt = region(o, NT * D_C).rearrange("p (t n) -> p t n", t=NT)
        o += NT * D_C
        LA = S + WA - 1
        ya_in = region(o, TA * LA).rearrange("p (c s) -> p c s", c=TA)
        o += TA * LA
        acc = region(o, TA * S).rearrange("p (c s) -> p c s", c=TA)
        o += TA * S
        LB = S + WB - 1
        yb_in = region(o, TB * LB).rearrange("p (c s) -> p c s", c=TB)
        o += TB * LB
        yb_t = region(o, TB * S).rearrange("p (c s) -> p c s", c=TB)
        o += TB * S
        lnc = region(o, 2 * D_C)
        o += 2 * D_C
        wsT = region(o, HC * P).rearrange("p (h i) -> p h i", h=HC)
        o += HC * P
        assert o <= 4 * KD * NC
        VAL, GATE, BG, CG, XB, U = 0, TA, 2 * TA, 2 * TA + TB, 2 * TA + 2 * TB, 2 * TA + 3 * TB

        with nc.Block() as block:
            @block.sync
            def _(sp):
                sp.dma_start(h[:, :, :], t["x"][0].rearrange("(t p) d -> p t d", p=P)).then_inc(first_in, 16)
                sp.dma_start(cst[:, :], t["consts"][:, :]).then_inc(first_in, 16)
                sp.dma_start(par[:, :], t["params"][:, :]).then_inc(first_in, 16)
                load_chunk(sp, 0)
                load_chunk(sp, 1)
                sp.dma_start(wsT[:, :, :], t["w_s_T"][:, :, :]).then_inc(late_in, 16)
                sp.dma_start(lnc[:, 0:D_C], t["ln_c_g"][0:1, :].to_broadcast([P, D_C])).then_inc(late_in, 16)
                sp.dma_start(lnc[:, D_C:2 * D_C], t["ln_c_b"][0:1, :].to_broadcast([P, D_C])).then_inc(late_in, 16)
                load_chunk(sp, 2)
                load_chunk(sp, 3)
                sp.wait_ge(first_in, 48)

        at["late"] += 48
        mixer_at = at["late"]
        normalise(h, NT, 0, param("g_mix"), tok, aT)

        def in_chunk(c):
            return (c // 4 if c < 8 else 3 + (c - 8) // 4), c % 4 * P
        jobs = [(*in_chunk(c), c, None) for c in range(8)] + [(2, 0, None, tt) for tt in range(NT)]
        jobs += [(*in_chunk(c), c, None) for c in range(8, 15)]
        made = {}
        for j, job in enumerate(jobs):
            made[job[2]] = j
        VJ = 8 + NT - 1
        NJ = len(jobs)

        v24 = vt[:, :, :].rearrange("p t (h c) -> p (t h) c", h=HC)
        sq24 = mixT[:, TA + TB:KD, :].rearrange("p c s -> p (c s)").rearrange("p (g c) -> p g c", c=HD)
        m24, s24, r24 = stat[:, 12:36], stat[:, 36:60], stat[:, 12:36]

        def over_t(x):
            return x.rearrange("p (o n) -> p o n", o=1).to_broadcast([P, NT, x.shape[1]])

        V_LN = {19: ["vsum", "vmean", "vsub"], 22: ["vvar"], 25: ["vr", "vscale", "vg", "vb"]}
        dv = steps("dve", [("pad", c) for c in range(TA)] + [("glu", c) for c in range(TA)]
                   + [x for k in range(WA) for x in V_LN.get(k, []) + [("tap", k, c) for c in range(TA)]]
                   + [("u1", i) for i in range(TC)] + [("u2", i) for i in range(TC)]
                   + [("am", c) for c in range(TA)] + [("ar", c) for c in range(TA)]
                   + [("as", c) for c in range(TA)])
        ac = steps("act", [x for j in range(NJ) for x in [("z", j)] + (["vsq"] if j == VJ + 1 else [])
                           + (["vsd"] if j == VJ + 2 else [])] + [("asq", c) for c in range(TA)] + [("asd", c) for c in range(TA)]
                   + [("silu", c) for c in range(TA)])
        pe = steps("pe", [("z", j) for j in range(NJ)] + [("mix", i) for i in range(TC)] + [("am", c) for c in range(TA)] + [("av", c) for c in range(TA)])
        po = steps("pool", ["ws", "pad"] + [("g", c) for c in range(TB)]
                   + [("t", k, c) for k in range(WB) for c in range(TB)]
                   + [("s", k, c) for k in range(1, WB) for c in range(TB)] + [("out", c) for c in range(TB)])
        with nc.Block() as block:
            @block.sync
            def _(sp):
                for c in range(5):
                    sp.wait_ge(pe_done, pe["z", max(j for j in range(NJ) if jobs[j][0] == c)])
                    load_chunk(sp, C_IN + c + 4)

            @block.scalar
            def _(eng):
                for j, (_, _, c, tt) in enumerate(jobs):
                    eng.wait_ge(pe_done, pe["z", j])
                    if c is None:
                        ins = nc.scalar.activation(vt[:, tt, :], bank[:, j % 8, 0:D_C], ACT.Copy)
                    else:
                        ins = nc.scalar.activation(zT[:, c, :], bank[:, j % 8, :],
                                                   ACT.Sigmoid if GATE <= c < BG else ACT.Copy)
                    ins.then_inc(act_done, 1)
                    if j == VJ + 1:
                        eng.wait_ge(dve_done, dv["vsub"])
                        nc.scalar.activation(sq24, v24, ACT.Square).then_inc(act_done, 1)
                    if j == VJ + 2:
                        eng.wait_ge(dve_done, dv["vvar"])
                        nc.scalar.activation(s24, s24, ACT.Sqrt, scale=1.0 / HD, bias=const("eps", 0, 1))\
                          .then_inc(act_done, 1)
                for c in range(TA):
                    eng.wait_ge(dve_done, dv["am", c])
                    nc.scalar.activation(zT[:, GATE + c, :], acc[:, c, :], ACT.Square).then_inc(act_done, 1)
                for c in range(TA):
                    eng.wait_ge(pe_done, pe["av", c])
                    nc.scalar.activation(zT[:, VAL + c, :], bank[:, 3 + c, :], ACT.Sqrt,
                                         bias=const("eps", 0, 1)).then_inc(act_done, 1)
                for c in range(TA):
                    eng.wait_ge(dve_done, dv["as", c])
                    nc.scalar.activation(mixT[:, c, :], acc[:, c, :], ACT.Silu, scale=param("ln_a_g", c, c + 1),
                                         bias=param("ln_a_b", c, c + 1)).then_inc(act_done, 1)

            @block.vector
            def _(eng):
                def v_norm(k):
                    if k == 19:
                        eng.wait_ge(act_done, ac["z", VJ])
                        nc.vector.tensor_reduce(m24, v24, AX, ALU.add).then_inc(dve_done, 1)
                        eng.wait_ge(dve_done, dv["vsum"])
                        nc.vector.tensor_scalar(m24, m24, 1.0 / HD, None, ALU.mult).then_inc(dve_done, 1)
                        eng.wait_ge(dve_done, dv["vmean"])
                        nc.vector.tensor_tensor(v24, v24, over(m24, HD), ALU.subtract).then_inc(dve_done, 1)
                    if k == 22:
                        eng.wait_ge(act_done, ac["vsq"])
                        nc.vector.tensor_reduce(s24, sq24, AX, ALU.add).then_inc(dve_done, 1)
                    if k == 25:
                        eng.wait_ge(act_done, ac["vsd"])
                        nc.vector.reciprocal(r24, s24).then_inc(dve_done, 1)
                        eng.wait_ge(dve_done, dv["vr"])
                        nc.vector.tensor_tensor(v24, v24, over(r24, HD), ALU.mult).then_inc(dve_done, 1)
                        eng.wait_ge(dve_done, dv["vscale"])
                        eng.wait_ge(late_in, mixer_at)
                        nc.vector.tensor_tensor(vt[:, :, :], vt[:, :, :], over_t(lnc[:, 0:D_C]), ALU.mult)\
                          .then_inc(dve_done, 1)
                        eng.wait_ge(dve_done, dv["vg"])
                        nc.vector.tensor_tensor(vt[:, :, :], vt[:, :, :], over_t(lnc[:, D_C:2 * D_C]), ALU.add)\
                          .then_inc(dve_done, 1)

                for c in range(TA):
                    nc.vector.memset(ya_in[:, c, 0:WA - 1], 0.0).then_inc(dve_done, 1)
                for c in range(TA):
                    eng.wait_ge(act_done, ac["z", made[GATE + c]])
                    nc.vector.tensor_tensor(ya_in[:, c, WA - 1:LA], zT[:, VAL + c, :], zT[:, GATE + c, :],
                                            ALU.mult).then_inc(dve_done, 1)
                for k in range(WA):
                    v_norm(k)
                    for c in range(TA):
                        w = param("conv_a_w", c * WA + k, c * WA + k + 1)
                        if k == 0:
                            eng.wait_ge(dve_done, dv["glu", c])
                            ins = nc.vector.tensor_scalar(acc[:, c, :], ya_in[:, c, 0:S], w,
                                                          param("conv_a_b", c, c + 1), ALU.mult, ALU.add)
                        else:
                            eng.wait_ge(dve_done, dv["tap", k - 1, c])
                            ins = nc.vector.scalar_tensor_tensor(out=acc[:, c, :], in0=ya_in[:, c, k:k + S], scalar=w,
                                                                 in1=acc[:, c, :], op0=ALU.mult, op1=ALU.add)
                        ins.then_inc(dve_done, 1)
                for i in range(TC):
                    eng.wait_ge(pe_done, pe["mix", i])
                    mixed = mixT[:, TA + TB + i, :].rearrange("p (t i) -> p t i", t=NT)
                    nc.vector.tensor_tensor(mixed, bank[:, i, :].rearrange("p (t i) -> p t i", t=NT),
                                            over_t(param("b_s", i * P, (i + 1) * P)), ALU.add).then_inc(dve_done, 1)
                for i in range(TC):
                    eng.wait_ge(dve_done, dv["u1", i])
                    eng.wait_ge(act_done, ac["z", made[U + i]])
                    nc.vector.tensor_tensor(mixT[:, TA + TB + i, :], mixT[:, TA + TB + i, :], zT[:, U + i, :],
                                            ALU.mult).then_inc(dve_done, 1)
                for c in range(TA):
                    eng.wait_ge(pe_done, pe["am", c])
                    nc.vector.tensor_tensor(acc[:, c, :], acc[:, c, :], bank[:, 4 + c % 4, :], ALU.subtract).then_inc(dve_done, 1)
                for c in range(TA):
                    eng.wait_ge(act_done, ac["asd", c])
                    nc.vector.reciprocal(zT[:, VAL + c, :], zT[:, VAL + c, :]).then_inc(dve_done, 1)
                for c in range(TA):
                    eng.wait_ge(dve_done, dv["ar", c])
                    nc.vector.tensor_tensor(acc[:, c, :], acc[:, c, :], zT[:, VAL + c, :], ALU.mult).then_inc(dve_done, 1)

            @block.tensor
            def _(eng):
                for j, (c, col, ch, tt) in enumerate(jobs):
                    if j == 0 or c != jobs[j - 1][0]:
                        wait_chunk(eng, c)
                    if j >= 8:
                        eng.wait_ge(act_done, ac["z", j - 8])
                    w = chunk_view(c)
                    for k in range(KD):
                        if ch is None:
                            mm = nc.tensor.matmul(bank[:, j % 8, 0:D_C], aT[:, k, tt * P:(tt + 1) * P], w[:, k, :],
                                                  start=k == 0, stop=k == KD - 1)
                        else:
                            mm = nc.tensor.matmul(bank[:, j % 8, :], w[:, k, col:col + P], aT[:, k, :],
                                                  start=k == 0, stop=k == KD - 1)
                    mm.then_inc(pe_done, 1)
                eng.wait_ge(act_done, ac["z", NJ - 1])
                eng.wait_ge(dve_done, dv["vb"])
                eng.wait_ge(pool_done, po["ws"])
                for i in range(TC):
                    for tt in range(NT):
                        for half in range(2):
                            hd = 2 * i + half
                            mm = nc.tensor.matmul(bank[half * HD:(half + 1) * HD, i, tt * P:(tt + 1) * P],
                                                  vt[:, tt, hd * HD:(hd + 1) * HD], wsT[:, hd, :],
                                                  start=True, stop=True)
                    mm.then_inc(pe_done, 1)
                for c in range(TA):
                    eng.wait_ge(dve_done, dv["tap", WA - 1, c])
                    nc.tensor.matmul(bank[:, 4 + c % 4, :], const("bones"), acc[:, c, :],
                                     start=True, stop=True).then_inc(pe_done, 1)
                for c in range(TA):
                    eng.wait_ge(act_done, ac["asq", c])
                    if c == 0:
                        eng.wait_ge(dve_done, dv["u1", TC - 1])
                        eng.wait_ge(dve_done, dv["am", TA - 1])
                    nc.tensor.matmul(bank[:, 3 + c, :], const("bones"), zT[:, GATE + c, :],
                                     start=True, stop=True).then_inc(pe_done, 1)

            @block.gpsimd
            def _(eng):
                eng.wait_ge(late_in, mixer_at)
                eng.tensor_tensor(wsT[:, :, :], wsT[:, :, :],
                                  const("wsmask").rearrange("p (o i) -> p o i", o=1).to_broadcast([P, HC, P]),
                                  ALU.mult).then_inc(pool_done, 1)
                eng.memset(yb_in[:, :, 0:WB - 1], 0.0).then_inc(pool_done, 1)
                for c in range(TB):
                    eng.wait_ge(act_done, ac["z", made[XB + c]])
                    eng.tensor_tensor(yb_in[:, c, WB - 1:LB], zT[:, CG + c, :], zT[:, XB + c, :], ALU.mult).then_inc(pool_done, 1)
                eng.wait_ge(pool_done, po["g", TB - 1])
                dst = [zT[:, CG:CG + TB, :], zT[:, XB:XB + TB, :], yb_t]
                for k in range(WB):
                    for c in range(TB):
                        w = param("conv_b_w", c * WB + k, c * WB + k + 1)
                        eng.tensor_scalar(dst[k][:, c, :], yb_in[:, c, k:k + S], w, None, ALU.mult).then_inc(pool_done, 1)
                for k in range(1, WB):
                    for c in range(TB):
                        eng.wait_ge(pool_done, po["t", k, c] if k == 1 else po["s", k - 1, c])
                        if k > 1:
                            eng.wait_ge(pool_done, po["t", k, c])
                        eng.tensor_tensor(dst[0][:, c, :], dst[0][:, c, :], dst[k][:, c, :], ALU.add).then_inc(pool_done, 1)
                for c in range(TB):
                    eng.wait_ge(pool_done, po["s", WB - 1, c])
                    eng.tensor_tensor(mixT[:, TA + c, :], dst[0][:, c, :], zT[:, BG + c, :], ALU.mult).then_inc(pool_done, 1)

        scores = region(0, NT * HH * NK).rearrange("p (t g k) -> p t g k", t=NT, g=HH)
        qT = region(12288, 4 * S).rearrange("p (c s) -> p c s", c=4)
        keysT = region(10240, HH * NK).rearrange("p (g k) -> p g k", g=HH)
        at["late"] += 16
        keys_at = at["late"]
        rows = region(0, NT * D).rearrange("p (t d) -> p t d", t=NT)
        project_and_normalise(C_OUT, mixT, rows, 0, None, aT, row_ap=t["g_ffn"][0:1, :],
                              sp_work=lambda sp: sp.dma_start(keysT[:, :, :], t["sub_keys_T"][:, :, :]).then_inc(late_in, 16))

        SW = region(NT * HH * NK, HH * NK).rearrange("p (g k) -> p g k", g=HH)
        o = 14336
        kv = region(o, HH * TOPK).rearrange("p (g k) -> p g k", g=HH)
        ki = region(o + 256, HH * TOPK).bitcast(U32).rearrange("p (g k) -> p g k", g=HH)

        def best_steps(src, v, i):
            return [lambda: nc.vector.max(v[:, 0:8], src),
                    lambda: nc.vector.max_index(i[:, 0:8], v[:, 0:8], src),
                    lambda: nc.vector.match_replace(src, v[:, 0:8], src, LOWEST),
                    lambda: nc.vector.max(v[:, 8:16], src),
                    lambda: nc.vector.max_index(i[:, 8:16], v[:, 8:16], src)]
        NBEST = 5

        pe = steps("pe", [x for g in range(HH + 1) for x in ([("q", g)] if g < HH else []) + ([("s", g - 1)] if g else [])])
        ac = steps("act", [("q", g) for g in range(HH)])
        dv = steps("dve", ["rows"] + [x for g in range(HH) for x in [("s", g), ("sw", g)] + [("best", g, i) for i in range(NBEST)]])
        with nc.Block() as block:
            @block.sync
            def _(sp):
                for c in range(2):
                    sp.wait_ge(pe_done, pe["q", 4 * c + 3])
                    load_chunk(sp, C_Q + c + 4)

            @block.tensor
            def _(eng):
                eng.wait_ge(late_in, keys_at)
                for g in range(HH + 1):
                    if g < HH:
                        if g % 4 == 0:
                            wait_chunk(eng, C_Q + g // 4)
                        if g >= 4:
                            eng.wait_ge(act_done, ac["q", g - 4])
                        w = chunk_view(C_Q + g // 4)
                        for k in range(KD):
                            mm = nc.tensor.matmul(bank[:, g % 4, :], w[:, k, g % 4 * P:(g % 4 + 1) * P], aT[:, k, :],
                                                  start=k == 0, stop=k == KD - 1)
                        mm.then_inc(pe_done, 1)
                    if g:
                        s = g - 1
                        eng.wait_ge(act_done, ac["q", s])
                        if s >= 4:
                            eng.wait_ge(dve_done, dv["s", s - 4])
                        for tt in range(NT):
                            mm = nc.tensor.matmul(bank[:, 4 + s % 4, tt * NK:(tt + 1) * NK],
                                                  qT[:, s % 4, tt * P:(tt + 1) * P], keysT[:, s, :], start=True, stop=True)
                        mm.then_inc(pe_done, 1)

            @block.scalar
            def _(eng):
                for g in range(HH):
                    eng.wait_ge(pe_done, pe["q", g])
                    if g >= 4:
                        eng.wait_ge(pe_done, pe["s", g - 4])
                    nc.scalar.activation(qT[:, g % 4, :], bank[:, g % 4, :], ACT.Copy).then_inc(act_done, 1)

            @block.vector
            def _(eng):
                nc.vector.tensor_copy(tok[:, :, :], rows[:, :, :]).then_inc(dve_done, 1)
                eng.wait_ge(dve_done, dv["rows"])
                for g in range(HH):
                    eng.wait_ge(pe_done, pe["s", g])
                    nc.vector.tensor_copy(scores[:, :, g, :], bank[:, 4 + g % 4, :].rearrange("p (t k) -> p t k", t=NT))\
                      .then_inc(dve_done, 1)
                    eng.wait_ge(dve_done, dv["s", g])
                    nc.vector.tensor_copy(SW[:, g, :], scores[:, 0, g, :]).then_inc(dve_done, 1)
                    for i, f in enumerate(best_steps(SW[:, g, :], kv[:, g, :], ki[:, g, :])):
                        eng.wait_ge(dve_done, dv["best", g, i - 1] if i else dv["sw", g])
                        f().then_inc(dve_done, 1)

        cand = region(10240, PH * TOPK * TOPK).rearrange("p (h c) -> p h c", h=PH)
        hot = region(12288, PH * TOPK * TOPK)
        o = 14336
        kf = region(o + 512, HH * TOPK).rearrange("p (g k) -> p g k", g=HH)
        cv = region(o + 768, PH * TOPK).rearrange("p (h k) -> p h k", h=PH)
        ci = region(o + 896, PH * TOPK).bitcast(U32)
        cq = region(o + 1024, 2 * PH * TOPK).bitcast(U32)
        cf = region(o + 1280, 2 * PH * TOPK)
        ef = region(o + 1536, 2 * PH * TOPK)
        sm = region(o + 1792, 2 * PH)
        ce = region(o + 1808, PH * TOPK).rearrange("p (h k) -> p h k", h=PH)
        GK = PH * TOPK
        gates = sb("gates", [P, (NT + 1) * GK])
        eidx = sb("eidx", [P, (NT + 1) * GK], I32)
        top = sem("top_steps")
        differ = sem("top_differ")
        exps = sem("top_exp")
        picked = sem("picked")

        def top_program():
            prog = []

            def step(need, f):
                prog.append((need, f))
                return len(prog)

            def best(src, v, i, pre):
                for f in best_steps(src, v, i):
                    pre = step(pre, f)
                return pre
            return prog, step, best

        prog, step, best = top_program()
        first = step(0, None)
        last = first
        for g in range(HH):
            last = best(SW[:, g, :], kv[:, g, :], ki[:, g, :], first)
        HALVES = last
        a = step(last, lambda: nc.vector.tensor_copy(kf, ki))
        kv4 = kv.rearrange("p (h two) k -> p h two k", two=2)
        kf4 = kf.rearrange("p (h two) k -> p h two k", two=2)
        c4 = cand.rearrange("p h (i j) -> p h i j", i=TOPK)
        for hd in range(PH):
            s = step(last, lambda hd=hd: nc.vector.tensor_tensor(
                c4[:, hd], kv4[:, hd, 0, :].rearrange("p (i o) -> p i o", o=1).to_broadcast([P, TOPK, TOPK]),
                kv4[:, hd, 1, :].rearrange("p (o j) -> p o j", o=1).to_broadcast([P, TOPK, TOPK]), ALU.add))
        lastc = s
        for hd in range(PH):
            lastc = best(cand[:, hd, :], cv[:, hd, :], ci[:, hd * TOPK:(hd + 1) * TOPK], s)
        s1 = step(lastc, lambda: nc.vector.tensor_scalar(cq[:, 0:GK], ci, 4, None, ALU.logical_shift_right))
        s2 = step(lastc, lambda: nc.vector.tensor_scalar(cq[:, GK:2 * GK], ci, 15, None, ALU.bitwise_and))
        s3 = step(s2, lambda: nc.vector.tensor_copy(cf, cq))
        hot3 = hot.rearrange("p (c i) -> p c i", i=TOPK)
        hot4 = hot.rearrange("p (h c i) -> p h c i", h=PH, i=TOPK)
        iota16 = const("iota", 0, TOPK).rearrange("p (o i) -> p o i", o=1).to_broadcast([P, GK, TOPK])
        s6 = s3
        for half in range(2):
            s4 = step(s6, lambda half=half: nc.vector.tensor_tensor(
                hot3, cf[:, half * GK:(half + 1) * GK].rearrange("p (c o) -> p c o", o=1).to_broadcast([P, GK, TOPK]),
                iota16, ALU.is_equal))
            s5 = s4
            for hd in range(PH):
                s5 = step(s4, lambda half=half, hd=hd: nc.vector.tensor_tensor(
                    hot4[:, hd], hot4[:, hd],
                    kf4[:, hd, half, :].rearrange("p (o i) -> p o i", o=1).to_broadcast([P, TOPK, TOPK]), ALU.mult))
            s6 = step(s5, lambda half=half: nc.vector.tensor_reduce(ef[:, half * GK:(half + 1) * GK], hot3, AX, ALU.add))
        IDX = step(s6, None)
        SUB = step(lastc, lambda: nc.vector.tensor_tensor(
            ce, cv, cv[:, :, 0:1].to_broadcast([P, PH, TOPK]), ALU.subtract))
        s7 = step(SUB, lambda: nc.vector.tensor_reduce(sm[:, 0:PH], ce, AX, ALU.add))
        s8 = step(s7, lambda: nc.vector.reciprocal(sm[:, PH:2 * PH], sm[:, 0:PH]))
        GAT = step(s8, None)
        NSTEP = len(prog)

        def pick_best(eng, tile, done=0):
            if done:
                eng.sem_inc(top, done)
            for n, (need, f) in enumerate(prog):
                if n < done:
                    continue
                if n == IDX:
                    eng.wait_ge(top, IDX)
                    eng.sem_inc(picked, 1)
                if n + 1 == s7:
                    eng.wait_ge(exps, tile + 1)
                elif need:
                    eng.wait_ge(top, need - (need > SUB))
                if n + 1 == first:
                    ins = nc.vector.tensor_copy(SW, X[:, bass.ds(tile * (HH * NK), HH * NK)]
                                                .rearrange("p (g k) -> p g k", g=HH))
                elif n + 1 == IDX:
                    ins = nc.vector.scalar_tensor_tensor(
                        out=eidx[:, bass.ds(tile * GK, GK)], in0=ef[:, 0:GK], scalar=float(NK),
                        in1=ef[:, GK:2 * GK], op0=ALU.mult, op1=ALU.add)
                elif n + 1 == GAT:
                    ins = nc.vector.tensor_tensor(
                        gates[:, bass.ds(tile * GK, GK)].rearrange("p (h k) -> p h k", h=PH), ce,
                        over(sm[:, PH:2 * PH], TOPK), ALU.mult)
                else:
                    ins = f()
                ins.then_inc(differ if n + 1 == SUB else top, 1)
            eng.wait_ge(top, NSTEP - 1)
            eng.sem_clear(top)

        def exponentials(eng, tile):
            eng.wait_ge(differ, tile + 1)
            nc.scalar.activation(ce, ce, ACT.Exp).then_inc(exps, 1)

        slot = [wring[C_PE % 4 + j // 4][:, j % 4 * D:(j % 4 + 1) * D] for j in range(GRP)]
        assert (C_PG % 4, (C_PG + 1) % 4, C_PE % 4) == (3, 0, 1) and GRP == 8
        work = aT[:, :, :].rearrange("p k s -> p (k s)")
        o = 0
        dots = work[:, o:o + GK]
        o += GK
        acts = work[:, o:o + GK]
        o += GK
        diag = work[:, o:o + GRP * P].rearrange("p (b m) -> p b m", b=GRP)
        o += GRP * P
        vsum = work[:, o:o + D]
        o += D
        cur = work[:, o:o + 2 * GRP].bitcast(I32)
        row_in_slot = [sem(f"row_in_slot{j}") for j in range(GRP)]
        slot_used = [sem(f"slot_used{j}") for j in range(GRP)]
        cur_ready = sem("cur_ready")
        pool_turn = sem("pool_turn")
        gelu_done = sem("gelu_done")
        acts_done = sem("acts_done")
        diag_done = sem("diag_done")
        vsum_step = sem("vsum_step")
        h_added = sem("h_added")
        dve_turn, act_turn = sem("dve_turn"), sem("act_turn")
        acc_zero = sem("acc_zero")
        acc_free = sem("acc_free")
        u_rows, v_rows = t["expert_u"][0], t["expert_v"][0]
        NG = GK // GRP
        NA = 5
        BY_DVE = (1, 4, 7)
        BY_PE = tuple(j for j in range(GRP) if j not in BY_DVE)
        PE_ROWS = NA * GRP + (NG - NA) * len(BY_PE)
        DVE_ROWS = (NG - NA) * len(BY_DVE)
        h2 = h[:, :, :].rearrange("p t d -> p (t d)")
        tok2 = tok[:, :, :].rearrange("p t d -> p (t d)")

        def turn(tt, g, v):
            return tt * (2 * NG) + g + (NG if v else 0)

        with nc.Block() as block:
            @block.gpsimd
            def _(eng):
                def gather(rows, tt, g, side, v):
                    ix = cur[:, side * GRP:(side + 1) * GRP]
                    eng.tensor_copy(ix, eidx[:, bass.ds(tt * GK + g * GRP, GRP)]).then_inc(cur_ready, 1)
                    eng.wait_ge(cur_ready, turn(tt, g, v) + 1)
                    eng.sem_inc(pool_turn, 1)
                    for j in range(GRP):
                        eng.wait_ge(slot_used[j], turn(tt, g, v) + 1)
                        eng.sem_inc(pool_turn, 1)
                        eng.indirect_dma_start(slot[j], None, rows, bass.IndirectOffsetOnAxis(ap=ix[:, j:j + 1], axis=0))\
                           .then_inc(row_in_slot[j], 16)

                with eng.Fori(0, NT) as tt:
                    eng.wait_ge(picked, tt + 1)
                    eng.sem_inc(pool_turn, 1)
                    for v, rows in enumerate((u_rows, v_rows)):
                        with eng.Fori(0, NG // 2) as pair:
                            gather(rows, tt, pair * 2, 0, v)
                            gather(rows, tt, pair * 2 + 1, 1, v)

            @block.vector
            def _(eng):
                eng.sem_inc(acc_free, 1)
                for j in range(GRP):
                    eng.sem_inc(slot_used[j], 1)
                pick_best(eng, 0, done=HALVES)
                with eng.Fori(0, NT) as tt:
                    nc.vector.memset(vsum, 0.0).then_inc(vsum_step, 1)
                    with eng.Fori(0, NG) as g:
                        for j in range(GRP):
                            eng.wait_ge(row_in_slot[j], (turn(tt, g, 0) + 1) * 16)
                            nc.vector.scalar_tensor_tensor(
                                out=slot[j], in0=slot[j], scalar=1.0, in1=tok2[:, bass.ds(tt * D, D)], op0=ALU.mult,
                                op1=ALU.mult, accum_out=dots[:, bass.ds(g * GRP + j, 1)]).then_inc(slot_used[j], 1)
                    eng.wait_ge(gelu_done, tt + 1)
                    nc.vector.tensor_tensor(acts, acts, gates[:, bass.ds(tt * GK, GK)], ALU.mult).then_inc(acts_done, 1)
                    with eng.If(tt < NT - 1):
                        pick_best(eng, tt + 1)
                    with eng.Else():
                        eng.nop()
                    eng.wait_ge(acts_done, tt + 1)
                    eng.sem_inc(dve_turn, 1)
                    with eng.Fori(0, NG - NA) as g:
                        for n, j in enumerate(BY_DVE):
                            eng.wait_ge(row_in_slot[j], (turn(tt, g + NA, 1) + 1) * 16)
                            eng.wait_ge(vsum_step, tt * (DVE_ROWS + 1) + g * len(BY_DVE) + (n + 1))
                            eng.sem_inc(dve_turn, 1)
                            nc.vector.scalar_tensor_tensor(out=vsum, in0=slot[j], scalar=acts[:, bass.ds((g + NA) * GRP + j, 1)],
                                                           in1=vsum, op0=ALU.mult, op1=ALU.add).then_inc(vsum_step, 1)
                            eng.wait_ge(vsum_step, tt * (DVE_ROWS + 1) + g * len(BY_DVE) + (n + 2))
                            eng.sem_inc(slot_used[j], 1)
                    hrow = h2[:, bass.ds(tt * D, D)]
                    for j in range(GRP):
                        eng.wait_ge(slot_used[j], turn(tt, 0, 0) + (2 * NG + 1))
                    eng.sem_inc(dve_turn, 1)
                    nc.vector.tensor_tensor(hrow, hrow, bank[:, 0:2, :].rearrange("p b n -> p (b n)"), ALU.add)\
                      .then_inc(acc_free, 1)
                    eng.wait_ge(acc_free, tt + 2)
                    nc.vector.tensor_tensor(hrow, hrow, vsum, ALU.add).then_inc(h_added, 1)
                    eng.wait_ge(h_added, tt + 1)
                    eng.sem_inc(dve_turn, 1)

            @block.scalar
            def _(eng):
                def diagonal(tt, g, j):
                    eng.wait_ge(slot_used[j], turn(tt, g, 1) + 1)
                    nc.scalar.activation(diag[:, j, :], ident, ACT.Copy,
                                         scale=acts[:, bass.ds(g * GRP + j, 1)]).then_inc(diag_done, 1)

                exponentials(eng, 0)
                with eng.Fori(0, NT) as tt:
                    for j in range(GRP):
                        eng.wait_ge(slot_used[j], turn(tt, 0, 1) + 1)
                    nc.scalar.activation(acts, dots, ACT.Gelu_apprx_tanh).then_inc(gelu_done, 1)
                    eng.wait_ge(acts_done, tt + 1)
                    eng.sem_inc(act_turn, 1)
                    with eng.Fori(0, NA) as g:
                        for j in range(GRP):
                            diagonal(tt, g, j)
                    with eng.If(tt < NT - 1):
                        exponentials(eng, tt + 1)
                    with eng.Else():
                        eng.nop()
                    with eng.Fori(NA, NG) as g:
                        for j in BY_PE:
                            diagonal(tt, g, j)

            @block.tensor
            def _(eng):
                def add_row(tt, g, j, rows):
                    eng.wait_ge(diag_done, tt * PE_ROWS + rows)
                    eng.wait_ge(row_in_slot[j], (turn(tt, g, 1) + 1) * 16)
                    for n in range(2):
                        mm = nc.tensor.matmul(bank[:, n, :], diag[:, j, :], slot[j][:, n * NC:(n + 1) * NC],
                                              start=False, stop=False, skip_group_check=True)
                    mm.then_inc(slot_used[j], 1)

                with eng.Fori(0, NT) as tt:
                    eng.wait_ge(acc_free, tt + 1)
                    for n in range(2):
                        mm = nc.tensor.matmul(bank[:, n, :], const("zero"), tok[:, 0, n * NC:(n + 1) * NC],
                                              start=True, stop=False, skip_group_check=True)
                    mm.then_inc(acc_zero, 1)
                    with eng.Fori(0, NA) as g:
                        for j in range(GRP):
                            add_row(tt, g, j, g * GRP + (j + 1))
                    with eng.Fori(0, NG - NA) as g:
                        for n, j in enumerate(BY_PE):
                            add_row(tt, g + NA, j, g * len(BY_PE) + (NA * GRP + n + 1))

        pT = region(0, 2 * S).rearrange("p (k s) -> p k s", k=2)
        gsb = region(2 * S, 2 * D).rearrange("p (t d) -> p t d", t=2)
        at["late"] += 16
        pT_at = at["late"]

        def ple_loads(sp):
            load_chunk(sp, C_PE)
            load_chunk(sp, C_PE + 1)
            sp.dma_start(pT[:, :, :], t["p_T"].rearrange("(k p) s -> p k s", p=P)).then_inc(late_in, 16)
            sp.wait_ge(late_in, pT_at)
        normalise(h, NT, 0, param("g_ple"), tok, aT,
                  sp_work=ple_loads)
        pel, dvl = [], []
        for i in range(NT + 1):
            if i < NT:
                pel += [("gate", i, 0), ("gate", i, 1), ("emb", i, 0), ("emb", i, 1)]
                dvl += [("mul", i, 0), ("mul", i, 1), ("add", i)]
            if i:
                pel += [("t", i - 1, 0), ("t", i - 1, 1)]
                dvl += [("out", i - 1, 0), ("out", i - 1, 1)]
            if i < NT:
                dvl += [("rstd", i, 0), ("scale", i, 0), ("rstd", i, 1), ("scale", i, 1)]
        pe, dv = steps("pe", pel), steps("dve", dvl)
        ac = steps("act", [x for i in range(NT) for x in [("sig", i, 0), ("sig", i, 1)]
                           + [(w, i, r) for r in range(2) for w in ("sq", "sd")]])
        at["row"] += 16
        row_at = at["row"]

        def half(x, n):
            return x[:, n * NC:(n + 1) * NC]
        with nc.Block() as block:
            @block.sync
            def _(sp):
                sp.dma_start(grow[:, :], t["g_final"].rearrange("(o d) -> o d", o=1).to_broadcast([P, D])).then_inc(row_in, 16)
                for c, last_use in ((C_PG, ("gate", NT - 1, 0)), (C_PG + 1, ("gate", NT - 1, 1)), (C_PE, ("emb", NT - 1, 1))):
                    sp.wait_ge(pe_done, pe[last_use])
                    load_chunk(sp, c + 4)

            @block.tensor
            def _(eng):
                for c in (C_PG, C_PG + 1, C_PE):
                    wait_chunk(eng, c)
                for i in range(NT + 1):
                    if i < NT:
                        for n in range(2):
                            if i:
                                eng.wait_ge(act_done, ac["sig", i - 1, n])
                            for k in range(KD):
                                mm = nc.tensor.matmul(bank[:, n, :], aT[:, k, i * P:(i + 1) * P],
                                                      chunk_view(C_PG + n)[:, k, :], start=k == 0, stop=k == KD - 1)
                            mm.then_inc(pe_done, 1)
                        for n in range(2):
                            if i:
                                eng.wait_ge(dve_done, dv["mul", i - 1, n])
                            for k in range(PLE // P):
                                mm = nc.tensor.matmul(bank[:, 2 + n, :], pT[:, k, i * P:(i + 1) * P],
                                                      half(chunk_view(C_PE)[:, k, :], n), start=k == 0, stop=k == PLE // P - 1)
                            mm.then_inc(pe_done, 1)
                    if i:
                        eng.wait_ge(dve_done, dv["scale", i - 1, 1])
                        for n in range(2):
                            if i >= 3:
                                eng.wait_ge(dve_done, dv["out", i - 3, n])
                            for k in range(4):
                                kk = 4 * n + k
                                mm = nc.tensor.transpose(bank[:, 4 + (2 * (i - 1) + n) % 4, k * P:(k + 1) * P],
                                                         tok[:, i - 1, kk * P:(kk + 1) * P], ident)
                            mm.then_inc(pe_done, 1)

            @block.scalar
            def _(eng):
                for i in range(NT):
                    for n in range(2):
                        eng.wait_ge(pe_done, pe["gate", i, n])
                        if i >= 2:
                            eng.wait_ge(dve_done, dv["add", i - 2])
                        nc.scalar.activation(half(gsb[:, i % 2, :], n), bank[:, n, :], ACT.Sigmoid).then_inc(act_done, 1)
                    for r in range(2):
                        eng.wait_ge(dve_done, dv["scale", i, 0] if r else dv["add", i])
                        c = 12 * r + i
                        nc.scalar.activation(tok[:, i, :], h[:, i, :], ACT.Square, accum_out=stat[:, c:c + 1]).then_inc(act_done, 1)
                        eng.wait_ge(act_done, ac["sq", i, r])
                        nc.scalar.activation(stat[:, c + 4:c + 5], stat[:, c:c + 1], ACT.Sqrt, scale=1.0 / D,
                                             bias=const("eps", r, r + 1)).then_inc(act_done, 1)

            @block.vector
            def _(eng):
                eng.wait_ge(row_in, row_at)
                for i in range(NT + 1):
                    if i < NT:
                        g = gsb[:, i % 2, :]
                        for n in range(2):
                            eng.wait_ge(act_done, ac["sig", i, n])
                            eng.wait_ge(pe_done, pe["emb", i, n])
                            nc.vector.tensor_tensor(half(g, n), bank[:, 2 + n, :], half(g, n), ALU.mult).then_inc(dve_done, 1)
                        eng.wait_ge(dve_done, dv["mul", i, 1])
                        nc.vector.tensor_tensor(h[:, i, :], h[:, i, :], g, ALU.add).then_inc(dve_done, 1)
                    if i:
                        for n in range(2):
                            eng.wait_ge(pe_done, pe["t", i - 1, n])
                            nc.vector.tensor_tensor(aT[:, 4 * n:4 * n + 4, (i - 1) * P:i * P],
                                                    bank[:, 4 + (2 * (i - 1) + n) % 4, :].rearrange("p (k m) -> p k m", k=4),
                                                    over(param("g_mix_2", 4 * n, 4 * n + 4), P), ALU.mult).then_inc(dve_done, 1)
                    if i < NT:
                        for r in range(2):
                            c = 12 * r + i
                            eng.wait_ge(act_done, ac["sd", i, r])
                            nc.vector.reciprocal(stat[:, c + 8:c + 9], stat[:, c + 4:c + 5]).then_inc(dve_done, 1)
                            eng.wait_ge(dve_done, dv["rstd", i, r])
                            if r == 0:
                                ins = nc.vector.scalar_tensor_tensor(out=h[:, i, :], in0=h[:, i, :], scalar=stat[:, c + 8:c + 9],
                                                                     in1=grow[:, :], op0=ALU.mult, op1=ALU.mult)
                            else:
                                ins = nc.vector.tensor_scalar(tok[:, i, :], h[:, i, :], stat[:, c + 8:c + 9], None, ALU.mult)
                            ins.then_inc(dve_done, 1)

        qk = region(0, 8 * S).rearrange("p (c s) -> p c s", c=8)
        v2 = region(4096, NT * S).rearrange("p (t n) -> p t n", t=NT)
        LU = S + PADU
        uT = region(6144, 4 * LU).rearrange("p (g s) -> p g s", g=4)
        jobs = []
        for c in range(4):
            jobs.append(t_job(C_IN2, c * P, aT, S, "act",
                              lambda b, c=c: nc.scalar.activation(qk[:, c, :], bank[:, b, :], ACT.Copy, scale=HD ** -0.5)))
        for c in range(4):
            jobs.append(t_job(C_IN2 + 1, c * P, aT, S, "dve",
                              lambda b, c=c: nc.vector.tensor_copy(qk[:, 4 + c, :], bank[:, b, :])))
        for tt in range(NT):
            jobs.append(tok_job(C_IN2 + 2, 0, NC, aT, tt, "act",
                                lambda b, tt=tt: nc.scalar.activation(v2[:, tt, :], bank[:, b, :], ACT.Copy)))
        for g in range(4):
            jobs.append(t_job(C_IN2 + 3, g * P, aT, S, "dve",
                              lambda b, g=g: nc.vector.tensor_copy(uT[:, g, PADU:LU], bank[:, b, :])))
        dense(jobs)

        OFF = [0, NC, 2 * NC, 2 * NC - P]
        ZW = 10 * P
        zs = [region(8256 + i * ZW, ZW) for i in range(2)]
        sp_ = [region(8256 + (2 + i) * ZW, ZW) for i in range(2)]
        wt = [region(8256 + (4 + i) * ZW, ZW) for i in range(2)]
        pa = aT[:, :, :].rearrange("p k s -> p (k s)")
        pl = [pa[:, i * LU:(i + 1) * LU] for i in range(2)]
        pooled = [pa[:, 2 * LU + g * S:2 * LU + (g + 1) * S] for g in range(4)]
        wpool = grow[:, 0:4 * P].rearrange("p (g e) -> p g e", g=4)
        sqs = [uT[:, k, 0:S] for k in range(4)] + pooled
        at["row"] += 16
        row_at = at["row"]
        ZBANK, ABANK, OBANK, GBANK = 0, 3, 6, 7

        def flat(b0):
            return bank[:, b0:b0 + 3, :].rearrange("p b n -> p (b n)")[:, 0:ZW]

        def seg(x, i):
            return x[:, OFF[i]:OFF[i] + S - i * P]

        def zpart(b0, i):
            return bank[:, b0 + OFF[i] // NC, OFF[i] % NC:OFF[i] % NC + S - i * P]

        def diagonals(x):
            return (x[:, 0:2 * NC].rearrange("p (j n) -> p j n", j=2)[:, :, 0:P],
                    x[:, OFF[3]:OFF[3] + 2 * P].rearrange("p (j n) -> p j n", j=2))
        below = const("lt").rearrange("p (o n) -> p o n", o=1).to_broadcast([P, 2, P])

        nsum = [1, 2, 3, 4]
        POOL_AT = 2
        dvl = [("z", 0), ("sp", 0), ("mask", 0, 0), ("mask", 0, 1)]
        acl = [("abs", 0), ("e", 0), ("l", 0)]
        pel = [("z", 0)]
        for it in range(SBH + 1):
            nxt, here = it + 1 < SBH, it < SBH
            dvl += ([("z", it + 1)] if nxt else []) + ([("t1", it), ("t2", it)] if here else [])
            dvl += [("sp", it + 1), ("mask", it + 1, 0), ("mask", it + 1, 1)] if nxt else []
            dvl += [("wmask", it, 0), ("wmask", it, 1)] if here else ["prec"] + [("sn", k) for k in range(4, 8)]
            dvl += [("o", it - 1)] if it else []
            acl += [("sq", (it - 3) // 2)] if it in (3, 5, 7) else []
            acl += [("abs", it + 1), ("e", it + 1), ("l", it + 1)] if nxt else []
            acl += [("w", it)] if here else ["psd"]
            acl += [("po", it - POOL_AT), ("sq", 4 + it - POOL_AT)] if 0 <= it - POOL_AT < 4 else []
            pel += ([("z", it + 1)] if nxt else []) + ([("a", it)] if here else []) + ([("o", it - 1)] if it else [])
            pel += [("pool", it - POOL_AT)] if 0 <= it - POOL_AT < 4 else []
            pel += ["psum"] if it == SBH - 1 else []
        dv = steps("dve", dvl + ["srec"] + [("sn", k) for k in range(4)])
        ac = steps("act", acl + [("sq", 3), "ssd"])
        pe = steps("pe", pel + ["ssum"])
        pool_labels = []
        for g in range(4):
            pool_labels += [("win", g, i) for i in range(nsum[g])] + [("mean", g), ("edge", g), ("less", g)]
        po = steps("pool", ["upad"] + pool_labels)
        with nc.Block() as block:
            @block.sync
            def _(sp):
                sp.dma_start(wpool, t["w_pool_2"][0].rearrange("g c e -> c g e")).then_inc(row_in, 16)
                for i in range(LEAST_LIVE, NBP, NT):
                    sp.dma_start(y_dram[i * P:(i + NT) * P, :].rearrange("(t p) d -> p t d", p=P), h[:, :, :])\
                      .then_inc(rows_filled, 16)
                sp.wait_ge(rows_filled, 16 * (NBP - LEAST_LIVE) // NT)

            @block.gpsimd
            def _(eng):
                eng.memset(uT[:, :, 0:PADU], 0.0).then_inc(pool_done, 1)
                prev = po["upad"]
                for g, win in enumerate(WINS):
                    src = uT[:, g, :]
                    step_ = 1
                    for i in range(nsum[g]):
                        dst = pl[i % 2]
                        lo = 2 * step_ - 1
                        eng.wait_ge(pool_done, prev)
                        eng.tensor_tensor(dst[:, lo:LU], src[:, lo:LU], src[:, lo - step_:LU - step_], ALU.add)\
                           .then_inc(pool_done, 1)
                        prev = po["win", g, i]
                        src = dst
                        step_ *= 2
                    dst = pooled[g]
                    eng.wait_ge(pool_done, prev)
                    eng.tensor_scalar(dst[:, PADU:S], src[:, 2 * PADU:LU], 1.0 / win, None, ALU.mult).then_inc(pool_done, 1)
                    eng.tensor_tensor(dst[:, 0:PADU], src[:, PADU:2 * PADU],
                                      const("rcount", g * PADU, (g + 1) * PADU), ALU.mult).then_inc(pool_done, 1)
                    eng.wait_ge(pool_done, po["edge", g])
                    eng.tensor_tensor(dst, dst, uT[:, g, PADU:LU], ALU.subtract).then_inc(pool_done, 1)
                    prev = po["less", g]

            @block.tensor
            def _(eng):
                def z_of(hd):
                    if hd:
                        eng.wait_ge(dve_done, dv["z", hd - 1])
                    r = hd % 2 * HD
                    for i in range(4):
                        mm = nc.tensor.matmul(zpart(ZBANK, i), qk[r:r + HD, 4 + hd // 2, i * P:(i + 1) * P],
                                              qk[r:r + HD, hd // 2, i * P:S], start=True, stop=True)
                    mm.then_inc(pe_done, 1)

                def sums_of(hd):
                    eng.wait_ge(dve_done, dv["mask", hd, 1])
                    if hd:
                        eng.wait_ge(dve_done, dv["t2", hd - 1])
                    for i in range(4):
                        for j in range(i, 4):
                            dst = zpart(ABANK, i)[:, (j - i) * P:]
                            mm = nc.tensor.matmul(dst, const("gt") if j == i else const("ones"), seg(sp_[hd % 2], j),
                                                  start=j == i, stop=j == 3, skip_group_check=True)
                    mm.then_inc(pe_done, 1)

                def result_of(hd):
                    eng.wait_ge(dve_done, dv["wmask", hd, 1])
                    if hd:
                        eng.wait_ge(dve_done, dv["o", hd - 1])
                    r = hd % 2 * HD
                    for i in range(4):
                        mm = nc.tensor.matmul(bank[r:r + HD, OBANK, i * P:S], v2[:, i, hd * HD:(hd + 1) * HD],
                                              seg(wt[hd % 2], i), start=i == 0, stop=i == 3, skip_group_check=True)
                    mm.then_inc(pe_done, 1)

                def squares(b, ks):
                    for k in ks:
                        eng.wait_ge(act_done, ac["sq", k])
                        mm = nc.tensor.matmul(bank[:, b, :], const("ones"), sqs[k], start=k % 4 == 0, stop=k % 4 == 3)
                    mm.then_inc(pe_done, 1)

                z_of(0)
                for it in range(SBH + 1):
                    if it + 1 < SBH:
                        z_of(it + 1)
                    if it < SBH:
                        sums_of(it)
                    if it:
                        result_of(it - 1)
                    g = it - POOL_AT
                    if 0 <= g < 4:
                        if g == 0:
                            eng.wait_ge(row_in, row_at)
                        else:
                            eng.wait_ge(act_done, ac["po", g - 1])
                        eng.wait_ge(pool_done, po["less", g])
                        nc.tensor.matmul(bank[:, GBANK, :], wpool[:, g, :], pooled[g], start=True, stop=True)\
                          .then_inc(pe_done, 1)
                    if it == SBH - 1:
                        squares(GBANK, range(4, 8))
                squares(ZBANK, range(4))

            @block.scalar
            def _(eng):
                def softplus(hd):
                    s = hd % 2
                    eng.wait_ge(dve_done, dv["z", hd])
                    if hd >= 2:
                        eng.wait_ge(pe_done, pe["a", hd - 2])
                    nc.scalar.activation(sp_[s], zs[s], ACT.Abs).then_inc(act_done, 1)
                    eng.wait_ge(act_done, ac["abs", hd])
                    nc.scalar.activation(sp_[s], sp_[s], ACT.Exp, scale=-1.0).then_inc(act_done, 1)
                    eng.wait_ge(act_done, ac["e", hd])
                    nc.scalar.activation(sp_[s], sp_[s], ACT.Ln, bias=const("ones", 0, 1)).then_inc(act_done, 1)

                def square(k):
                    if k < 4:
                        eng.wait_ge(pool_done, po["less", 3])
                        eng.wait_ge(dve_done, dv["o", 2 * k + 1])
                    else:
                        eng.wait_ge(act_done, ac["po", k - 4])
                    nc.scalar.activation(sqs[k], mixT[:, k, :], ACT.Square).then_inc(act_done, 1)

                def deviation(n, b, name):
                    eng.wait_ge(pe_done, pe[name])
                    if n == 0:
                        eng.wait_ge(pe_done, pe["o", SBH - 1])
                    dst = v2[:, 0, :] if n == 0 else qk[:, 0, :]
                    nc.scalar.activation(dst, bank[:, b, :], ACT.Sqrt, scale=1.0 / S,
                                         bias=const("eps", 1, 2)).then_inc(act_done, 1)

                softplus(0)
                for it in range(SBH + 1):
                    if it in (3, 5, 7):
                        square((it - 3) // 2)
                    if it + 1 < SBH:
                        softplus(it + 1)
                    if it < SBH:
                        eng.wait_ge(dve_done, dv["t2", it])
                        nc.scalar.activation(wt[it % 2], wt[it % 2], ACT.Exp).then_inc(act_done, 1)
                    else:
                        deviation(1, GBANK, "psum")
                    g = it - POOL_AT
                    if 0 <= g < 4:
                        eng.wait_ge(pe_done, pe["pool", g])
                        nc.scalar.activation(mixT[:, 4 + g, :], bank[:, GBANK, :], ACT.Copy,
                                             scale=param("pool_scale", g, g + 1)).then_inc(act_done, 1)
                        square(4 + g)
                square(3)
                deviation(0, ZBANK, "ssum")

            @block.vector
            def _(eng):
                def logits(hd):
                    eng.wait_ge(pe_done, pe["z", hd])
                    if hd >= 2:
                        eng.wait_ge(dve_done, dv["t1", hd - 2])
                    nc.vector.tensor_copy(zs[hd % 2], flat(ZBANK)).then_inc(dve_done, 1)

                def mask(x):
                    for d in diagonals(x):
                        nc.vector.tensor_tensor(d, d, below, ALU.mult).then_inc(dve_done, 1)

                def softplus(hd):
                    s = hd % 2
                    eng.wait_ge(act_done, ac["l", hd])
                    eng.wait_ge(dve_done, dv["z", hd])
                    nc.vector.scalar_tensor_tensor(out=sp_[s], in0=zs[s], scalar=0.0, in1=sp_[s],
                                                   op0=ALU.max, op1=ALU.add).then_inc(dve_done, 1)
                    eng.wait_ge(dve_done, dv["sp", hd])
                    mask(sp_[s])

                def normed(ks, recip, dev):
                    for k in ks:
                        eng.wait_ge(dve_done, dv[recip])
                        g = param("g_sb", k, k + 1) if k < 4 else param("g_pool", k - 4, k - 3)
                        nc.vector.scalar_tensor_tensor(out=mixT[:, k, :], in0=mixT[:, k, :], scalar=g, in1=dev,
                                                       op0=ALU.mult, op1=ALU.mult).then_inc(dve_done, 1)

                logits(0)
                softplus(0)
                for it in range(SBH + 1):
                    s = it % 2
                    if it + 1 < SBH:
                        logits(it + 1)
                    if it < SBH:
                        eng.wait_ge(dve_done, dv["mask", it, 1])
                        if it >= 2:
                            eng.wait_ge(pe_done, pe["o", it - 2])
                        nc.vector.tensor_tensor(wt[s], zs[s], sp_[s], ALU.subtract).then_inc(dve_done, 1)
                        eng.wait_ge(dve_done, dv["t1", it])
                        eng.wait_ge(pe_done, pe["a", it])
                        nc.vector.tensor_tensor(wt[s], wt[s], flat(ABANK), ALU.subtract).then_inc(dve_done, 1)
                    if it + 1 < SBH:
                        softplus(it + 1)
                    if it < SBH:
                        eng.wait_ge(act_done, ac["w", it])
                        mask(wt[s])
                    else:
                        eng.wait_ge(act_done, ac["psd"])
                        nc.vector.reciprocal(qk[:, 0, :], qk[:, 0, :]).then_inc(dve_done, 1)
                        normed(range(4, 8), "prec", qk[:, 0, :])
                    if it:
                        hd = it - 1
                        eng.wait_ge(pe_done, pe["o", hd])
                        r = hd % 2 * HD
                        nc.vector.tensor_copy(mixT[r:r + HD, hd // 2, :], bank[r:r + HD, OBANK, :]).then_inc(dve_done, 1)
                eng.wait_ge(act_done, ac["ssd"])
                nc.vector.reciprocal(v2[:, 0, :], v2[:, 0, :]).then_inc(dve_done, 1)
                normed(range(4), "srec", v2[:, 0, :])

        mem = region(0, TM * D).rearrange("p (t d) -> p t d", t=TM)
        memT = region(2048, KD * NMEM).rearrange("p (k m) -> p k m", k=KD)
        kmT = region(4096, KD * NMEM).rearrange("p (k m) -> p k m", k=KD)
        vm = region(6144, TM * D).rearrange("p (t d) -> p t d", t=TM)
        qm = region(8192, KD * S).rearrange("p (k s) -> p k s", k=KD)
        prob = region(12288, NT * MH * NMEM).rearrange("p (t h m) -> p t h m", t=NT, h=MH)
        rows = region(12288, NT * D).rearrange("p (t d) -> p t d", t=NT)
        mem_rows = region(8192, TM * D).rearrange("p (t d) -> p t d", t=TM)
        at["late"] += 16
        project_and_normalise(C_OUT2, mixT, rows, 1, param("g_mem_q"), aT,
                              sp_work=lambda sp: sp.dma_start(mem[:, :, :], t["mem_2"][0].rearrange("(t p) d -> p t d", p=P))
                              .then_inc(late_in, 16),
                              aside=[(mem[:, i, :], mem_rows[:, i, :], param("g_mem_kv"), memT[:, :, i * P:(i + 1) * P])
                                     for i in range(TM)])
        jobs = []
        for c in range(8):
            jobs.append(t_job(C_KV + c // 4, c % 4 * P, memT, NMEM, "act",
                              lambda b, c=c: nc.scalar.activation(kmT[:, c, :], bank[:, b, 0:NMEM], ACT.Copy)))
        for n in range(2):
            for mt in range(TM):
                jobs.append(tok_job(C_KV + 2 + n, 0, NC, memT, mt, "dve",
                                    lambda b, mt=mt, n=n: nc.vector.tensor_copy(vm[:, mt, n * NC:(n + 1) * NC], bank[:, b, :])))
        dense(jobs + [t_job(C_MQ + c // 4, c % 4 * P, aT, S, "act" if c % 2 else "dve",
                     (lambda b, c=c: nc.scalar.activation(qm[:, c, :], bank[:, b, :], ACT.Copy)) if c % 2 else
                     (lambda b, c=c: nc.vector.tensor_copy(qm[:, c, :], bank[:, b, :]))) for c in range(8)])

        SCALE = (D // MH) ** -0.5
        units = [(tt, half) for tt in range(NT) for half in range(2)]
        pTt = aT[:, :, :].rearrange("p (h m) s -> p h m s", h=MH)
        mx, nmx, rs, ri = stat[:, 0:16], stat[:, 16:32], stat[:, 32:48], stat[:, 48:64]
        pe = steps("pe", [("s", u) for u in range(8)] + [("t", hd, mt) for hd in range(MH) for mt in range(TM)]
                   + [("o", c) for c in range(8)])
        dv = steps("dve", [x for u in range(8) for x in (("max", u), ("neg", u))] + ["rec"]
                   + [("p", u) for u in range(8)] + [("t", k) for k in range(0, 8, 2)] + [("o", c) for c in range(0, 8, 2)])
        ac = steps("act", [("e", u, j) for u in range(8) for j in range(2)]
                   + [("t", k) for k in range(1, 8, 2)] + [("o", c) for c in range(1, 8, 2)])
        with nc.Block() as block:
            @block.tensor
            def _(eng):
                for u, (tt, half) in enumerate(units):
                    for j in range(2):
                        hd = 2 * half + j
                        for k in range(2):
                            mm = nc.tensor.matmul(bank[:, u, j * NMEM:(j + 1) * NMEM],
                                                  qm[:, 2 * hd + k, tt * P:(tt + 1) * P], kmT[:, 2 * hd + k, :],
                                                  start=k == 0, stop=k == 1)
                    mm.then_inc(pe_done, 1)
                for hd in range(MH):
                    for mt in range(TM):
                        b = hd * TM + mt
                        for tt in range(NT):
                            eng.wait_ge(dve_done, dv["p", 7])
                            mm = nc.tensor.transpose(bank[:, b, tt * P:(tt + 1) * P], prob[:, tt, hd, mt * P:(mt + 1) * P], ident)
                        mm.then_inc(pe_done, 1)
                for c in range(8):
                    hd = c // 2
                    for mt in range(TM):
                        k = hd * TM + mt
                        eng.wait_ge(*((dve_done, dv["t", k]) if k % 2 == 0 else (act_done, ac["t", k])))
                    if c % 2 == 0:
                        eng.wait_ge(dve_done, dv["t", c])
                    else:
                        eng.wait_ge(act_done, ac["t", c])
                    for mt in range(TM):
                        mm = nc.tensor.matmul(bank[:, c, :], vm[:, mt, c * P:(c + 1) * P], pTt[:, hd, mt, :],
                                              start=mt == 0, stop=mt == TM - 1)
                    mm.then_inc(pe_done, 1)

            @block.vector
            def _(eng):
                for u, (tt, half) in enumerate(units):
                    eng.wait_ge(pe_done, pe["s", u])
                    nc.vector.tensor_reduce(mx[:, 2 * u:2 * u + 2], bank[:, u, :].rearrange("p (j m) -> p j m", j=2),
                                            AX, ALU.max).then_inc(dve_done, 1)
                    eng.wait_ge(dve_done, dv["max", u])
                    nc.vector.tensor_scalar(nmx[:, 2 * u:2 * u + 2], mx[:, 2 * u:2 * u + 2], -SCALE, None, ALU.mult)\
                      .then_inc(dve_done, 1)
                eng.wait_ge(act_done, ac["e", 7, 1])
                nc.vector.reciprocal(ri, rs).then_inc(dve_done, 1)
                eng.wait_ge(dve_done, dv["rec"])
                for u, (tt, half) in enumerate(units):
                    pr = prob[:, tt, 2 * half:2 * half + 2, :]
                    nc.vector.tensor_tensor(pr, pr, over(ri[:, 2 * u:2 * u + 2], NMEM), ALU.mult).then_inc(dve_done, 1)
                for k in range(0, 8, 2):
                    eng.wait_ge(pe_done, pe["t", k // TM, k % TM])
                    nc.vector.tensor_copy(pTt[:, k // TM, k % TM, :], bank[:, k, :]).then_inc(dve_done, 1)
                for c in range(0, 8, 2):
                    eng.wait_ge(pe_done, pe["o", c])
                    nc.vector.tensor_copy(mixT[:, c, :], bank[:, c, :]).then_inc(dve_done, 1)

            @block.scalar
            def _(eng):
                for u, (tt, half) in enumerate(units):
                    eng.wait_ge(dve_done, dv["neg", u])
                    for j in range(2):
                        nc.scalar.activation(prob[:, tt, 2 * half + j, :], bank[:, u, j * NMEM:(j + 1) * NMEM], ACT.Exp,
                                             scale=SCALE, bias=nmx[:, 2 * u + j:2 * u + j + 1],
                                             accum_out=rs[:, 2 * u + j:2 * u + j + 1]).then_inc(act_done, 1)
                for k in range(1, 8, 2):
                    eng.wait_ge(pe_done, pe["t", k // TM, k % TM])
                    nc.scalar.activation(pTt[:, k // TM, k % TM, :], bank[:, k, :], ACT.Copy).then_inc(act_done, 1)
                for c in range(1, 8, 2):
                    eng.wait_ge(pe_done, pe["o", c])
                    nc.scalar.activation(mixT[:, c, :], bank[:, c, :], ACT.Copy).then_inc(act_done, 1)

        o = 0
        wr = region(o, KD * NE).rearrange("p (k e) -> p k e", k=KD)
        o += KD * NE
        br = region(o, NE)
        o += NE
        bexp = X[0:3 * NE, o:o + 3 * D]
        o += 3 * D
        bh = region(o, 3 * D // 2).bitcast(BF16)[0:3 * NE, :]
        o += 3 * D // 2
        b3 = sb("b3", [3 * NE, 3 * D], BF16)
        at["late"] += 48 + 32
        r_at = at["late"]
        po = steps("pool", ["hi", "r1", "mid", "r2", "lo", "midc"])

        def router_loads(sp):
            sp.dma_start(wr[:, :, :], t["w_router_2"][0].rearrange("(k p) e -> p k e", p=P)).then_inc(late_in, 16)
            sp.dma_start(br[:, :], t["b_router_2"][0:1, :].to_broadcast([P, NE])).then_inc(late_in, 16)
            for i in range(3):
                sp.dma_start(bexp[i * NE:(i + 1) * NE, :], t["b_expert"][:, :]).then_inc(late_in, 16)

        def split_biases(eng):
            B = bexp
            eng.wait_ge(late_in, r_at)
            eng.tensor_copy(b3[:, :], B).then_inc(pool_done, 1)
            eng.wait_ge(pool_done, po["hi"])
            eng.tensor_tensor(B, B, b3[:, :], ALU.subtract).then_inc(pool_done, 1)
            eng.wait_ge(pool_done, po["r1"])
            eng.tensor_copy(bh, B).then_inc(pool_done, 1)
            eng.wait_ge(pool_done, po["mid"])
            eng.tensor_tensor(B, B, bh, ALU.subtract).then_inc(pool_done, 1)
            eng.wait_ge(pool_done, po["r2"])
            eng.tensor_copy(b3[2 * NE:3 * NE, :], B[2 * NE:3 * NE, :]).then_inc(pool_done, 1)
            eng.tensor_copy(b3[NE:2 * NE, :], bh[NE:2 * NE, :]).then_inc(pool_done, 1)

        project_and_normalise(C_MO, mixT, rows, 1, None, aT, row_ap=t["g_ffn_2"][0:1, :], sp_work=router_loads,
                              pool_work=split_biases)

        lg = region(o, NT * NE).rearrange("p (t e) -> p t e", t=NT)
        o += NT * NE
        tv = region(o, NT * 8).rearrange("p (t k) -> p t k", t=NT)
        o += NT * 8
        ti = region(o, NT * 8).bitcast(U32).rearrange("p (t k) -> p t k", t=NT)
        o += NT * 8
        tf = region(o, NT * 8).rearrange("p (t k) -> p t k", t=NT)
        o += NT * 8
        oh = region(o, NT * EK * NE).rearrange("p (t k e) -> p t k e", t=NT, k=EK)
        o += NT * EK * NE
        oh2 = region(o, NT * EK * NE).rearrange("p (t k e) -> p t k e", t=NT, k=EK)
        o += NT * EK * NE
        M = region(o, NT * NE).rearrange("p (t e) -> p t e", t=NT)
        o += NT * NE
        R = region(o, NT * NE)
        o += NT * NE
        q4 = region(o, NT * NE)
        o += NT * NE
        tq = region(o, NT * NE)
        o += NT * NE
        rowhot = region(o, NT * EK * P).rearrange("p (c r) -> p c r", c=NT * EK)
        o += NT * EK * P
        blkhot = region(o, NT * EK * NBP).rearrange("p (c b) -> p c b", c=NT * EK)
        o += NT * EK * NBP
        nb = region(o, NE)
        o += NE
        gsum = stat[:, 32:32 + 2 * NT]
        nb2 = region(o, NE)
        o += NE
        bend = region(o, NE)
        o += NE
        bst = region(o, NE)
        o += NE
        cmpb = region(o, NBP * NE).rearrange("p (b e) -> p b e", b=NBP)
        o += NBP * NE
        rows = region(12288, NT * D).rearrange("p (t d) -> p t d", t=NT)
        assert o <= 12288
        gk = sb("gk", [P, NT * EK])
        srow = sb("srow", [P, NT * EK], I32)
        blkf = sb("blkf", [P, NBP + 1])
        blki = sb("blki", [P, NBP + 1], I32)
        live = sb("live", [P, 1], I32)
        slots = sb("slots", [P, NBP + 1], I32)
        dvl = ["lg"] + [("mx", i) for i in range(NT)] + [("ix", i) for i in range(NT)] + ["tf", "tsub"]
        dvl += [("oh", i) for i in range(NT)] + ["M"]
        dvl += ["nb0", "nb1", "nb2", "nb3", "bend", "bst", "live", "cmp", "blkf", "blkm", "blki"]
        dvl += ["R", "q1", "q2", "q2a", "q3", "q3a", "p", "bq"]
        dvl += ["selr", "row", "rowhot", "selq", "blk", "blkeq", "blkhot", "frow", "srow"]
        dvl += ["esum", "erec", "gk", "slots"]
        dv = steps("dve", dvl)
        ac = steps("act", ["exp"])
        pe = steps("pe", ["lg", "cnt", "rank", "slots"])
        ws = [wring[i][:, :] for i in range(4)] + [region(0, KD * NC), region(KD * NC, KD * NC)]
        w1s = [w.rearrange("p (k n) -> p k n", k=KD) for w in ws[0:4]]
        w2s = [w.rearrange("p (k n) -> p k n", k=4) for w in ws[4:6]]
        o = 2 * KD * NC
        xg = region(o, D)
        gsb_ = region(o + D, D)
        usb = region(o + 2 * D, D)
        act_ = region(o + 3 * D, D)
        ysb = region(o + 4 * D, D)
        ohb = X[0:3 * NE, o + 5 * D:o + 5 * D + P // 2].bitcast(BF16)
        curs = region(o + 5 * D + P, 1).bitcast(I32)
        xT = aT[:, 0:2, :].rearrange("p k s -> p (k s)").rearrange("p (k m) -> p k m", k=KD)
        hT = aT[:, 2:4, :].rearrange("p k s -> p (k s)").rearrange("p (k m) -> p k m", k=KD)
        w1_in = [sem(f"w1_in{i}") for i in range(4)]
        w2_in = [sem(f"w2_in{i}") for i in range(2)]
        rows_in = sem("rows_in")
        curs_ready = sem("curs_ready")
        x_t = sem("x_t")
        x_e = sem("x_e")
        oh_ready = sem("oh_ready")
        gu_done = sem("gu_done")
        gate_ok = sem("gate_ok")
        up_ok = sem("up_ok")
        sig_ok = sem("sig_ok")
        mul_ok = sem("mul_ok")
        act_ok = sem("act_ok")
        h_t = sem("h_t")
        h_e = sem("h_e")
        y_done = sem("y_done")
        y_out = sem("y_out")
        y_st = sem("y_st")
        all_stored = sem("all_stored")
        we1, we2 = t["w_expert_in_2"][0], t["w_expert_out_2"][0]
        GU = [0, 2 * 512, 512, 3 * 512]
        HB, GB, YB = 0, 2, 6


        def load_w1(sp, e, c):
            sp.dma_start(w1s[c], we1[bass.ds(e, 1), :, GU[c]:GU[c] + NC]
                         .rearrange("o (k p) n -> p (o k) n", p=P)).then_inc(w1_in[c], 16)

        def load_w2(sp, e, c):
            sp.dma_start(w2s[c], we2[bass.ds(e, 1), c * NC:(c + 1) * NC, :]
                         .rearrange("o (k p) n -> p (o k) n", p=P)).then_inc(w2_in[c], 16)

        rows_out = sem("rows_out")
        with nc.Block() as block:
            @block.sync
            def _(sp):
                sp.dma_start(xn_dram.rearrange("(t p) d -> p t d", p=P), rows[:, :, :]).then_inc(rows_out, 16)
                sp.wait_ge(dve_done, dv["blki"])
                e = sp.value_load(blki[0:1, 0:1], min_val=0, max_val=NE - 1)
                for c in range(4):
                    load_w1(sp, e, c)
                sp.wait_ge(rows_out, 16)

            @block.tensor
            def _(eng):
                eng.wait_ge(late_in, r_at)
                for tt in range(NT):
                    for k in range(KD):
                        mm = nc.tensor.matmul(bank[:, 0, tt * NE:(tt + 1) * NE], aT[:, k, tt * P:(tt + 1) * P], wr[:, k, :],
                                              start=k == 0, stop=k == KD - 1)
                mm.then_inc(pe_done, 1)
                eng.wait_ge(dve_done, dv["M"])
                for j in range(NT):
                    mm = nc.tensor.matmul(bank[:, 2, 0:NE], const("ones"), M[:, j, :], start=j == 0, stop=j == NT - 1)
                mm.then_inc(pe_done, 1)
                for tt in range(NT):
                    for j in range(tt + 1):
                        mm = nc.tensor.matmul(bank[:, 1, tt * NE:(tt + 1) * NE], const("lt") if j == tt else const("ones"),
                                              M[:, j, :], start=j == 0, stop=j == tt)
                mm.then_inc(pe_done, 1)
                eng.wait_ge(dve_done, dv["blkhot"])
                for c in range(NT * EK):
                    mm = nc.tensor.matmul(bank[:, 3, 0:NBP], rowhot[:, c, :], blkhot[:, c, :], start=c == 0,
                                          stop=c == NT * EK - 1)
                mm.then_inc(pe_done, 1)

            @block.scalar
            def _(eng):
                eng.wait_ge(dve_done, dv["tsub"])
                nc.scalar.activation(tv[:, :, EK:2 * EK], tv[:, :, EK:2 * EK], ACT.Exp).then_inc(act_done, 1)

            @block.vector
            def _(eng):
                eng.wait_ge(late_in, r_at)
                eng.wait_ge(pe_done, pe["lg"])
                nc.vector.tensor_tensor(lg, bank[:, 0, 0:NT * NE].rearrange("p (t e) -> p t e", t=NT),
                                        over_t(br[:, :]), ALU.add).then_inc(dve_done, 1)
                eng.wait_ge(dve_done, dv["lg"])
                for i in range(NT):
                    nc.vector.max(tv[:, i, :], lg[:, i, :]).then_inc(dve_done, 1)
                for i in range(NT):
                    eng.wait_ge(dve_done, dv["mx", i])
                    nc.vector.max_index(ti[:, i, :], tv[:, i, :], lg[:, i, :]).then_inc(dve_done, 1)
                eng.wait_ge(dve_done, dv["ix", NT - 1])
                nc.vector.tensor_copy(tf, ti).then_inc(dve_done, 1)
                nc.vector.tensor_tensor(tv[:, :, EK:2 * EK], tv[:, :, 0:EK], tv[:, :, 0:1].to_broadcast([P, NT, EK]), ALU.subtract)\
                  .then_inc(dve_done, 1)
                eng.wait_ge(dve_done, dv["tf"])
                for i in range(NT):
                    nc.vector.tensor_tensor(oh[:, i, :, :], over(tf[:, i, 0:EK], NE),
                                            over_t(const("iota", 0, NE)), ALU.is_equal).then_inc(dve_done, 1)
                eng.wait_ge(dve_done, dv["oh", NT - 1])
                nc.vector.tensor_reduce(M, oh.rearrange("p t k e -> p t e k"), AX, ALU.add).then_inc(dve_done, 1)
                eng.wait_ge(pe_done, pe["cnt"])
                cnt = bank[:, 2, 0:NE]
                nc.vector.tensor_scalar(nb, cnt, 0.0, None, ALU.is_gt).then_inc(dve_done, 1)
                prev, a, b = "nb0", nb, nb2
                for j in range(1, 4):
                    eng.wait_ge(dve_done, dv[prev])
                    nc.vector.scalar_tensor_tensor(out=b, in0=cnt, scalar=float(P * j), in1=a, op0=ALU.is_gt, op1=ALU.add)\
                      .then_inc(dve_done, 1)
                    prev, a, b = f"nb{j}", b, a
                eng.wait_ge(dve_done, dv["nb3"])
                nc.vector.tensor_tensor_scan(out=bend, data0=const("ones", 0, NE), data1=a, initial=0.0,
                                             op0=ALU.mult, op1=ALU.add).then_inc(dve_done, 1)
                eng.wait_ge(dve_done, dv["bend"])
                nc.vector.tensor_tensor(bst, bend, a, ALU.subtract).then_inc(dve_done, 1)
                nc.vector.tensor_copy(live[:, :], bend[:, NE - 1:NE]).then_inc(dve_done, 1)
                nc.vector.tensor_tensor(cmpb, bend.rearrange("p (o e) -> p o e", o=1).to_broadcast([P, NBP, NE]),
                                        over(const("iota", 0, NBP), NE), ALU.is_le).then_inc(dve_done, 1)
                eng.wait_ge(dve_done, dv["cmp"])
                nc.vector.tensor_reduce(blkf[:, 0:NBP], cmpb, AX, ALU.add).then_inc(dve_done, 1)
                eng.wait_ge(dve_done, dv["blkf"])
                nc.vector.tensor_scalar(blkf[:, 0:NBP], blkf[:, 0:NBP], float(NE - 1), None, ALU.min).then_inc(dve_done, 1)
                eng.wait_ge(dve_done, dv["blkm"])
                nc.vector.tensor_copy(blki[:, 0:NBP], blkf[:, 0:NBP]).then_inc(dve_done, 1)
                eng.wait_ge(pe_done, pe["rank"])
                nc.vector.tensor_copy(R, bank[:, 1, 0:NT * NE]).then_inc(dve_done, 1)
                eng.wait_ge(dve_done, dv["R"])
                nc.vector.tensor_scalar(q4, R, float(P), None, ALU.is_ge).then_inc(dve_done, 1)
                eng.wait_ge(dve_done, dv["q1"])
                nc.vector.tensor_scalar(tq, R, float(2 * P), None, ALU.is_ge).then_inc(dve_done, 1)
                eng.wait_ge(dve_done, dv["q2"])
                nc.vector.tensor_tensor(q4, q4, tq, ALU.add).then_inc(dve_done, 1)
                eng.wait_ge(dve_done, dv["q2a"])
                nc.vector.tensor_scalar(tq, R, float(3 * P), None, ALU.is_ge).then_inc(dve_done, 1)
                eng.wait_ge(dve_done, dv["q3"])
                nc.vector.tensor_tensor(q4, q4, tq, ALU.add).then_inc(dve_done, 1)
                eng.wait_ge(dve_done, dv["q3a"])
                nc.vector.scalar_tensor_tensor(out=R, in0=q4, scalar=float(-P), in1=R, op0=ALU.mult, op1=ALU.add)\
                  .then_inc(dve_done, 1)
                nc.vector.tensor_tensor(q4.rearrange("p (t e) -> p t e", t=NT), q4.rearrange("p (t e) -> p t e", t=NT),
                                        over_t(bst), ALU.add).then_inc(dve_done, 1)
                eng.wait_ge(dve_done, dv["bq"])
                rsel, qsel, frow = stat[:, 0:16], stat[:, 16:32], stat[:, 40:56]
                for src, dst, l1, l2 in ((R, rsel, "selr", "row"), (q4, qsel, "selq", "blk")):
                    s3 = src.rearrange("p (t o e) -> p t o e", t=NT, o=1).to_broadcast([P, NT, EK, NE])
                    nc.vector.tensor_tensor(oh2, oh, s3, ALU.mult).then_inc(dve_done, 1)
                    eng.wait_ge(dve_done, dv[l1])
                    nc.vector.tensor_reduce(dst, oh2.rearrange("p t k e -> p (t k) e"), AX, ALU.add).then_inc(dve_done, 1)
                    eng.wait_ge(dve_done, dv[l2])
                    if l2 == "row":
                        nc.vector.tensor_tensor(rowhot, const("iota").rearrange("p (o r) -> p o r", o=1)
                                                .to_broadcast([P, NT * EK, P]), over(dst, P), ALU.is_equal).then_inc(dve_done, 1)
                    else:
                        nc.vector.tensor_tensor(blkhot, const("iota", 0, NBP).rearrange("p (o r) -> p o r", o=1)
                                                .to_broadcast([P, NT * EK, NBP]), over(dst, NBP), ALU.is_equal).then_inc(dve_done, 1)
                eng.wait_ge(dve_done, dv["blkeq"])
                bh4 = blkhot.rearrange("p (t k) b -> p t (k b)", t=NT)
                nc.vector.tensor_tensor(bh4, bh4, over(const("tok"), EK * NBP), ALU.mult).then_inc(dve_done, 1)
                nc.vector.scalar_tensor_tensor(out=frow, in0=qsel, scalar=float(P), in1=rsel, op0=ALU.mult, op1=ALU.add)\
                  .then_inc(dve_done, 1)
                eng.wait_ge(dve_done, dv["frow"])
                nc.vector.tensor_copy(srow[:, :], frow).then_inc(dve_done, 1)
                eng.wait_ge(act_done, ac["exp"])
                nc.vector.tensor_reduce(gsum[:, 0:NT], tv[:, :, EK:2 * EK], AX, ALU.add).then_inc(dve_done, 1)
                eng.wait_ge(dve_done, dv["esum"])
                nc.vector.reciprocal(gsum[:, NT:2 * NT], gsum[:, 0:NT]).then_inc(dve_done, 1)
                eng.wait_ge(dve_done, dv["erec"])
                nc.vector.tensor_tensor(gk[:, :].rearrange("p (t k) -> p t k", t=NT), tv[:, :, EK:2 * EK],
                                        over(gsum[:, NT:2 * NT], EK), ALU.mult).then_inc(dve_done, 1)
                eng.wait_ge(pe_done, pe["slots"])
                nc.vector.tensor_copy(slots[:, 0:NBP], bank[:, 3, 0:NBP]).then_inc(dve_done, 1)

        def each_block(eng, body, ahead=0):
            n = eng.value_load(live[0:1, 0:1], min_val=1, max_val=NBLK)
            with eng.Fori(0, NBP // BATCH) as batch:
                with eng.If(batch * BATCH + ahead < n):
                    with eng.Fori(0, BATCH) as i:
                        b = batch * BATCH + i
                        with eng.If(b + ahead < n):
                            body(b)
                        with eng.Else():
                            eng.nop()
                with eng.Else():
                    eng.nop()
            return n

        with nc.Block() as block:
            @block.sync
            def _(eng):
                e = eng.value_load(blki[0:1, 0:1], min_val=0, max_val=NE - 1)
                for c in range(2):
                    load_w2(eng, e, c)

                def body(b):
                    e = eng.value_load(blki[0:1, bass.ds(b + 1, 1)], min_val=0, max_val=NE - 1)
                    for c in range(4):
                        eng.wait_ge(gu_done, b * 4 + (c + 1))
                        load_w1(eng, e, c)
                    for c in range(2):
                        eng.wait_ge(y_done, b * 2 + (c + 1))
                        load_w2(eng, e, c)
                each_block(eng, body, ahead=1)

            @block.gpsimd
            def _(eng):
                def gather(col, turn):
                    eng.tensor_copy(curs, slots[:, col]).then_inc(curs_ready, 1)
                    eng.wait_ge(curs_ready, turn)
                    eng.sem_inc(pool_turn, 1)
                    eng.indirect_dma_start(xg, None, xn_dram, bass.IndirectOffsetOnAxis(ap=curs, axis=0))\
                       .then_inc(rows_in, 16)
                gather(slice(0, 1), 1)

                def body(b):
                    eng.wait_ge(x_t, b * 2 + 2)
                    eng.sem_inc(pool_turn, 1)
                    gather(bass.ds(b + 1, 1), b + 2)
                each_block(eng, body)

            @block.tensor
            def _(eng):
                def transpose_rows():
                    for half in range(2):
                        for k in range(4):
                            kk = half * 4 + k
                            mm = nc.tensor.transpose(bank[:, GB + half, k * P:(k + 1) * P], xg[:, kk * P:(kk + 1) * P], ident)
                        mm.then_inc(x_t, 1)

                def transpose_act(half):
                    for k in range(4):
                        kk = half * 4 + k
                        mm = nc.tensor.transpose(bank[:, HB + half, k * P:(k + 1) * P], act_[:, kk * P:(kk + 1) * P], ident)
                    mm.then_inc(h_t, 1)

                def down(half, ks):
                    for k in ks:
                        for n in range(2):
                            mm = nc.tensor.matmul(bank[:, YB + n, :], hT[:, half * 4 + k, :],
                                                  w2s[half][:, k, n * NC:(n + 1) * NC], start=False,
                                                  stop=half == 1 and k == 3, skip_group_check=True)
                    return mm

                eng.wait_ge(rows_in, 16)
                transpose_rows()

                def body(b):
                    for c in range(4):
                        eng.wait_ge(w1_in[c], b * 16 + 16)
                        if c == 0:
                            eng.wait_ge(x_e, b * 2 + 2)
                        for k in range(KD):
                            nc.tensor.matmul(bank[:, GB + c, :], xT[:, k, :], w1s[c][:, k, :], start=k == 0, stop=False)
                        if c == 0:
                            eng.wait_ge(oh_ready, b + 1)
                        nc.tensor.matmul(bank[:, GB + c, :], ohb, b3[:, GU[c]:GU[c] + NC],
                                         start=False, stop=True).then_inc(gu_done, 1)
                        if c == 2:
                            eng.wait_ge(act_ok, b * 2 + 1)
                            transpose_act(0)
                    eng.wait_ge(rows_in, b * 16 + 32)
                    transpose_rows()
                    eng.wait_ge(y_out, b * 2 + 2)
                    for n in range(2):
                        nc.tensor.matmul(bank[:, YB + n, :], ohb, b3[:, 2 * FF + n * NC:2 * FF + (n + 1) * NC],
                                         start=True, stop=False, skip_group_check=True)
                    eng.wait_ge(h_e, b * 2 + 1)
                    eng.wait_ge(w2_in[0], b * 16 + 16)
                    down(0, (0, 1))
                    eng.wait_ge(act_ok, b * 2 + 2)
                    transpose_act(1)
                    down(0, (2, 3)).then_inc(y_done, 1)
                    eng.wait_ge(h_e, b * 2 + 2)
                    eng.wait_ge(w2_in[1], b * 16 + 16)
                    down(1, range(4)).then_inc(y_done, 1)
                each_block(eng, body)

            @block.scalar
            def _(eng):
                eng.sem_inc(y_out, 1)

                def copy_rows(count):
                    eng.wait_ge(x_t, count)
                    nc.scalar.activation(xT[:, 4:8, :], bank[:, GB + 1, :].rearrange("p (k m) -> p k m", k=4), ACT.Copy)\
                      .then_inc(x_e, 1)
                copy_rows(2)

                def body(b):
                    for half in range(2):
                        eng.wait_ge(gate_ok, b * 2 + half + 1)
                        nc.scalar.activation(act_[:, half * NC:(half + 1) * NC], gsb_[:, half * NC:(half + 1) * NC],
                                             ACT.Sigmoid, scale=1.702).then_inc(sig_ok, 1)
                        if half:
                            copy_rows(b * 2 + 4)
                        eng.wait_ge(h_t, b * 2 + half + 1)
                        nc.scalar.activation(hT[:, half * 4:half * 4 + 4, :],
                                             bank[:, HB + half, :].rearrange("p (k m) -> p k m", k=4), ACT.Copy).then_inc(h_e, 1)
                    eng.wait_ge(y_done, b * 2 + 2)
                    eng.wait_ge(y_st, b * 16 + 16)
                    nc.scalar.activation(ysb[:, 0:NC], bank[:, YB, :], ACT.Copy).then_inc(y_out, 1)
                    eng.wait_ge(y_out, b * 2 + 4)
                    eng.dma_start(y_dram[bass.ds(b * P, P), :], ysb).then_inc(y_st, 16)
                n = each_block(eng, body)
                eng.wait_ge(y_st, n * 16 + 16)
                eng.sem_inc(all_stored, 1)

            @block.vector
            def _(eng):
                eng.sem_inc(y_out, 1)
                eng.sem_inc(y_st, 16)

                def pick(col):
                    nc.vector.tensor_scalar(ohb, cst[0:3 * NE, _C["emod"][0]:_C["emod"][0] + P],
                                            blkf[0:3 * NE, col], None, ALU.is_equal).then_inc(oh_ready, 1)

                def copy_rows(count):
                    eng.wait_ge(x_t, count)
                    nc.vector.tensor_copy(xT[:, 0:4, :], bank[:, GB, :].rearrange("p (k m) -> p k m", k=4)).then_inc(x_e, 1)
                pick(slice(0, 1))
                copy_rows(1)

                def body(b):
                    for half in range(2):
                        lo, hi = half * NC, (half + 1) * NC
                        eng.wait_ge(gu_done, b * 4 + 2 * half + 1)
                        nc.vector.tensor_scalar(gsb_[:, lo:hi], bank[:, GB + 2 * half, :], 7.0, None, ALU.min).then_inc(gate_ok, 1)
                        eng.wait_ge(gu_done, b * 4 + 2 * half + 2)
                        nc.vector.tensor_scalar(usb[:, lo:hi], bank[:, GB + 2 * half + 1, :], 7.0, -7.0, ALU.min, ALU.max)\
                          .then_inc(up_ok, 1)
                        eng.wait_ge(up_ok, b * 2 + half + 1)
                        nc.vector.scalar_tensor_tensor(out=usb[:, lo:hi], in0=usb[:, lo:hi], scalar=1.0, in1=gsb_[:, lo:hi],
                                                       op0=ALU.add, op1=ALU.mult).then_inc(mul_ok, 1)
                        eng.wait_ge(mul_ok, b * 2 + half + 1)
                        eng.wait_ge(sig_ok, b * 2 + half + 1)
                        nc.vector.tensor_tensor(act_[:, lo:hi], act_[:, lo:hi], usb[:, lo:hi], ALU.mult).then_inc(act_ok, 1)
                    copy_rows(b * 2 + 3)
                    eng.wait_ge(y_done, b * 2 + 2)
                    pick(bass.ds(b + 1, 1))
                    eng.wait_ge(y_st, b * 16 + 16)
                    nc.vector.tensor_copy(ysb[:, NC:D], bank[:, YB + 1, :]).then_inc(y_out, 1)
                each_block(eng, body)

        got = [region(j * D, D) for j in range(8)]
        got_in = [sem(f"got_in{j}") for j in range(8)]
        stored = sem("stored")
        dv = steps("dve", [x for tt in range(NT) for x in [("add", tt, k) for k in range(EK)]
                           + ([("rstd", tt - 1), ("scale", tt - 1)] if tt else [])] + [("rstd", NT - 1), ("scale", NT - 1)])
        ac = steps("act", [x for tt in range(NT) for x in (("sq", tt), ("sd", tt))])
        at["row"] += 16
        row_at = at["row"]
        with nc.Block() as block:
            @block.gpsimd
            def _(eng):
                for n in range(NT * EK):
                    tt, k = n // EK, n % EK
                    if n >= 8:
                        eng.wait_ge(dve_done, dv["add", tt - 8 // EK, k])
                    eng.indirect_dma_start(got[n % 8], None, y_dram,
                                           bass.IndirectOffsetOnAxis(ap=srow[:, n:n + 1], axis=0))\
                       .then_inc(got_in[n % 8], 16)

            @block.vector
            def _(eng):
                def scale(tt):
                    rstd = stat[:, 8 + tt:9 + tt]
                    eng.wait_ge(act_done, ac["sd", tt])
                    nc.vector.reciprocal(rstd, stat[:, 4 + tt:5 + tt]).then_inc(dve_done, 1)
                    eng.wait_ge(dve_done, dv["rstd", tt])
                    nc.vector.scalar_tensor_tensor(out=tok[:, tt, :], in0=h[:, tt, :], scalar=rstd, in1=grow[:, :],
                                                   op0=ALU.mult, op1=ALU.mult).then_inc(dve_done, 1)

                eng.wait_ge(row_in, row_at)
                for tt in range(NT):
                    for k in range(EK):
                        n = tt * EK + k
                        eng.wait_ge(got_in[n % 8], 16 * (n // 8 + 1))
                        if k:
                            eng.wait_ge(dve_done, dv["add", tt, k - 1])
                        nc.vector.scalar_tensor_tensor(out=h[:, tt, :], in0=got[n % 8], scalar=gk[:, n:n + 1],
                                                       in1=h[:, tt, :], op0=ALU.mult, op1=ALU.add).then_inc(dve_done, 1)
                    if tt:
                        scale(tt - 1)
                scale(NT - 1)

            @block.scalar
            def _(eng):
                for tt in range(NT):
                    eng.wait_ge(dve_done, dv["add", tt, EK - 1])
                    nc.scalar.activation(tok[:, tt, :], h[:, tt, :], ACT.Square, accum_out=stat[:, tt:tt + 1])\
                      .then_inc(act_done, 1)
                    eng.wait_ge(act_done, ac["sq", tt])
                    nc.scalar.activation(stat[:, 4 + tt:5 + tt], stat[:, tt:tt + 1], ACT.Sqrt, scale=1.0 / D,
                                         bias=const("eps", 1, 2)).then_inc(act_done, 1)

            @block.sync
            def _(sp):
                sp.dma_start(grow[:, :], t["g_final_2"].rearrange("(o d) -> o d", o=1).to_broadcast([P, D]))\
                  .then_inc(row_in, 16)
                for tt in range(NT):
                    sp.wait_ge(dve_done, dv["scale", tt])
                    sp.dma_start(out[0, tt * P:(tt + 1) * P, :], tok[:, tt, :]).then_inc(stored, 16)
                sp.wait_ge(stored, 16 * NT)


_RAW = ["x", "w_in", "ln_c_g", "ln_c_b", "w_out", "g_ffn", "w_q", "expert_u", "expert_v", "w_pe", "w_pg", "g_final",
        "mem_2", "w_in_2", "w_pool_2", "w_out_2", "w_mem_q_2", "w_mem_kv_2", "w_mem_o_2", "g_ffn_2", "w_router_2",
        "b_router_2", "w_expert_in_2", "w_expert_out_2", "g_final_2"]


def _channels(a, tiles):
    a = np.asarray(a)
    a = a.reshape(tiles, P, -1)
    return np.ascontiguousarray(a.transpose(1, 0, 2)).reshape(P, -1)


def kernel(**inputs):
    import concourse.bacc as _bacc
    from concourse.bass_utils import run_bass_kernel_spmd as _run

    i = {k: np.asarray(v) for k, v in inputs.items()}
    arrays = {n: np.ascontiguousarray(i[n]) for n in _RAW}
    b_s = i["b_s"][0].reshape(TC, 2, P)
    parts = {
        "g_mix": _channels(i["g_mix"][0], KD), "conv_a_w": _channels(i["conv_a_w"][0].T, TA),
        "conv_a_b": _channels(i["conv_a_b"][0], TA), "ln_a_g": _channels(i["ln_a_g"][0], TA),
        "ln_a_b": _channels(i["ln_a_b"][0], TA), "conv_b_w": _channels(i["conv_b_w"][0].T, TB),
        "g_ple": _channels(i["g_ple"][0], KD), "g_mix_2": _channels(i["g_mix_2"][0], KD),
        "g_sb": _channels(i["g_sb_out_2"][0], 4), "g_pool": _channels(i["g_pool_out_2"][0], 4),
        "pool_scale": _channels(i["pool_scale_2"][0], 4), "g_mem_q": _channels(i["g_mem_q_2"][0], KD),
        "g_mem_kv": _channels(i["g_mem_kv_2"][0], KD),
        "b_s": np.repeat(b_s.transpose(1, 0, 2).reshape(2, TC * P), HD, axis=0),
    }
    arrays["params"] = np.ascontiguousarray(np.concatenate([parts[n] for n in _Q], axis=1))
    arrays["consts"] = constants()
    arrays["w_s_T"] = np.ascontiguousarray(i["w_s"][0].transpose(2, 0, 1))
    arrays["sub_keys_T"] = np.ascontiguousarray(i["sub_keys"][0].reshape(HH, NK, P).transpose(2, 0, 1))
    arrays["p_T"] = np.ascontiguousarray(i["p"][0, 0].T)
    arrays["b_expert"] = np.ascontiguousarray(np.concatenate([i["b_expert_in_2"][0], i["b_expert_out_2"][0]], axis=1))

    nc = _bacc.Bacc("TRN2", target_bir_lowering=False, num_devices=1)
    t = {n: nc.dram_tensor(f"in_{n}", a.shape, mybir.dt.from_np(a.dtype), kind="ExternalInput").ap()
         for n, a in arrays.items()}
    out = nc.dram_tensor("out_0", (1, S, D), F32, kind="ExternalOutput").ap()
    build(nc, t, out)
    r = _run(nc, [{f"in_{n}": a for n, a in arrays.items()}], core_ids=[0])
    return r.results[0]["out_0"]
```
